# Optimizing a Trainium2 kernel written in Bass

```python
import math
import jax
import jax.numpy as jnp
from jax import lax
import numpy as np

D_MODEL = 1024
BATCH = 1
SEQ = 1024
DEPTH = 1
DEC_BATCH = 8
DEC_SEQ = 1
PAST_LEN = 2048
PAGE_SIZE = 128

ATT_HEADS = 8
ATT_KV_HEADS = 2
HEAD_DIM = 64
GQA = ATT_HEADS // ATT_KV_HEADS
WINDOW = 128
ATT_BLOCK = 128
N_BUCKETS = 32
MAX_DISTANCE = WINDOW
DN_HEADS = 8
DN_DK = 64
DN_DV = 64
CONV_WIDTH = 4
DN_CHUNK = 64
ATT_WIDTH = ATT_HEADS * HEAD_DIM
KV_WIDTH = ATT_KV_HEADS * HEAD_DIM
DN_QK_WIDTH = DN_HEADS * DN_DK
DN_WIDTH = DN_HEADS * DN_DV
MIX_WIDTH = ATT_WIDTH + DN_WIDTH
CONV_CH = 2 * DN_QK_WIDTH + DN_WIDTH
IN_SPLITS = (ATT_WIDTH, KV_WIDTH, KV_WIDTH, DN_QK_WIDTH, DN_QK_WIDTH, DN_WIDTH, DN_HEADS, DN_HEADS, DN_WIDTH)
IN_WIDTH = sum(IN_SPLITS)
IN_OFFSETS = tuple(int(o) for o in np.cumsum(IN_SPLITS)[:-1])
N_GROUPS = 4
EXPERTS_PER_GROUP = 8
N_EXPERTS = N_GROUPS * EXPERTS_PER_GROUP
TOP_K = 2
D_EXPERT = 256
PLE_DIM = 256
EPS = 1e-6

kernel_name = 'hymba_swa_gdn_hier_moe_step'

def rmsnorm(x, g):
    xf = x.astype(jnp.float32)
    y = xf * lax.rsqrt(jnp.mean(xf * xf, axis=-1, keepdims=True) + EPS)
    return (y * g.astype(jnp.float32)).astype(x.dtype)

def l2norm(x):
    return x * lax.rsqrt(jnp.sum(x * x, axis=-1, keepdims=True) + EPS)

def t5_bucket(dist):
    max_exact = N_BUCKETS // 2
    d = jnp.maximum(dist, 0)
    ratio = jnp.log(jnp.maximum(d, 1).astype(jnp.float32) / max_exact) / math.log(MAX_DISTANCE / max_exact)
    large = jnp.minimum(max_exact + (ratio * (N_BUCKETS - max_exact)).astype(jnp.int32), N_BUCKETS - 1)
    return jnp.where(d < max_exact, d, large)

def head_bias(dist, rel_bias):
    b = rel_bias[t5_bucket(dist)].astype(jnp.float32)
    b = jnp.moveaxis(b, -1, 0)
    return b.reshape((ATT_KV_HEADS, GQA) + dist.shape)

def sink_softmax(s, sink, mask):
    s = jnp.where(mask, s, -jnp.inf)
    m = jnp.maximum(jnp.max(s, axis=-1, keepdims=True), sink)
    p = jnp.exp(s - m)
    return p / (jnp.sum(p, axis=-1, keepdims=True) + jnp.exp(sink - m))

def attn_prompt(q, k, v, rel_bias, att_sink):
    B, L = q.shape[:2]
    nb = L // ATT_BLOCK
    qb = q.reshape(B, nb, ATT_BLOCK, ATT_KV_HEADS, GQA, HEAD_DIM).astype(jnp.float32)
    kb = k.reshape(B, nb, ATT_BLOCK, ATT_KV_HEADS, HEAD_DIM)
    vb = v.reshape(B, nb, ATT_BLOCK, ATT_KV_HEADS, HEAD_DIM)
    pad = ((0, 0), (1, 0), (0, 0), (0, 0), (0, 0))
    kk = jnp.concatenate([jnp.pad(kb[:, :-1], pad), kb], axis=2).astype(jnp.float32)
    vv = jnp.concatenate([jnp.pad(vb[:, :-1], pad), vb], axis=2).astype(jnp.float32)
    qi = jnp.arange(ATT_BLOCK)[:, None]
    kj = jnp.arange(2 * ATT_BLOCK)[None, :]
    dist = qi + ATT_BLOCK - kj
    band = (dist >= 0) & (dist < WINDOW)
    not_before_start = (jnp.arange(nb)[:, None, None] > 0) | (kj[None] >= ATT_BLOCK)
    mask = (band[None] & not_before_start)[:, None, None]
    s = jnp.einsum('bnqkgd,bnjkd->bnkgqj', qb, kk) * (HEAD_DIM ** -0.5) + head_bias(dist, rel_bias)
    sink = att_sink.astype(jnp.float32).reshape(ATT_KV_HEADS, GQA, 1, 1)
    pr = sink_softmax(s, sink, mask)
    o = jnp.einsum('bnkgqj,bnjkd->bnqkgd', pr, vv).reshape(B, L, ATT_WIDTH).astype(q.dtype)
    buf = min(WINDOW, L)
    return o, k[:, L - buf:], v[:, L - buf:]

def attn_sample(q, k, v, cache_k, cache_v, rel_bias, att_sink):
    Bd, T = q.shape[:2]
    Lb = cache_k.shape[1]
    kk = jnp.concatenate([cache_k.astype(k.dtype), k], axis=1)
    vv = jnp.concatenate([cache_v.astype(v.dtype), v], axis=1)
    qh = q.reshape(Bd, T, ATT_KV_HEADS, GQA, HEAD_DIM).astype(jnp.float32)
    dist = (Lb + jnp.arange(T))[:, None] - jnp.arange(Lb + T)[None, :]
    mask = (dist >= 0) & (dist < WINDOW)
    s = jnp.einsum('btkgd,bjkd->bkgtj', qh, kk.astype(jnp.float32)) * (HEAD_DIM ** -0.5) + head_bias(dist, rel_bias)
    sink = att_sink.astype(jnp.float32).reshape(ATT_KV_HEADS, GQA, 1, 1)
    pr = sink_softmax(s, sink, mask)
    o = jnp.einsum('bkgtj,bjkd->btkgd', pr, vv.astype(jnp.float32)).reshape(Bd, T, ATT_WIDTH).astype(q.dtype)
    return o, kk[:, T:], vv[:, T:]

def gated_delta_chunked(q, k, v, g, beta, S0, chunk):
    B, L, H, dk = q.shape
    dv = v.shape[-1]
    n = L // chunk

    def blk(t):
        t = t.reshape((B, n, chunk, H) + t.shape[3:])
        return jnp.moveaxis(t, 3, 1)

    q, k, v, g, beta = blk(q), blk(k), blk(v), blk(g), blk(beta)
    gam = jnp.cumsum(g, axis=-1)
    causal = jnp.tril(jnp.ones((chunk, chunk), dtype=bool))
    strict = jnp.tril(jnp.ones((chunk, chunk), dtype=bool), -1)
    decay = jnp.exp(jnp.where(causal, gam[..., :, None] - gam[..., None, :], -jnp.inf))
    kb = k * beta[..., None]
    A = jnp.where(strict, jnp.einsum('bhncd,bhnjd->bhncj', kb, k) * decay, 0.0)
    eye = jnp.eye(chunk, dtype=A.dtype)
    rhs = jnp.concatenate([v * beta[..., None], kb * jnp.exp(gam)[..., None]], axis=-1)
    sol = lax.linalg.triangular_solve(eye + A, rhs, left_side=True, lower=True, unit_diagonal=True)
    u, w = sol[..., :dv], sol[..., dv:]
    qk = jnp.where(causal, jnp.einsum('bhncd,bhnjd->bhncj', q, k) * decay, 0.0)
    qg = q * jnp.exp(gam)[..., None]
    kd = k * jnp.exp(gam[..., -1:] - gam)[..., None]
    gl = jnp.exp(gam[..., -1])
    xs = tuple(jnp.moveaxis(t, 2, 0) for t in (u, w, qk, qg, kd, gl))

    def step(S, inp):
        u_c, w_c, qk_c, qg_c, kd_c, gl_c = inp
        v_new = u_c - jnp.einsum('bhcd,bhde->bhce', w_c, S)
        o = jnp.einsum('bhcd,bhde->bhce', qg_c, S) + jnp.einsum('bhcj,bhje->bhce', qk_c, v_new)
        S = S * gl_c[..., None, None] + jnp.einsum('bhcd,bhce->bhde', kd_c, v_new)
        return S, o

    S, o = lax.scan(step, S0, xs)
    o = jnp.moveaxis(jnp.moveaxis(o, 0, 2), 1, 3).reshape(B, L, H, dv)
    return o, S

def gated_deltanet(dq, dk, dv, db, da, dz, conv_prev, S0, conv_w, A_log, dt_bias, dn_norm):
    B, L, _ = dq.shape
    xc = jnp.concatenate([dq, dk, dv], axis=-1)
    xp = jnp.concatenate([conv_prev.astype(xc.dtype), xc], axis=1)
    y = xp[:, 0:L] * conv_w[0]
    for j in range(1, CONV_WIDTH):
        y = y + xp[:, j:j + L] * conv_w[j]
    y = jax.nn.silu(y.astype(jnp.float32))
    new_conv = xp[:, L:]
    q = l2norm(y[..., :DN_QK_WIDTH].reshape(B, L, DN_HEADS, DN_DK)) * (DN_DK ** -0.5)
    k = l2norm(y[..., DN_QK_WIDTH:2 * DN_QK_WIDTH].reshape(B, L, DN_HEADS, DN_DK))
    v = y[..., 2 * DN_QK_WIDTH:].reshape(B, L, DN_HEADS, DN_DV)
    beta = jax.nn.sigmoid(db.astype(jnp.float32))
    g = -jnp.exp(A_log.astype(jnp.float32)) * jax.nn.softplus(da.astype(jnp.float32) + dt_bias.astype(jnp.float32))
    chunk = DN_CHUNK if L % DN_CHUNK == 0 else L
    o, S = gated_delta_chunked(q, k, v, g, beta, S0.astype(jnp.float32), chunk)
    o = rmsnorm(o, dn_norm) * jax.nn.silu(dz.reshape(B, L, DN_HEADS, DN_DV).astype(jnp.float32))
    return o.reshape(B, L, DN_WIDTH).astype(dq.dtype), new_conv, S

def hier_moe(x, w_rg, w_re, w_gate, w_up, w_down):
    B, L, D = x.shape
    xt = x.reshape(B * L, D)
    pg = jax.nn.softmax((xt @ w_rg).astype(jnp.float32), axis=-1)
    gsel = jnp.argmax(pg, axis=-1)
    pgsel = jnp.take_along_axis(pg, gsel[:, None], axis=-1)
    le = (xt @ w_re).astype(jnp.float32).reshape(-1, N_GROUPS, EXPERTS_PER_GROUP)
    le = jnp.take_along_axis(le, gsel[:, None, None], axis=1)[:, 0]
    topv, topi = lax.top_k(jax.nn.softmax(le, axis=-1), TOP_K)
    topv = topv / jnp.sum(topv, axis=-1, keepdims=True)
    eidx = gsel[:, None] * EXPERTS_PER_GROUP + topi
    gates = jnp.sum(jax.nn.one_hot(eidx, N_EXPERTS, dtype=jnp.float32) * (topv * pgsel)[..., None], axis=1)
    hg = jnp.einsum('td,edf->tef', xt, w_gate)
    hu = jnp.einsum('td,edf->tef', xt, w_up)
    hm = jax.nn.silu(hg) * hu * gates[..., None].astype(x.dtype)
    return jnp.einsum('tef,efd->td', hm, w_down).reshape(B, L, D)

def layer(h, p, kv_cache, conv_prev, S0, lw, rel_bias):
    (norm_mix, w_in, att_sink, conv_w, A_log, dt_bias, dn_norm, w_out,
     norm_ffn, w_rg, w_re, w_gate, w_up, w_down, w_pp, w_pg, norm_ple) = lw
    B, L, _ = h.shape
    hn = rmsnorm(h, norm_mix)
    aq, ak, av, dq, dk, dv, db, da, dz = jnp.split(hn @ w_in, IN_OFFSETS, axis=-1)
    aq = aq.reshape(B, L, ATT_HEADS, HEAD_DIM)
    ak = ak.reshape(B, L, ATT_KV_HEADS, HEAD_DIM)
    av = av.reshape(B, L, ATT_KV_HEADS, HEAD_DIM)
    if kv_cache is None:
        o_att, k_new, v_new = attn_prompt(aq, ak, av, rel_bias, att_sink)
    else:
        o_att, k_new, v_new = attn_sample(aq, ak, av, kv_cache[0], kv_cache[1], rel_bias, att_sink)
    o_dn, conv_new, S_new = gated_deltanet(dq, dk, dv, db, da, dz, conv_prev, S0, conv_w, A_log, dt_bias, dn_norm)
    h = h + jnp.concatenate([o_att, o_dn], axis=-1) @ w_out
    h = h + hier_moe(rmsnorm(h, norm_ffn), w_rg, w_re, w_gate, w_up, w_down)
    h = h + (p.astype(h.dtype) @ w_pp) * jax.nn.sigmoid(rmsnorm(h, norm_ple) @ w_pg)
    return h, k_new, v_new, conv_new, S_new

def setup_inputs(seed: int = 0) -> dict:
    key = jax.random.key(seed)
    ks = jax.random.split(key, 32)
    f32 = jnp.float32

    def nrm(k, shape, s):
        return s * jax.random.normal(k, shape, f32)

    def gain(k, shape):
        return 1.0 + 0.02 * jax.random.normal(k, shape, f32)

    buf = min(WINDOW, PAST_LEN)
    dt = jnp.exp(jax.random.uniform(ks[16], (DEPTH, DN_HEADS), f32, math.log(1e-3), math.log(1e-1)))
    return {
        'x_prompt': nrm(ks[0], (BATCH, SEQ, D_MODEL), 1.0),
        'x_sample': nrm(ks[1], (DEC_BATCH, DEC_SEQ, D_MODEL), 1.0),
        'p_prompt': nrm(ks[2], (DEPTH, BATCH, SEQ, PLE_DIM), 1.0),
        'p_sample': nrm(ks[3], (DEPTH, DEC_BATCH, DEC_SEQ, PLE_DIM), 1.0),
        'cache_k': nrm(ks[4], (DEPTH, DEC_BATCH, buf, ATT_KV_HEADS, HEAD_DIM), 1.0),
        'cache_v': nrm(ks[5], (DEPTH, DEC_BATCH, buf, ATT_KV_HEADS, HEAD_DIM), 1.0),
        'state_conv': nrm(ks[6], (DEPTH, DEC_BATCH, CONV_WIDTH - 1, CONV_CH), 1.0),
        'state_S': nrm(ks[7], (DEPTH, DEC_BATCH, DN_HEADS, DN_DK, DN_DV), 0.1),
        'rel_bias': nrm(ks[8], (N_BUCKETS, ATT_HEADS), 0.5),
        'norm_mix': gain(ks[9], (DEPTH, D_MODEL)),
        'w_in': nrm(ks[10], (DEPTH, D_MODEL, IN_WIDTH), D_MODEL ** -0.5),
        'att_sink': nrm(ks[11], (DEPTH, ATT_HEADS), 0.5),
        'conv_w': nrm(ks[12], (DEPTH, CONV_WIDTH, CONV_CH), CONV_WIDTH ** -0.5),
        'dn_A_log': jnp.log(jax.random.uniform(ks[13], (DEPTH, DN_HEADS), f32, 1.0, 16.0)),
        'dn_dt_bias': dt + jnp.log(-jnp.expm1(-dt)),
        'dn_norm': gain(ks[14], (DEPTH, DN_DV)),
        'w_out': nrm(ks[15], (DEPTH, MIX_WIDTH, D_MODEL), MIX_WIDTH ** -0.5),
        'norm_ffn': gain(ks[17], (DEPTH, D_MODEL)),
        'w_router_group': nrm(ks[18], (DEPTH, D_MODEL, N_GROUPS), D_MODEL ** -0.5),
        'w_router_expert': nrm(ks[19], (DEPTH, D_MODEL, N_EXPERTS), D_MODEL ** -0.5),
        'w_gate': nrm(ks[20], (DEPTH, N_EXPERTS, D_MODEL, D_EXPERT), D_MODEL ** -0.5),
        'w_up': nrm(ks[21], (DEPTH, N_EXPERTS, D_MODEL, D_EXPERT), D_MODEL ** -0.5),
        'w_down': nrm(ks[22], (DEPTH, N_EXPERTS, D_EXPERT, D_MODEL), D_EXPERT ** -0.5),
        'w_ple_proj': nrm(ks[23], (DEPTH, PLE_DIM, D_MODEL), PLE_DIM ** -0.5),
        'w_ple_gate': nrm(ks[24], (DEPTH, D_MODEL, D_MODEL), D_MODEL ** -0.5),
        'norm_ple': gain(ks[25], (DEPTH, D_MODEL)),
        'norm_final': gain(ks[26], (D_MODEL,)),
    }

def reference(x_prompt, x_sample, p_prompt, p_sample, cache_k, cache_v, state_conv, state_S,
              rel_bias, norm_mix, w_in, att_sink, conv_w, dn_A_log, dn_dt_bias, dn_norm, w_out,
              norm_ffn, w_router_group, w_router_expert, w_gate, w_up, w_down,
              w_ple_proj, w_ple_gate, norm_ple, norm_final):
    hp, hs = x_prompt, x_sample
    kp_l, vp_l, cp_l, sp_l = [], [], [], []
    ks_l, vs_l, cs_l, ss_l = [], [], [], []
    for i in range(DEPTH):
        lw = (norm_mix[i], w_in[i], att_sink[i], conv_w[i], dn_A_log[i], dn_dt_bias[i], dn_norm[i], w_out[i],
              norm_ffn[i], w_router_group[i], w_router_expert[i], w_gate[i], w_up[i], w_down[i],
              w_ple_proj[i], w_ple_gate[i], norm_ple[i])
        conv0 = jnp.zeros((hp.shape[0], CONV_WIDTH - 1, CONV_CH), hp.dtype)
        S0 = jnp.zeros((hp.shape[0], DN_HEADS, DN_DK, DN_DV), jnp.float32)
        hp, kp, vp, cp, sp = layer(hp, p_prompt[i], None, conv0, S0, lw, rel_bias)
        hs, kn, vn, cn, sn = layer(hs, p_sample[i], (cache_k[i], cache_v[i]), state_conv[i], state_S[i], lw, rel_bias)
        kp_l.append(kp); vp_l.append(vp); cp_l.append(cp); sp_l.append(sp)
        ks_l.append(kn); vs_l.append(vn); cs_l.append(cn); ss_l.append(sn)
    y_prompt = rmsnorm(hp, norm_final)
    y_sample = rmsnorm(hs, norm_final)
    return (y_prompt, y_sample,
            jnp.stack(kp_l), jnp.stack(vp_l), jnp.stack(cp_l), jnp.stack(sp_l),
            jnp.stack(ks_l), jnp.stack(vs_l), jnp.stack(cs_l), jnp.stack(ss_l))


_drawn_inputs = setup_inputs


def setup_inputs(seed=0):
    import zlib

    import numpy as np

    out = dict(_drawn_inputs(seed))
    spreads = {}
    factors = {'att_sink': 8.0, 'dn_norm': 3.724, 'norm_ple': 8.0, 'norm_final': 2.76}
    for name, (base, spread) in spreads.items():
        noise = np.random.default_rng([zlib.crc32(name.encode()), seed]).standard_normal(out[name].shape)
        drawn = base * np.exp(spread * noise) if base else spread * noise
        out[name] = jnp.asarray(drawn.astype(out[name].dtype))
    for name, factor in factors.items():
        out[name] = (out[name] * factor).astype(out[name].dtype)
    return out
```

```python
from contextlib import ExitStack

import numpy as np

import concourse.bass as bass
from concourse import mybir

F32 = mybir.dt.float32
I32 = mybir.dt.int32
ALU = mybir.AluOpType
ACT = mybir.ActivationFunctionType
AX = mybir.AxisListType

P = 128
D = 1024
KD = D // P
SEQ = 1024
NT = SEQ // P
DEC = 8
TOK = SEQ + DEC
AH, HD, GQA = 8, 64, 4
NH = 8
CW = 4
CCH = 3 * NH * HD
FT_DN = CCH // P
A_Q, A_K, A_V, D_Q, D_B = 0, 512, 640, 768, 2304
IN_W = 2832
NG, EPG, NE, DE = 4, 8, 32, 256
PLE = 256
KE = DE // P
EPS = 1e-6
BIG = 1.0e30
XB = (2 * TOK - 1) // P
MAXB = NE + XB
DUMP = 1 << 20

C_ID, C_U, C_NEG, C_LV, C_HOT, C_HOTD, C_US, C_SWAP = 0, 128, 256, 384, 1280, 1664, 1792, 1920
C_TOK, C_GP, C_EP, C_EI, C_E128, C_THR, C_OV, C_FLAG, C_VAL, C_TT, C_END = \
    2048, 2049, 2053, 2061, 2093, 2125, 2133, 2149, 2157, 2166, 2175


def constants():
    c = np.zeros((P, C_END), np.float32)
    i = np.arange(P)
    row, col = i[:, None], i[None, :]
    c[:, C_ID:C_ID + P] = row == col
    c[:, C_U:C_U + P] = row <= col
    c[:, C_NEG:C_NEG + P] = np.where(col >= row, 0.0, -BIG)
    for n in range(7):
        s = 1 << n
        c[:, C_LV + n * P:C_LV + (n + 1) * P] = (row // (2 * s) == col // (2 * s)) & (row // s < col // s)
    c[:, C_US:C_US + P] = row < col
    c[:, C_SWAP:C_SWAP + P] = row == (col + 64) % P

    def bucket(d):
        d = np.maximum(d, 0)
        ratio = np.log(np.maximum(d, 1).astype(np.float32) / 16) / np.log(8.0)
        return np.where(d < 16, d, np.minimum(16 + (ratio * 16).astype(np.int32), 31))

    m = np.arange(3 * P)
    dist = 2 * P - 1 - m
    b = np.where((dist >= 0) & (dist < P), bucket(dist), 32)
    c[b, C_HOT + m] = 1.0
    dist = np.where(i == 0, 0, P - i)
    c[bucket(dist), C_HOTD + i] = 1.0
    c[:, C_TOK] = i
    c[:, C_GP:C_GP + NG] = NG - np.arange(NG)
    c[:, C_EP:C_EP + EPG] = EPG - np.arange(EPG)
    c[:, C_EI:C_EI + NE] = np.arange(NE)
    c[:, C_E128:C_E128 + NE] = np.arange(NE) * P
    c[:, C_THR:C_THR + 8] = (np.arange(8) + 1) * P
    c[:, C_OV:C_OV + XB] = np.arange(XB)
    c[:, C_FLAG] = -BIG
    c[:, C_VAL:C_VAL + NT] = 1.0
    c[:DEC, C_VAL + NT] = 1.0
    c[:, C_TT:C_TT + NT + 1] = i[:, None] + P * np.arange(NT + 1)
    return c


class Layout:

    def __init__(self, tensor):
        self.tensor, self.at = tensor, 0

    def take(self, *shape):
        n = 1
        for s in shape:
            n *= s
        view = self.tensor[:, self.at:self.at + n]
        self.at += n
        assert self.at <= self.tensor.shape[1], self.at
        if len(shape) == 2:
            return view.rearrange("p (a b) -> p a b", b=shape[1])
        if len(shape) == 3:
            return view.rearrange("p (a b c) -> p a b c", b=shape[1], c=shape[2])
        return view


def bc(ap, n):
    return ap.unsqueeze(2).to_broadcast([ap.shape[0], ap.shape[1], n])


def bm(ap, n):
    return ap.unsqueeze(1).to_broadcast([ap.shape[0], n, ap.shape[1]])


def even_odd(x):
    return x.rearrange("p (a f) -> p a f", a=2)


def program(nc, I, O, dbg=None):
    es = ExitStack()
    sems, stages = {}, []

    def S(name):
        if name not in sems:
            sems[name] = nc.alloc_semaphore(name=f"{name}_{len(stages)}")
        return sems[name]

    def stage_ends():
        nc.clear_and_free_semaphores(list(sems.values()))
        sems.clear()
        stages.append(None)
        nc.all_engine_barrier()

    def settle(eng):
        eng.sem_inc(S(f"settled_{eng.engine}".replace(".", "_")), 1)

    def dram(name, *shape, dt=F32):
        return nc.dram_tensor(name, shape, dt).ap()

    with es:
        mem = Layout(es.enter_context(nc.sbuf_tensor("mem", [P, 50400], F32)))
        psum = es.enter_context(nc.psum_tensor("psum", [P, 8, 512], F32))

        y_d = dram("conv_out_d", P, FT_DN, SEQ)
        ydec_d = dram("conv_dec_d", 3, DEC, NH * HD)
        sz_d = dram("gate_d", TOK, NH * HD)
        h_d = dram("h_d", TOK, D)
        xs_d = dram("xs_d", TOK, D)
        ye_d = dram("ye_d", 2 * TOK, D)
        tab_d = dram("tab_d", MAXB * P, 4, dt=I32)
        bias_d = dram("bias_d", AH, P, 3 * P)
        gbd_d = dram("gbd_d", 2, DEC, NH)
        od_d = dram("od_d", DEC, NH * HD)

        cst = mem.take(C_END)
        ident = cst[:, C_ID:C_ID + P]
        small = mem.take(1024)
        at = [0]

        def col(n):
            at[0] += n
            assert at[0] <= 1024
            return small[:, at[0] - n:at[0]]

        g_mix, g_ffn, g_ple = col(KD), col(KD), col(KD)
        half = col(1)
        normB, sinkB, sinkC, lg_pad = col(HD), col(AH), col(1), col(1)
        ones = mem.take(P)
        gb = mem.take(NT + 1, 16)
        qf = mem.take(4, TOK)
        kf = mem.take(P + TOK)
        ksw = mem.take(P + TOK)
        vt = mem.take(NT + 2, P)
        lg = mem.take(NT + 1, NG + NE)
        tabI = mem.take(4, MAXB).bitcast(I32)
        blk = mem.take(XB + 1).bitcast(I32)
        mixD = mem.take(KD, DEC)
        stay = mem.at

        def bank(i, n=1):
            return psum[:, i, :] if n == 1 else psum[:, i:i + n, :]

        def flat(i, n):
            return psum[:, i:i + n, :].rearrange("p a b -> p (a b)")

        hnT = mem.take(KD, TOK)
        xin, xs, xT = mem.take(2, D), mem.take(2, D), mem.take(2, KD, P)
        wtok = mem.take(KD, 144 + 512)
        wf = mem.take(2, KD, P)
        XP = CW - 1 + SEQ + DEC * CW
        xp = mem.take(2, XP + 1)
        yc = mem.take(2, XP + 1)
        ys = mem.take(2, XP + 1)
        tails = mem.take(FT_DN, 27)
        stT = mem.take(FT_DN, 24)
        cwT = mem.take(FT_DN, CW)
        strow = mem.take(CCH)
        cwrow = mem.take(P)
        szt = mem.take(2, 512)
        ydT = mem.take(FT_DN, DEC)
        ydrow = mem.take(CCH)
        dtN, alN, dtB, alB = (col(NH) for _ in range(4))
        small_a, small_b, small_c = (col((NT + 1) * NH) for _ in range(3))
        rr = [(col(1), col(1), col(1)) for _ in range(2)]
        w_in = I["w_in"][0].rearrange("(p k) n -> p k n", k=KD)
        NV = XP - CW + 1

        with nc.Block() as block:
            @block.sync
            def _(sp):
                sp.dma_start(cst, I["cst"]).then_inc(S("cst"), 16)
                for v, name in ((g_mix, "norm_mix"), (g_ffn, "norm_ffn"), (g_ple, "norm_ple")):
                    sp.dma_start(v, I[name][0].rearrange("(p k) -> p k", k=KD)).then_inc(S("gains"), 16)
                sp.dma_start(dtN, I["dn_dt_bias"][0].partition_broadcast(P)).then_inc(S("gains"), 16)
                sp.dma_start(alN, I["dn_A_log"][0].partition_broadcast(P)).then_inc(S("gains"), 16)
                sp.dma_start(normB, I["dn_norm"][0].partition_broadcast(P)).then_inc(S("gains"), 16)

                def load_x(n, u, t):
                    sp.wait_ge(S(f"xs{u}"), n)
                    if t is None:
                        sp.dma_start(xin[0:DEC, u, :], I["x_sample"][:, 0, :]).then_inc(S(f"x{u}"), 16)
                    else:
                        sp.dma_start(xin[:, u, :], I["x_prompt"][0, bass.ds(t * P, P), :]).then_inc(S(f"x{u}"), 16)

                load_x(0, 0, 0)
                load_x(0, 1, 1)
                sp.dma_start(wtok[:, :, 0:P], w_in[:, :, A_V:A_V + P]).then_inc(S("wtok"), 16)
                sp.dma_start(wtok[:, :, P:], w_in[:, :, D_B:IN_W]).then_inc(S("wtok"), 16)
                sp.dma_start(strow[0:24, :], I["state_conv"][0].rearrange("b j c -> (b j) c")).then_inc(S("small"), 16)
                sp.dma_start(cwrow[0:48, :], I["conv_w"][0].rearrange("j (f c) -> (j f) c", c=P)).then_inc(S("small"), 16)
                with sp.Fori(1, 4) as n:
                    for u in range(2):
                        load_x(n, u, 2 * n + u)
                load_x(4, 0, None)

                def load_w(n, u, c0):
                    sp.wait_ge(S(f"f_psum{u}"), n)
                    sp.dma_start(wf[:, u], w_in[:, :, bass.ds(c0, P)]).then_inc(S(f"wf{u}"), 16)

                with sp.Fori(0, FT_DN // 2) as n:
                    for u in range(2):
                        load_w(n, u, D_Q + (2 * n + u) * P)
                for a in range(5):
                    load_w(6 + a // 2, a % 2, a * P)

                sp.wait_ge(S("tok_out0"), 5)
                sp.wait_ge(S("tok_out1"), 4)
                sp.dma_start(O["cache_v_prompt"][0, 0].rearrange("t h d -> t (h d)"), vt[:, NT, :]).then_inc(S("o1"), 16)
                sp.dma_start(O["cache_v_sample"][0, :, P - 1].rearrange("b h d -> b (h d)"), vt[0:DEC, NT + 1, :]).then_inc(S("o1"), 16)
                for new, old in (("cache_k_sample", "cache_k"), ("cache_v_sample", "cache_v")):
                    sp.dma_start(O[new][0, :, 0:P - 1].rearrange("b t h d -> b t (h d)"),
                                 I[old][0, :, 1:P].rearrange("b t h d -> b t (h d)")).then_inc(S("o1"), 16)
                sp.wait_ge(S("tails_row"), 1)
                sp.dma_start(O["state_conv_prompt"][0, 0], strow[0:3, :]).then_inc(S("o1"), 16)
                sp.dma_start(O["state_conv_sample"][0].rearrange("b j c -> (b j) c"), strow[3:27, :]).then_inc(S("o1"), 16)
                sp.wait_ge(S("ydrow"), 1)
                sp.dma_start(ydec_d.rearrange("i b c -> b i c"), ydrow[0:DEC, :].rearrange("b (i c) -> b i c", i=3)).then_inc(S("o1"), 16)
                sp.wait_ge(S("krow"), 1)
                sp.dma_start(O["cache_k_prompt"][0, 0].rearrange("t h d -> t (h d)"), cwrow).then_inc(S("o1"), 16)
                sp.wait_ge(S("krow"), 2)
                sp.dma_start(O["cache_k_sample"][0, :, P - 1].rearrange("b h d -> b (h d)"), yc[0:DEC, 0, 0:P]).then_inc(S("o1"), 16)
                sp.wait_ge(S("o1"), 16 * 9)

            @block.gpsimd
            def _(g):
                g.memset(half, -0.5).then_inc(S("half"), 1)
                g.memset(ones, 1.0).then_inc(S("ones"), 1)
                g.memset(kf[:, 0:P], 0.0).then_inc(S("zeros"), 1)
                g.memset(ksw[:, 0:P], 0.0).then_inc(S("zeros"), 1)
                g.memset(vt[:, 0, :], 0.0).then_inc(S("zeros"), 1)
                g.memset(vt[:, NT + 1, :], 0.0).then_inc(S("zeros"), 1)
                g.memset(gb[:, NT, :], 0.0).then_inc(S("zeros"), 1)
                g.memset(lg[:, NT, :], 0.0).then_inc(S("zeros"), 1)
                g.memset(xp[:, :, 0:CW - 1], 0.0).then_inc(S("zeros"), 1)
                g.wait_ge(S("half"), 1)

                def rstd(n, u):
                    g.wait_ge(S(f"var{u}"), n + 1)
                    g.tensor_tensor(rr[u][2], rr[u][1], half, ALU.pow).then_inc(S(f"rstd{u}"), 1)

                with g.Fori(0, 4) as n:
                    for u in range(2):
                        rstd(n, u)
                rstd(4, 0)

            @block.vector
            def _(v):
                def scale(n, u):
                    v.wait_ge(S(f"ss{u}"), n + 1)
                    nc.vector.tensor_scalar(rr[u][1], rr[u][0], 1.0 / D, EPS, ALU.mult, ALU.add).then_inc(S(f"var{u}"), 1)
                    v.wait_ge(S(f"rstd{u}"), n + 1)
                    nc.vector.tensor_scalar(xs[:, u, :], xin[:, u, :], rr[u][2], None, ALU.mult).then_inc(S(f"xs{u}"), 1)

                def gain(n, u):
                    v.wait_ge(S(f"xT_psum{u}"), n + 1)
                    v.wait_ge(S(f"tok_psum{u}"), n)
                    v.wait_ge(S(f"hnT{u}"), n)
                    nc.vector.tensor_tensor(xT[:, u], flat(2 * u, 2).rearrange("p (k c) -> p k c", c=P),
                                            bc(g_mix, P), ALU.mult).then_inc(S(f"xT{u}"), 1)

                v.wait_ge(S("gains"), 96)
                nc.vector.tensor_copy(even_odd(dtB), dtN.rearrange("p (f a) -> p a f", a=2)).then_inc(S("dtB"), 1)
                scale(0, 0)
                with v.Fori(0, 4) as n:
                    scale(n, 1)
                    gain(n, 0)
                    scale(n + 1, 0)
                    gain(n, 1)
                gain(4, 0)

                v.wait_ge(S("st_psum"), 1)
                nc.vector.tensor_copy(stT, bank(6)[:, 0:24 * FT_DN].rearrange("p (f c) -> p f c", c=24)).then_inc(S("stT"), 1)
                nc.vector.tensor_copy(cwT, bank(7)[:, 0:48].rearrange("p (j f) -> p f j", f=FT_DN)).then_inc(S("stT"), 1)
                v.wait_ge(S("stT"), 2)

                def conv(n, u, ft):
                    dec = xp[:, u, CW - 1 + SEQ:XP].rearrange("p (b j) -> p b j", j=CW)
                    v.wait_ge(S(f"tails{u}"), n)
                    nc.vector.tensor_copy(dec[:, :, 0:CW - 1], stT[:, ft, :].rearrange("p (b j) -> p b j", j=CW - 1))
                    v.wait_ge(S(f"f_psum{u}"), n + 1)
                    nc.vector.tensor_copy(dec[:, :, CW - 1], bank(3 * u + 2)[:, 0:DEC]).then_inc(S(f"xp_dec{u}"), 1)
                    v.wait_ge(S(f"xp_dec{u}"), n + 1)
                    v.wait_ge(S(f"xp{u}"), n + 1)
                    v.wait_ge(S(f"silu{u}"), n)
                    nc.vector.tensor_scalar(yc[:, u, 0:NV], xp[:, u, 0:NV], cwT[:, ft, 0:1], None,
                                            ALU.mult).then_inc(S(f"conv{u}"), 1)
                    for j in range(1, CW):
                        v.wait_ge(S(f"conv{u}"), CW * n + j)
                        nc.vector.scalar_tensor_tensor(yc[:, u, 0:NV], xp[:, u, j:j + NV], cwT[:, ft, j:j + 1],
                                                       yc[:, u, 0:NV], ALU.mult, ALU.add).then_inc(S(f"conv{u}"), 1)
                    nc.vector.tensor_copy(tails[:, ft, 0:3], xp[:, u, SEQ:SEQ + 3])
                    nc.vector.tensor_copy(tails[:, ft, 3:27].rearrange("p (b j) -> p b j", j=3),
                                          dec[:, :, 1:CW]).then_inc(S(f"tails{u}"), 1)

                v.wait_ge(S("zeros"), 7)
                with v.Fori(0, FT_DN // 2) as n:
                    for u in range(2):
                        conv(n, u, 2 * n + u)
                for a in range(5):
                    n, u = 6 + a // 2, a % 2
                    v.wait_ge(S(f"f_psum{u}"), n + 1)
                    dst = qf[:, a, SEQ:TOK] if a < 4 else kf[:, P + SEQ:P + TOK]
                    nc.vector.tensor_copy(dst, bank(3 * u + 2)[:, 0:DEC]).then_inc(S(f"dec_out{u}"), 1)
                v.wait_ge(S("tails_psum"), 1)
                nc.vector.tensor_copy(strow[0:27, :], flat(3, 3)[0:27, :]).then_inc(S("tails_row"), 1)
                v.wait_ge(S("yd_psum"), 1)
                nc.vector.tensor_copy(ydrow[0:DEC, :], flat(3, 3)[0:DEC, :]).then_inc(S("ydrow"), 1)
                v.wait_ge(S("ksw_psum"), 1)
                nc.vector.tensor_copy(ksw[:, P:P + SEQ], flat(0, 2)).then_inc(S("ksw"), 1)
                nc.vector.tensor_copy(ksw[:, P + SEQ:], bank(2)[:, 0:DEC]).then_inc(S("ksw"), 1)
                v.wait_ge(S("krow_psum"), 1)
                nc.vector.tensor_copy(cwrow, bank(6)[:, 0:P]).then_inc(S("krow"), 1)
                nc.vector.tensor_copy(yc[0:DEC, 0, 0:P], bank(6)[0:DEC, P:2 * P]).then_inc(S("krow"), 1)

                v.wait_ge(S("sig"), 1)
                nc.vector.tensor_scalar(small_a, small_a, 1.0, None, ALU.add).then_inc(S("gbc"), 1)
                v.wait_ge(S("gbc"), 1)
                nc.vector.reciprocal(gb[:, :, 0:NH], small_a.rearrange("p (t h) -> p t h", h=NH)).then_inc(S("gbc"), 1)
                da = gb[:, :, NH:2 * NH]
                v.wait_ge(S("dtB"), 1)
                nc.vector.tensor_tensor(da, da, bm(dtB, NT + 1), ALU.add).then_inc(S("gbc"), 1)
                v.wait_ge(S("gbc"), 3)
                nc.vector.tensor_scalar(small_b.rearrange("p (t h) -> p t h", h=NH), da, 0.0, None, ALU.max).then_inc(S("gbc"), 1)
                v.wait_ge(S("gbc"), 4)
                nc.vector.scalar_tensor_tensor(small_c.rearrange("p (t h) -> p t h", h=NH), small_b.rearrange("p (t h) -> p t h", h=NH), -2.0, da,
                                               ALU.mult, ALU.add).then_inc(S("negabs"), 1)
                v.wait_ge(S("sp"), 1)
                nc.vector.tensor_tensor(small_b, small_b, small_c, ALU.add).then_inc(S("gbc"), 1)
                v.wait_ge(S("gbc"), 5)
                nc.vector.scalar_tensor_tensor(da, small_b.rearrange("p (t h) -> p t h", h=NH), -1.0, bm(alB, NT + 1),
                                               ALU.mult, ALU.mult).then_inc(S("gbc"), 1)

            @block.scalar
            def _(act):
                def square(n, u):
                    act.wait_ge(S(f"x{u}"), 16 * n + 16)
                    act.wait_ge(S(f"xT_psum{u}"), n)
                    nc.scalar.activation(xs[:, u, :], xin[:, u, :], ACT.Square, accum_out=rr[u][0]).then_inc(S(f"ss{u}"), 1)

                def keep_hnT(n, u, cols, m):
                    act.wait_ge(S(f"xT{u}"), n + 1)
                    nc.scalar.activation(hnT[:, :, cols], xT[:, u, :, 0:m], ACT.Copy).then_inc(S(f"hnT{u}"), 1)

                def keep_tok(n, u, t, R):
                    act.wait_ge(S(f"tok_psum{u}"), n + 1)
                    act.wait_ge(S(f"sz_out{u}"), 16 * n)
                    nc.scalar.activation(vt[0:R, t + 1, :], bank(4 + 2 * u)[0:R, 0:P], ACT.Copy)
                    nc.scalar.activation(gb[0:R, t, :].rearrange("p (i a f) -> p i a f", i=2, a=2),
                                         bank(4 + 2 * u)[0:R, P:P + 16].rearrange("p (i f a) -> p i a f", i=2, a=2), ACT.Copy)
                    nc.scalar.activation(szt[0:R, u, :], bank(5 + 2 * u)[0:R, :], ACT.Silu).then_inc(S(f"tok_out{u}"), 1)
                    act.wait_ge(S(f"tok_out{u}"), n + 1)
                    dst = sz_d[SEQ:TOK, :] if R == DEC else sz_d[bass.ds(t * P, P), :]
                    act.dma_start(dst, szt[0:R, u, :]).then_inc(S(f"sz_out{u}"), 16)

                act.wait_ge(S("zeros"), 7)
                square(0, 0)
                with act.Fori(0, 4) as n:
                    square(n, 1)
                    keep_hnT(n, 0, bass.ds(2 * n * P, P), P)
                    square(n + 1, 0)
                    keep_hnT(n, 1, bass.ds((2 * n + 1) * P, P), P)
                    keep_tok(n, 0, 2 * n, P)
                    keep_tok(n, 1, 2 * n + 1, P)
                keep_hnT(4, 0, slice(SEQ, TOK), DEC)
                keep_tok(4, 0, NT, DEC)

                def conv_in(n, u):
                    act.wait_ge(S(f"f_psum{u}"), n + 1)
                    act.wait_ge(S(f"tails{u}"), n)
                    nc.scalar.activation(xp[:, u, CW - 1:CW - 1 + SEQ], flat(3 * u, 2), ACT.Copy).then_inc(S(f"xp{u}"), 1)

                def silu(n, u, ft):
                    act.wait_ge(S(f"conv{u}"), CW * n + CW)
                    act.wait_ge(S(f"y_out{u}"), 16 * n)
                    nc.scalar.activation(ys[:, u, 0:NV], yc[:, u, 0:NV], ACT.Silu).then_inc(S(f"silu{u}"), 1)
                    act.wait_ge(S(f"silu{u}"), n + 1)
                    act.dma_start(y_d[:, ft, :], ys[:, u, 0:SEQ]).then_inc(S(f"y_out{u}"), 16)
                    nc.scalar.activation(ydT[:, ft, :],
                                         ys[:, u, CW - 1 + SEQ:CW - 1 + SEQ + DEC * CW].rearrange("p (b j) -> p b j", j=CW)[:, :, 0],
                                         ACT.Copy).then_inc(S("ydT"), 1)

                with act.Fori(0, FT_DN // 2) as n:
                    conv_in(n, 0)
                    conv_in(n, 1)
                    silu(n, 0, 2 * n)
                    silu(n, 1, 2 * n + 1)
                for a in range(5):
                    n, u = 6 + a // 2, a % 2
                    act.wait_ge(S(f"f_psum{u}"), n + 1)
                    dst = qf[:, a, 0:SEQ] if a < 4 else kf[:, P:P + SEQ]
                    nc.scalar.activation(dst, flat(3 * u, 2), ACT.Copy).then_inc(S(f"att_out{u}"), 1)
                nc.scalar.activation(small_a.rearrange("p (t h) -> p t h", h=NH), gb[:, :, 0:NH], ACT.Exp, scale=-1.0).then_inc(S("sig"), 1)
                act.wait_ge(S("gains"), 96)
                nc.scalar.activation(even_odd(alB), alN.rearrange("p (f a) -> p a f", a=2), ACT.Exp)
                act.wait_ge(S("negabs"), 1)
                nc.scalar.activation(small_c, small_c, ACT.Exp).then_inc(S("spc"), 1)
                act.wait_ge(S("spc"), 1)
                nc.scalar.activation(small_c, small_c, ACT.Ln, bias=1.0).then_inc(S("sp"), 1)
                act.wait_ge(S("sz_out0"), 80)
                act.wait_ge(S("sz_out1"), 64)
                act.wait_ge(S("y_out0"), 96)
                act.wait_ge(S("y_out1"), 96)

            @block.tensor
            def _(pe):
                def turn(n, u):
                    pe.wait_ge(S(f"xs{u}"), n + 1)
                    pe.wait_ge(S(f"xT{u}"), n)
                    for k in range(KD):
                        mm = nc.tensor.transpose(flat(2 * u, 2)[:, k * P:(k + 1) * P],
                                                 xs[:, u, :].rearrange("p (c k) -> p k c", k=KD)[:, k, :], ident)
                    mm.then_inc(S(f"xT_psum{u}"), 1)

                def project(n, u):
                    pe.wait_ge(S(f"xT{u}"), n + 1)
                    pe.wait_ge(S(f"tok_out{u}"), n)
                    for k in range(KD):
                        nc.tensor.matmul(bank(4 + 2 * u)[:, 0:144], xT[:, u, k, :], wtok[:, k, 0:144], start=(k == 0), stop=(k == KD - 1))
                    for k in range(KD):
                        mm = nc.tensor.matmul(bank(5 + 2 * u), xT[:, u, k, :], wtok[:, k, 144:], start=(k == 0), stop=(k == KD - 1))
                    mm.then_inc(S(f"tok_psum{u}"), 1)

                pe.wait_ge(S("cst"), 16)
                turn(0, 0)
                pe.wait_ge(S("wtok"), 32)
                with pe.Fori(0, 4) as n:
                    turn(n, 1)
                    project(n, 0)
                    turn(n + 1, 0)
                    project(n, 1)
                project(4, 0)
                pe.wait_ge(S("small"), 32)
                pe.wait_ge(S("tok_out1"), 4)
                for f in range(FT_DN):
                    nc.tensor.transpose(bank(6)[:, 24 * f:24 * f + 24], strow[0:24, f * P:(f + 1) * P], ident[0:24, 0:24])
                nc.tensor.transpose(bank(7)[:, 0:48], cwrow[0:48, :], ident[0:48, 0:48]).then_inc(S("st_psum"), 1)
                pe.wait_ge(S("hnT0"), 5)
                pe.wait_ge(S("hnT1"), 4)
                pe.wait_ge(S("tok_out0"), 5)

                def features(n, u, att=False):
                    pe.wait_ge(S(f"wf{u}"), 16 * n + 16)
                    if not att or n == 6:
                        pe.wait_ge(S(f"xp{u}"), n if not att else 6)
                        pe.wait_ge(S(f"xp_dec{u}"), n if not att else 6)
                    else:
                        pe.wait_ge(S(f"att_out{u}"), n - 6)
                        pe.wait_ge(S(f"dec_out{u}"), n - 6)
                    for b, lo, hi in ((0, 0, 512), (1, 512, 1024), (2, SEQ, TOK)):
                        for k in range(KD):
                            mm = nc.tensor.matmul(bank(3 * u + b)[:, 0:hi - lo], wf[:, u, k, :], hnT[:, k, lo:hi],
                                                  start=(k == 0), stop=(k == KD - 1))
                    mm.then_inc(S(f"f_psum{u}"), 1)

                with pe.Fori(0, FT_DN // 2) as n:
                    for u in range(2):
                        features(n, u)
                for a in range(5):
                    features(6 + a // 2, a % 2, True)
                pe.wait_ge(S("att_out1"), 2)
                pe.wait_ge(S("dec_out1"), 2)
                pe.wait_ge(S("tails0"), 6)
                pe.wait_ge(S("tails1"), 6)
                for f in range(FT_DN):
                    mm = nc.tensor.transpose(flat(3, 3)[0:27, f * P:(f + 1) * P], tails[:, f, :], ident)
                mm.then_inc(S("tails_psum"), 1)
                pe.wait_ge(S("tails_row"), 1)
                pe.wait_ge(S("ydT"), FT_DN)
                for f in range(FT_DN):
                    mm = nc.tensor.transpose(flat(3, 3)[0:DEC, f * P:(f + 1) * P], ydT[:, f, :], ident)
                mm.then_inc(S("yd_psum"), 1)
                pe.wait_ge(S("att_out0"), 3)
                pe.wait_ge(S("dec_out0"), 3)
                swap = cst[:, C_SWAP:C_SWAP + P]
                for b, lo, hi in ((0, 0, 512), (1, 512, 1024), (2, SEQ, TOK)):
                    mm = nc.tensor.matmul(bank(b)[:, 0:hi - lo], swap, kf[:, P + lo:P + hi], start=True, stop=True)
                mm.then_inc(S("ksw_psum"), 1)
                pe.wait_ge(S("stT"), 2)
                nc.tensor.transpose(bank(6)[:, 0:P], kf[:, SEQ:SEQ + P], ident)
                nc.tensor.transpose(bank(6)[0:DEC, P:2 * P], kf[:, P + SEQ:P + TOK], ident).then_inc(S("krow_psum"), 1)

        stage_ends()
        mem.at = stay
        biasS = mem.take(AH, 2 * P)
        mixer = mem.at
        kc, vc, kcT = mem.take(DEC, P), mem.take(DEC, P), mem.take(DEC, P)
        sinkN = mem.take(AH)
        relb, relw = mem.take(AH), mem.take(AH, P)
        toep = mem.take(2, 3 * P)
        qblk = mem.take(DEC, AH)
        biasD = mem.take(P)
        sD, pTD = mem.take(DEC, P), mem.take(DEC, AH)
        oD = mem.take(DEC, AH)
        mD, eD, dD, rD = (mem.take(DEC) for _ in range(4))
        odr = mem.take(NH * HD)
        S0, prod = mem.take(HD, HD), mem.take(HD, HD)
        qkv = mem.take(3, HD)
        szd = mem.take(HD)
        sqd = mem.take(3, HD)
        kS, qS, vn1, o1, o2 = (mem.take(HD) for _ in range(5))
        bD, gD, egD, qkD, n1, m1, r1 = (mem.take(1) for _ in range(7))
        n2, m2, r2 = (mem.take(2) for _ in range(3))
        PR = DEC * NH

        with nc.Block() as block:
            @block.sync
            def _(sp):
                sp.dma_start(relb[0:32, :], I["rel_bias"]).then_inc(S("d_rel"), 16)
                for i in range(2):
                    for a in range(2):
                        sp.dma_start(gbd_d[i, :, a::2], gb[0:DEC, NT, NH * i + 4 * a:NH * i + 4 * a + 4], allow_slow_non_contiguous=True).then_inc(S("gbd"), 16)
                sp.dma_start(kc, I["cache_k"][0].rearrange("b t h d -> t b (h d)")).then_inc(S("kc"), 16)
                sp.dma_start(vc[1:P], I["cache_v"][0, :, 1:P].rearrange("b t h d -> t b (h d)")).then_inc(S("vc"), 16)
                sp.dma_start(vc[0:1], O["cache_v_sample"][0, :, P - 1].rearrange("b h d -> b (h d)").unsqueeze(0)).then_inc(S("vc"), 16)
                sp.dma_start(sinkN, I["att_sink"][0].partition_broadcast(P)).then_inc(S("sinks"), 16)
                sp.dma_start(sinkC[0:AH], I["att_sink"][0].unsqueeze(1)).then_inc(S("sinks"), 16)
                for i in range(3):
                    sp.dma_start(qkv[0:PR, i, :], ydec_d[i].rearrange("b (h d) -> (b h) d", d=HD)).then_inc(S("qkv"), 16)
                sp.dma_start(szd[0:PR], sz_d[SEQ:TOK].rearrange("b (h d) -> (b h) d", d=HD)).then_inc(S("qkv"), 16)
                sp.dma_start(S0[0:PR], I["state_S"][0].rearrange("b h d e -> (b h) d e")).then_inc(S("S0"), 16)
                sp.wait_ge(S("gbd"), 64)
                sp.dma_start(bD[0:PR], gbd_d[0].rearrange("b (h o) -> (b h) o", o=1)).then_inc(S("bg"), 16)
                sp.dma_start(gD[0:PR], gbd_d[1].rearrange("b (h o) -> (b h) o", o=1)).then_inc(S("bg"), 16)
                for h in range(AH):
                    sp.wait_ge(S("toep"), h + 1)
                    sp.dma_start(bias_d[h], toep[:, h % 2, :]).then_inc(S(f"toep_out{h % 2}"), 16)
                sp.wait_ge(S("toep_out0"), 64)
                sp.wait_ge(S("toep_out1"), 64)
                skew = bias_d.rearrange("h p m -> h (p m)")[:, P - 1:P - 1 + P * (3 * P - 1)].rearrange("h (p m) -> p h m", m=3 * P - 1)
                for g in range(2):
                    for a in range(2):
                        sp.dma_start(biasS[:, 4 * g + 2 * a:4 * g + 2 * a + 2], skew[:, 4 * g + a:4 * g + a + 3:2, 0:2 * P]).then_inc(S("biasS"), 16)
                sp.wait_ge(S("S1"), 1)
                sp.dma_start(O["state_S_sample"][0].rearrange("b h d e -> (b h) d e"), S0[0:PR]).then_inc(S("o2"), 16)
                sp.wait_ge(S("o_dn"), 1)
                sp.dma_start(od_d.rearrange("b (h d) -> (b h) d", d=HD), o2[0:PR]).then_inc(S("od"), 16)
                sp.wait_ge(S("od"), 16)
                sp.dma_start(odr[0:DEC, :], od_d).then_inc(S("odr"), 16)
                sp.wait_ge(S("biasS"), 64)
                sp.wait_ge(S("o2"), 16)
                sp.wait_ge(S("odr"), 16)
                sp.wait_ge(S("sinks"), 32)

            @block.gpsimd
            def _(g):
                g.memset(qblk, 0.0).then_inc(S("qblk0"), 1)
                g.wait_ge(S("n2"), 1)
                g.tensor_tensor(r2[0:PR], m2[0:PR], half[0:PR].to_broadcast([PR, 2]), ALU.pow).then_inc(S("r2"), 1)
                g.wait_ge(S("n1"), 1)
                g.tensor_tensor(r1[0:PR], m1[0:PR], half[0:PR], ALU.pow).then_inc(S("r1"), 1)

            @block.scalar
            def _(act):
                for h in range(AH):
                    act.wait_ge(S("toep_ps"), h + 1)
                    act.wait_ge(S(f"toep_out{h % 2}"), 16 * (h // 2))
                    nc.scalar.activation(toep[:, h % 2, :], bank(h % 2)[:, 0:3 * P], ACT.Copy).then_inc(S("toep"), 1)
                act.wait_ge(S("xD"), 1)
                nc.scalar.activation(sD[0:AH], sD[0:AH], ACT.Exp)
                nc.scalar.activation(eD[0:AH], eD[0:AH], ACT.Exp).then_inc(S("eD"), 1)
                act.wait_ge(S("bg"), 32)
                nc.scalar.activation(egD[0:PR], gD[0:PR], ACT.Exp).then_inc(S("egD"), 1)

            @block.tensor
            def _(pe):
                pe.wait_ge(S("relw"), 1)
                for h in range(AH):
                    pe.wait_ge(S("toep"), h - 1) if h > 1 else None
                    nc.tensor.matmul(bank(h % 2)[:, 0:3 * P], relw[0:33, h, :], cst[0:33, C_HOT:C_HOT + 3 * P], start=True, stop=True).then_inc(S("toep_ps"), 1)
                nc.tensor.matmul(bank(4)[0:AH, 0:P], relb[0:33, :], cst[0:33, C_HOTD:C_HOTD + P], start=True, stop=True)
                nc.tensor.matmul(bank(4)[:, P:P + 4 * DEC], cst[:, C_SWAP:C_SWAP + P], qf[:, :, SEQ:TOK], start=True, stop=True)
                pe.wait_ge(S("kc"), 16)
                for b in range(DEC):
                    mm = nc.tensor.transpose(flat(2, 2)[:, b * P:(b + 1) * P], kc[:, b, :], ident)
                mm.then_inc(S("kcT_ps"), 1)
                pe.wait_ge(S("kcT"), 1)
                for b in range(DEC):
                    mm = nc.tensor.matmul(flat(5, 2)[0:AH, b * P:(b + 1) * P], qblk[:, b, :], kcT[:, b, :], start=True, stop=True)
                mm.then_inc(S("sD_ps"), 1)
                pe.wait_ge(S("pD"), 1)
                for b in range(DEC):
                    mm = nc.tensor.transpose(bank(7)[:, b * AH:(b + 1) * AH], sD[0:AH, b, :], ident[0:AH, 0:AH])
                mm.then_inc(S("pTD_ps"), 1)
                pe.wait_ge(S("pTD"), 1)
                pe.wait_ge(S("vc"), 32)
                for b in range(DEC):
                    mm = nc.tensor.matmul(bank(2)[:, b * AH:(b + 1) * AH], vc[:, b, :], pTD[:, b, :], start=True, stop=True)
                mm.then_inc(S("oD_ps"), 1)
                pe.wait_ge(S("oD"), 1)
                nc.tensor.matmul(bank(3)[:, 0:DEC * AH], cst[:, C_SWAP:C_SWAP + P], oD.rearrange("p b h -> p (b h)"), start=True, stop=True).then_inc(S("osw"), 1)
                pe.wait_ge(S("odr"), 16)
                for k in range(4):
                    mm = nc.tensor.transpose(bank(7)[:, k * DEC:(k + 1) * DEC], odr[0:DEC, k * P:(k + 1) * P], ident[0:DEC, 0:DEC])
                mm.then_inc(S("odT"), 1)

            @block.vector
            def _(v):
                tick = [0]

                def chain(ins):
                    tick[0] += 1
                    ins.then_inc(S("dve_decode"), 1)
                    v.wait_ge(S("dve_decode"), tick[0])

                chain(nc.vector.memset(relb[32:33, :], -BIG))
                v.wait_ge(S("d_rel"), 16)
                nc.vector.tensor_copy(relw[0:33], bc(relb[0:33], P)).then_inc(S("relw"), 1)
                v.wait_ge(S("kcT_ps"), 1)
                v.wait_ge(S("qblk0"), 1)
                chain(nc.vector.tensor_copy(kcT, flat(2, 2).rearrange("p (b j) -> p b j", j=P)))
                nc.vector.tensor_copy(kcT[:, :, 0], kf[:, P + SEQ:])
                qsw = bank(4)[:, P:P + 4 * DEC].rearrange("p (i b) -> p i b", b=DEC)
                for h in range(AH):
                    lo = (h // GQA) * HD
                    src = qf[lo:lo + HD, h // 2, SEQ:TOK] if (h % 2) * HD == lo else qsw[lo:lo + HD, h // 2, :]
                    nc.vector.tensor_copy(qblk[lo:lo + HD, :, h], src)
                nc.vector.tensor_copy(biasD[0:AH], bank(4)[0:AH, 0:P]).then_inc(S("kcT"), 1)
                v.wait_ge(S("kcT"), 1)
                v.wait_ge(S("sD_ps"), 1)
                v.wait_ge(S("sinks"), 32)
                nc.vector.tensor_copy(sinkB.rearrange("p (g a f) -> p g a f", g=2, a=2), sinkN.rearrange("p (g f a) -> p g a f", g=2, a=2))
                sp_ = flat(5, 2)[0:AH].rearrange("p (b j) -> p b j", j=P)
                chain(nc.vector.scalar_tensor_tensor(sD[0:AH], sp_, HD ** -0.5, bm(biasD[0:AH], DEC), ALU.mult, ALU.add))
                chain(nc.vector.tensor_reduce(mD[0:AH], sD[0:AH], AX.X, ALU.max))
                chain(nc.vector.tensor_scalar(mD[0:AH], mD[0:AH], sinkC[0:AH], None, ALU.max))
                nc.vector.tensor_tensor(sD[0:AH], sD[0:AH], bc(mD[0:AH], P), ALU.subtract)
                nc.vector.tensor_scalar(eD[0:AH], mD[0:AH], sinkC[0:AH], -1.0, ALU.subtract, ALU.mult).then_inc(S("xD"), 1)

                v.wait_ge(S("qkv"), 64)
                v.wait_ge(S("bg"), 32)
                chain(nc.vector.tensor_tensor(sqd[0:PR, 0:2], qkv[0:PR, 0:2], qkv[0:PR, 0:2], ALU.mult))
                chain(nc.vector.tensor_reduce(n2[0:PR], sqd[0:PR, 0:2], AX.X, ALU.add))
                nc.vector.tensor_scalar(m2[0:PR, 0:1], n2[0:PR, 0:1], float(HD), HD * EPS, ALU.mult, ALU.add)
                nc.vector.tensor_scalar(m2[0:PR, 1:2], n2[0:PR, 1:2], 1.0, EPS, ALU.mult, ALU.add).then_inc(S("n2"), 1)
                v.wait_ge(S("r2"), 1)
                chain(nc.vector.tensor_tensor(qkv[0:PR, 0:2], qkv[0:PR, 0:2], bc(r2[0:PR], HD), ALU.mult))
                q_, k_, v_ = (qkv[0:PR, i, :] for i in range(3))
                v.wait_ge(S("S0"), 16)
                S0e = S0[0:PR].rearrange("p d e -> p e d")
                chain(nc.vector.tensor_tensor(prod[0:PR], S0e, bm(k_, HD), ALU.mult))
                chain(nc.vector.tensor_reduce(kS[0:PR], prod[0:PR], AX.X, ALU.add))
                chain(nc.vector.tensor_tensor(prod[0:PR], S0e, bm(q_, HD), ALU.mult))
                chain(nc.vector.tensor_reduce(qS[0:PR], prod[0:PR], AX.X, ALU.add))
                chain(nc.vector.tensor_tensor(sqd[0:PR, 2], q_, k_, ALU.mult))
                chain(nc.vector.tensor_reduce(qkD[0:PR], sqd[0:PR, 2], AX.X, ALU.add))
                v.wait_ge(S("egD"), 1)
                chain(nc.vector.tensor_scalar(kS[0:PR], kS[0:PR], egD[0:PR], None, ALU.mult))
                chain(nc.vector.tensor_tensor(vn1[0:PR], v_, kS[0:PR], ALU.subtract))
                chain(nc.vector.tensor_scalar(vn1[0:PR], vn1[0:PR], bD[0:PR], None, ALU.mult))
                chain(nc.vector.tensor_scalar(o1[0:PR], qS[0:PR], egD[0:PR], None, ALU.mult))
                chain(nc.vector.scalar_tensor_tensor(o1[0:PR], vn1[0:PR], qkD[0:PR], o1[0:PR], ALU.mult, ALU.add))
                chain(nc.vector.tensor_tensor(prod[0:PR], bc(k_, HD), bm(vn1[0:PR], HD), ALU.mult))
                nc.vector.scalar_tensor_tensor(S0[0:PR], S0[0:PR], egD[0:PR], prod[0:PR], ALU.mult, ALU.add).then_inc(S("S1"), 1)
                chain(nc.vector.tensor_tensor(sqd[0:PR, 0], o1[0:PR], o1[0:PR], ALU.mult))
                chain(nc.vector.tensor_reduce(n1[0:PR], sqd[0:PR, 0], AX.X, ALU.add))
                nc.vector.tensor_scalar(m1[0:PR], n1[0:PR], 1.0 / HD, EPS, ALU.mult, ALU.add).then_inc(S("n1"), 1)
                v.wait_ge(S("r1"), 1)
                chain(nc.vector.scalar_tensor_tensor(o2[0:PR], o1[0:PR], r1[0:PR], normB[0:PR], ALU.mult, ALU.mult))
                nc.vector.tensor_tensor(o2[0:PR], o2[0:PR], szd[0:PR], ALU.mult).then_inc(S("o_dn"), 1)

                v.wait_ge(S("eD"), 1)
                chain(nc.vector.tensor_reduce(dD[0:AH], sD[0:AH], AX.X, ALU.add))
                chain(nc.vector.tensor_tensor(dD[0:AH], dD[0:AH], eD[0:AH], ALU.add))
                chain(nc.vector.reciprocal(rD[0:AH], dD[0:AH]))
                nc.vector.tensor_tensor(sD[0:AH], sD[0:AH], bc(rD[0:AH], P), ALU.mult).then_inc(S("pD"), 1)
                v.wait_ge(S("pTD_ps"), 1)
                nc.vector.tensor_copy(pTD, bank(7)[:, 0:DEC * AH].rearrange("p (b h) -> p b h", h=AH)).then_inc(S("pTD"), 1)
                v.wait_ge(S("oD_ps"), 1)
                nc.vector.tensor_copy(oD, bank(2)[:, 0:DEC * AH].rearrange("p (b h) -> p b h", h=AH)).then_inc(S("oD"), 1)
                v.wait_ge(S("oD"), 1)
                v.wait_ge(S("osw"), 1)
                oS = bank(3)[:, 0:DEC * AH].rearrange("p (b h) -> p b h", h=AH)
                for h in range(AH):
                    lo = (h % 2) * HD
                    src = oD if (h // GQA) * HD == lo else oS
                    nc.vector.tensor_copy(mixD[lo:lo + HD, h // 2, :], src[lo:lo + HD, :, h])
                v.wait_ge(S("odT"), 1)
                nc.vector.tensor_copy(mixD[:, 4:8, :], bank(7)[:, 0:4 * DEC].rearrange("p (k b) -> p k b", b=DEC)).then_inc(S("mixD"), 1)

        stage_ends()
        mem.at = mixer
        qst, kst, kswst, vst = mem.take(4, P), mem.take(2 * P), mem.take(2 * P), mem.take(2 * P)
        yst = mem.take(FT_DN, P)
        szst = mem.take(NH * HD)
        sA = [mem.take(GQA, 2 * P) for _ in range(2)]
        pT = mem.take(2 * GQA, P)
        mix = mem.take(KD, P)
        qk = mem.take(KD, P)
        qkT = mem.take(KD, P)
        vtok = mem.take(NH, HD)
        E_ = mem.take(NH, P)
        gU = mem.take(NH, P)
        AT = mem.take(NH, P)
        QK = mem.take(NH, P)
        Lo = [mem.take(NH, P) for _ in range(2)]
        Xs = mem.take(NH, P)
        sq = Xs.rearrange("p h i -> p (h i)")
        MT = [mem.take(NH, P) for _ in range(2)]
        M_ = mem.take(NH, P)
        r_, vn, vn2, tmp, o_ = (mem.take(NH, HD) for _ in range(5))
        Sst = mem.take(4, HD)
        xres, hh_, xs2 = mem.take(D), mem.take(D), mem.take(D)
        xT2 = mem.take(KD, P)
        wout = mem.take(KD, D)
        wr = mem.take(KD, NG + NE)
        ss16, m16, r16 = mem.take(16), mem.take(16), mem.take(16)
        ss8, m8, r8, egam, kdec, eglS = (mem.take(NH) for _ in range(6))
        mx, mm_, nm_, es_, den, rcp = ([mem.take(GQA) for _ in range(2)] for _ in range(6))
        ssx, msx, rsx = mem.take(1), mem.take(1), mem.take(1)
        LV = 7

        ORD = (0, 2, 1, 3)
        SLOT = (0, 2, 4, 6, 1, 3, 5, 7)

        kqS_ps = flat(4, 2).rearrange("p (a n f e) -> p a n f e", a=2, n=2, f=4)

        def slots(x):
            return x.rearrange("p (a f) d -> p a f d", a=2)

        def natural(x):
            return x.rearrange("p (f a d) -> p a f d", a=2, d=HD)

        def scores_ps(g):
            return flat(2 * g, 2).rearrange("p (h j) -> p h j", h=GQA)

        with nc.Block() as block:
            @block.sync
            def _(sp):
                sp.dma_start(wout, I["w_out"][0].rearrange("(k p) n -> p k n", p=P)).then_inc(S("wout"), 16)
                sp.dma_start(wr[:, :, 0:NG], I["w_router_group"][0].rearrange("(p k) n -> p k n", k=KD)).then_inc(S("wr"), 16)
                sp.dma_start(wr[:, :, NG:], I["w_router_expert"][0].rearrange("(p k) n -> p k n", k=KD)).then_inc(S("wr"), 16)
                with sp.Fori(0, NT) as t:
                    rows = sp.snap(t * P)
                    sp.wait_ge(S("av_ps"), t)
                    sp.dma_start(qst, qf[:, :, bass.ds(rows, P)]).then_inc(S("att_in"), 16)
                    sp.dma_start(kst, kf[:, bass.ds(rows, 2 * P)]).then_inc(S("att_in"), 16)
                    sp.dma_start(kswst, ksw[:, bass.ds(rows, 2 * P)]).then_inc(S("att_in"), 16)
                    sp.dma_start(vst.rearrange("p (a b) -> p a b", b=P), vt[:, bass.ds(t, 2), :]).then_inc(S("att_in"), 16)
                    sp.wait_ge(S("tok_ps"), t)
                    settle(sp)
                    sp.dma_start(yst, y_d[:, :, bass.ds(rows, P)]).then_inc(S("y_in"), 16)
                    sp.wait_ge(S("og"), t)
                    sp.dma_start(szst, sz_d[bass.ds(rows, P), :]).then_inc(S("sz_in"), 16)
                    sp.wait_ge(S("h"), t)
                    sp.dma_start(xres, I["x_prompt"][0, bass.ds(rows, P), :]).then_inc(S("xres"), 16)
                sp.wait_ge(S("h"), NT)
                sp.dma_start(xres[0:DEC, :], I["x_sample"][:, 0, :]).then_inc(S("xres"), 16)
                sp.wait_ge(S("S"), NT + 1)
                for hp in range(2):
                    sp.dma_start(O["state_S_prompt"][0, 0, hp::2].rearrange("h d e -> d h e"), Sst[hp * HD:(hp + 1) * HD]).then_inc(S("o3"), 16)
                sp.wait_ge(S("o3"), 32)

            @block.gpsimd
            def _(g):
                g.memset(Sst, 0.0).then_inc(S("S"), 1)
                g.wait_ge(S("S"), 1)

                def rms_pow(name, out, in_, n, t):
                    g.wait_ge(S("m_" + name), t + 1)
                    g.tensor_tensor(out, in_, half[0:out.shape[0]].to_broadcast([out.shape[0], n]), ALU.pow).then_inc(S("r_" + name), 1)

                with g.Fori(0, NT) as t:
                    g.wait_ge(S("gam_ps"), t)
                    g.tensor_tensor(gU, bm(cst[:, C_U:C_U + P], NH), bc(gb[:, t, NH:2 * NH], P), ALU.mult).then_inc(S("gU"), 1)
                    rms_pow("qk", r16, m16, 16, t)
                    for l in range(LV):
                        if l == 0:
                            g.wait_ge(S("AT"), t + 1)
                            g.wait_ge(S("X1_ps"), (LV - 1) * t)
                        elif l >= 3:
                            g.wait_ge(S("X1_ps"), (LV - 1) * t + l - 2)
                        elif l == 2:
                            g.wait_ge(S("MT1"), LV * t + 1)
                        g.tensor_tensor(Lo[l % 2], AT, bm(cst[:, C_LV + l * P:C_LV + (l + 1) * P], NH), ALU.mult).then_inc(S("Lo"), 1)
                    rms_pow("o", r8, m8, NH, t)
                    rms_pow("x", rsx, msx, 1, t)
                rms_pow("x", rsx[0:DEC], msx[0:DEC], 1, NT)

            @block.vector
            def _(v):
                V = nc.vector

                def h_rows(t, R, dst):
                    v.wait_ge(S("proj_ps"), t + 1)
                    v.wait_ge(S("xres"), 16 * t + 16)
                    v.wait_ge(S("h_out"), 16 * t)
                    V.tensor_tensor(hh_[0:R], xres[0:R], flat(0, 2)[0:R], ALU.add).then_inc(S("h"), 1)
                    v.wait_ge(S("ssx"), t + 1)
                    V.tensor_scalar(msx[0:R], ssx[0:R], 1.0 / D, EPS, ALU.mult, ALU.add).then_inc(S("m_x"), 1)
                    v.wait_ge(S("r_x"), t + 1)
                    V.tensor_scalar(xs2[0:R], hh_[0:R], rsx[0:R], None, ALU.mult).then_inc(S("xs2"), 1)
                    v.wait_ge(S("xT2_ps"), t + 1)
                    V.tensor_tensor(xT2[:, :, 0:R], flat(4, 2).rearrange("p (k c) -> p k c", c=P)[:, :, 0:R], bc(g_ffn, R), ALU.mult).then_inc(S("xT2"), 1)
                    v.wait_ge(S("lg_ps"), t + 1)
                    V.tensor_copy(dst, bank(6)[0:R, 256:256 + NG + NE]).then_inc(S("lg"), 1)

                with v.Fori(0, NT) as t:
                    for g in range(2):
                        v.wait_ge(S(f"sc{g}"), t + 1)
                        V.scalar_tensor_tensor(sA[g], scores_ps(g), HD ** -0.5, biasS[:, GQA * g:GQA * g + GQA, :], ALU.mult, ALU.add).then_inc(S(f"s{g}"), 1)
                    for g in range(2):
                        v.wait_ge(S(f"s{g}"), t + 1)
                        V.tensor_scalar(sA[g][:, :, 0:P], sA[g][:, :, 0:P], cst[:, bass.ds(C_FLAG + t, 1)], None, ALU.add).then_inc(S(f"sf{g}"), 1)
                    v.wait_ge(S("gam_ps"), t + 1)
                    gB = flat(4, 2).rearrange("p (h i) -> p h i", i=P)
                    gL = gB[:, :, P - 1]
                    V.tensor_copy(m8, bank(6)[:, 0:NH]).then_inc(S("v_gC"), 1)
                    v.wait_ge(S("v_gC"), t + 1)
                    V.tensor_tensor(E_, gB, bc(m8, P), ALU.subtract).then_inc(S("v_D"), 1)
                    V.tensor_tensor(kdec, gL, m8, ALU.subtract).then_inc(S("kd_in"), 1)
                    v.wait_ge(S("v_D"), t + 1)
                    V.tensor_tensor(E_, E_, bm(cst[:, C_NEG:C_NEG + P], NH), ALU.add).then_inc(S("D"), 1)
                    for g in range(2):
                        v.wait_ge(S(f"sf{g}"), t + 1)
                        V.tensor_reduce(mx[g], sA[g], AX.X, ALU.max).then_inc(S(f"v_mx{g}"), 1)
                        v.wait_ge(S(f"v_mx{g}"), t + 1)
                        V.tensor_tensor(mm_[g], mx[g], sinkB[:, GQA * g:GQA * g + GQA], ALU.max).then_inc(S(f"v_mm{g}"), 1)
                        v.wait_ge(S(f"v_mm{g}"), t + 1)
                        V.tensor_scalar(nm_[g], mm_[g], -1.0, None, ALU.mult)
                        V.tensor_tensor(es_[g], sinkB[:, GQA * g:GQA * g + GQA], mm_[g], ALU.subtract).then_inc(S(f"nm{g}"), 1)
                    v.wait_ge(S("sq"), t + 1)
                    V.tensor_reduce(ss16, sq.rearrange("p (h d) -> p h d", d=HD), AX.X, ALU.add).then_inc(S("v_ss"), 1)
                    v.wait_ge(S("v_ss"), t + 1)
                    V.tensor_scalar(m16[:, 0:NH], ss16[:, 0:NH], float(HD), HD * EPS, ALU.mult, ALU.add)
                    V.tensor_scalar(m16[:, NH:], ss16[:, NH:], 1.0, EPS, ALU.mult, ALU.add).then_inc(S("m_qk"), 1)
                    for g in range(2):
                        v.wait_ge(S(f"p{g}"), t + 1)
                        V.tensor_tensor(den[g], den[g], es_[g], ALU.add).then_inc(S(f"v_den{g}"), 1)
                        v.wait_ge(S(f"v_den{g}"), t + 1)
                        V.reciprocal(rcp[g], den[g]).then_inc(S(f"v_rcp{g}"), 1)
                        v.wait_ge(S(f"v_rcp{g}"), t + 1)
                        V.tensor_tensor(sA[g], sA[g], bc(rcp[g], 2 * P), ALU.mult).then_inc(S(f"pn{g}"), 1)
                        if g == 0:
                            v.wait_ge(S("r_qk"), t + 1)
                            V.tensor_tensor(qk.rearrange("p f (a d) -> p (f a) d", d=HD), flat(0, 2).rearrange("p (h d) -> p h d", d=HD),
                                            bc(r16, HD), ALU.mult).then_inc(S("qk"), 1)
                    v.wait_ge(S("G_ps"), t + 1)
                    v.wait_ge(S("E"), t + 1)
                    v.wait_ge(S("Lo"), LV * t)
                    V.tensor_tensor(AT, flat(6, 2).rearrange("p (h i) -> p h i", i=P), E_, ALU.mult).then_inc(S("v_AT"), 1)
                    v.wait_ge(S("v_AT"), t + 1)
                    V.tensor_tensor(AT, AT, bc(gb[:, t, 0:NH], P), ALU.mult).then_inc(S("AT"), 1)
                    v.wait_ge(S("QK_ps"), t + 1)
                    V.tensor_tensor(QK, flat(4, 2).rearrange("p (h i) -> p h i", i=P), E_, ALU.mult).then_inc(S("QK"), 1)
                    v.wait_ge(S("Lo"), LV * t + 1)
                    for g in range(2):
                        hs = slice(4 * g, 4 * g + 4)
                        V.tensor_tensor(MT[0][:, hs], bm(ident, 4), Lo[0][:, hs], ALU.subtract).then_inc(S(f"MT{g}"), 1)
                    for l in range(1, LV):
                        for g in range(2):
                            hs = slice(4 * g, 4 * g + 4)
                            v.wait_ge(S(f"PT{g}_ps"), (LV - 1) * t + l)
                            V.tensor_tensor(MT[l % 2][:, hs], MT[(l - 1) % 2][:, hs], bank(6 + g).rearrange("p (h i) -> p h i", i=P),
                                            ALU.subtract).then_inc(S(f"MT{g}"), 1)
                    v.wait_ge(S("egam"), t + 1)
                    v.wait_ge(S("kS_ps"), t + 1)
                    V.tensor_tensor(slots(tmp), kqS_ps[:, :, 0], slots(bc(egam, HD)), ALU.mult).then_inc(S("v_kS"), 1)
                    v.wait_ge(S("v_kS"), t + 1)
                    V.tensor_tensor(r_, vtok, tmp, ALU.subtract).then_inc(S("r"), 1)
                    v.wait_ge(S("r"), t + 1)
                    V.tensor_tensor(slots(tmp), kqS_ps[:, :, 1], slots(bc(egam, HD)), ALU.mult).then_inc(S("v_qS"), 1)
                    v.wait_ge(S("v_ps"), t + 1)
                    V.tensor_tensor(vn, bank(2).rearrange("p (h d) -> p h d", d=HD), bc(gb[:, t, 0:NH], HD), ALU.mult).then_inc(S("vn"), 1)
                    v.wait_ge(S("vn"), t + 1)
                    V.tensor_tensor(vn2, vn, bc(kdec, HD), ALU.mult).then_inc(S("vn2"), 1)
                    v.wait_ge(S("o_ps"), t + 1)
                    V.tensor_tensor(o_, bank(3).rearrange("p (h d) -> p h d", d=HD), tmp, ALU.add).then_inc(S("o"), 1)
                    V.tensor_tensor(Sst, Sst, bc(eglS[:, 0:4], HD), ALU.mult).then_inc(S("v_S"), 1)
                    v.wait_ge(S("v_S"), t + 1)
                    v.wait_ge(S("dS_ps"), t + 1)
                    V.tensor_tensor(Sst, Sst, bank(6)[:, 0:4 * HD].rearrange("p (f e) -> p f e", e=HD), ALU.add).then_inc(S("S"), 1)
                    v.wait_ge(S("osq"), t + 1)
                    V.tensor_reduce(ss8, tmp, AX.X, ALU.add).then_inc(S("v_ss8"), 1)
                    v.wait_ge(S("v_ss8"), t + 1)
                    V.tensor_scalar(m8, ss8, 1.0 / HD, EPS, ALU.mult, ALU.add).then_inc(S("m_o"), 1)
                    v.wait_ge(S("sz_in"), 16 * t + 16)
                    V.tensor_tensor(slots(r_), natural(szst), slots(bm(normB, NH)), ALU.mult).then_inc(S("v_sz"), 1)
                    v.wait_ge(S("r_o"), t + 1)
                    V.tensor_tensor(o_, o_, bc(r8, HD), ALU.mult).then_inc(S("v_on"), 1)
                    v.wait_ge(S("v_on"), t + 1)
                    V.tensor_tensor(natural(vn.rearrange("p h d -> p (h d)")), slots(o_), slots(r_), ALU.mult).then_inc(S("og"), 1)
                    h_rows(t, P, lg[:, t, :])
                h_rows(NT, DEC, lg[0:DEC, NT, :])

            @block.scalar
            def _(act):
                A = nc.scalar

                def norm_rows(t, R, rows):
                    act.wait_ge(S("h"), t + 1)
                    act.wait_ge(S("xT2_ps"), t)
                    act.wait_ge(S("xs_out"), 16 * t)
                    A.activation(xs2[0:R], hh_[0:R], ACT.Square, accum_out=ssx[0:R]).then_inc(S("ssx"), 1)
                    act.dma_start(h_d[rows, :], hh_[0:R]).then_inc(S("h_out"), 16)
                    act.wait_ge(S("xs2"), t + 1)
                    act.dma_start(xs_d[rows, :], xs2[0:R]).then_inc(S("xs_out"), 16)

                with act.Fori(0, NT) as t:
                    act.wait_ge(S("tok_ps"), t + 1)
                    A.activation(sq, flat(0, 2), ACT.Square).then_inc(S("sq"), 1)
                    A.activation(slots(vtok), natural(bank(7)), ACT.Copy).then_inc(S("vtok"), 1)
                    act.wait_ge(S("D"), t + 1)
                    act.wait_ge(S("kd_in"), t + 1)
                    A.activation(E_, E_, ACT.Exp).then_inc(S("E"), 1)
                    A.activation(kdec, kdec, ACT.Exp)
                    A.activation(egam, bank(6)[:, 0:NH], ACT.Exp)
                    gL = flat(4, 2).rearrange("p (h i) -> p h i", i=P)[:, :, P - 1]
                    A.activation(eglS[0:HD, 0:4], gL[0:HD, 0:4], ACT.Exp)
                    A.activation(eglS[HD:P, 0:4], gL[HD:P, 4:8], ACT.Exp).then_inc(S("egam"), 1)
                    for g in range(2):
                        act.wait_ge(S(f"nm{g}"), t + 1)
                        for i in range(GQA):
                            A.activation(sA[g][:, i, :], sA[g][:, i, :], ACT.Exp, bias=nm_[g][:, i:i + 1], accum_out=den[g][:, i:i + 1])
                        A.activation(es_[g], es_[g], ACT.Exp).then_inc(S(f"p{g}"), 1)
                    act.wait_ge(S("pT0_ps"), t + 1)
                    A.activation(pT, flat(2, 2).rearrange("p (a q) -> p a q", q=P), ACT.Copy).then_inc(S("pT0"), 1)
                    act.wait_ge(S("qkT_ps"), t + 1)
                    A.activation(qkT, flat(4, 2).rearrange("p (a q) -> p a q", q=P), ACT.Copy).then_inc(S("qkT"), 1)
                    act.wait_ge(S("pT1_ps"), t + 1)
                    act.wait_ge(S("av0_ps"), t + 1)
                    A.activation(pT, flat(0, 2).rearrange("p (a q) -> p a q", q=P), ACT.Copy).then_inc(S("pT1"), 1)
                    act.wait_ge(S("av_ps"), t + 1)
                    A.activation(mix[:, 0:4, :], bank(2).rearrange("p (f q) -> p f q", q=P), ACT.Copy).then_inc(S("mixA"), 1)
                    for l in range(LV):
                        for g in range(2):
                            hs = slice(4 * g, 4 * g + 4)
                            if l > 0:
                                act.wait_ge(S(f"X{g}_ps"), (LV - 1) * t + l)
                                A.activation(Xs[:, hs], bank(2 + g).rearrange("p (h i) -> p h i", i=P), ACT.Copy).then_inc(S(f"X{g}"), 1)
                        for g in range(2):
                            hs = slice(4 * g, 4 * g + 4)
                            if l < LV - 1:
                                act.wait_ge(S(f"Tr{g}_ps"), (LV - 1) * t + l + 1)
                                A.activation(M_[:, hs], bank(g).rearrange("p (h i) -> p h i", i=P), ACT.Copy).then_inc(S(f"M{g}"), 1)
                    act.wait_ge(S("o"), t + 1)
                    A.activation(tmp, o_, ACT.Square).then_inc(S("osq"), 1)
                    act.wait_ge(S("oT_ps"), t + 1)
                    A.activation(mix[:, 4:8, :], bank(7).rearrange("p (f q) -> p f q", q=P), ACT.Copy).then_inc(S("mixB"), 1)
                    norm_rows(t, P, bass.ds(t * P, P))
                norm_rows(NT, DEC, slice(SEQ, TOK))
                act.wait_ge(S("h_out"), 16 * (NT + 1))
                act.wait_ge(S("xs_out"), 16 * (NT + 1))

            @block.tensor
            def _(pe):
                T = nc.tensor

                def half_of(h):
                    return slice((h % 2) * HD, (h % 2) * HD + HD)

                def out_rows(t, R, src):
                    for n in range(2):
                        for k in range(KD):
                            mm = T.matmul(bank(n)[0:R], src[:, k, :], wout[:, k, n * 512:(n + 1) * 512], start=(k == 0), stop=(k == KD - 1))
                    mm.then_inc(S("proj_ps"), 1)
                    pe.wait_ge(S("xs2"), t + 1)
                    for k in range(KD):
                        mm = T.transpose(flat(4, 2)[:, k * P:k * P + R], xs2[0:R].rearrange("p (c k) -> p k c", k=KD)[:, k, :], ident[0:R, 0:R])
                    mm.then_inc(S("xT2_ps"), 1)
                    pe.wait_ge(S("xT2"), t + 1)
                    pe.wait_ge(S("wr"), 32)
                    for k in range(KD):
                        mm = T.matmul(bank(6)[0:R, 256:256 + NG + NE], xT2[:, k, 0:R], wr[:, k, :], start=(k == 0), stop=(k == KD - 1))
                    mm.then_inc(S("lg_ps"), 1)

                with pe.Fori(0, NT) as t:
                    pe.wait_ge(S("att_in"), 64 * t + 64)
                    pe.wait_ge(S("h"), t)
                    for g in range(2):
                        for i in range(GQA):
                            h = GQA * g + ORD[i]
                            ks = kst if h % 2 == g else kswst
                            mm = T.matmul(scores_ps(g)[:, i, :], qst[half_of(h), h // 2, :], ks[half_of(h), :], start=True, stop=True)
                        mm.then_inc(S(f"sc{g}"), 1)
                    pe.wait_ge(S("gU"), t + 1)
                    pe.wait_ge(S("lg"), t)
                    T.matmul(bank(6)[:, 0:NH], cst[:, C_U:C_U + P], gb[:, t, NH:2 * NH], start=True, stop=True)
                    for n in range(2):
                        mm = T.matmul(bank(4 + n), ones, gU[:, 4 * n:4 * n + 4].rearrange("p h i -> p (h i)"), start=True, stop=True)
                    mm.then_inc(S("gam_ps"), 1)
                    pe.wait_ge(S("y_in"), 16 * t + 16)
                    pe.wait_ge(S("s0"), t + 1)
                    pe.wait_ge(S("mixB"), t)
                    for f in range(4):
                        T.transpose(bank(7)[:, f * P:(f + 1) * P], yst[:, 8 + f, :], ident)
                    for f in range(8):
                        mm = T.transpose(flat(0, 2)[:, f * P:(f + 1) * P], yst[:, f, :], ident)
                    mm.then_inc(S("tok_ps"), 1)
                    pe.wait_ge(S("pn0"), t + 1)
                    pe.wait_ge(S("s1"), t + 1)
                    for i in range(GQA):
                        for b in range(2):
                            mm = T.transpose(flat(2, 2)[:, (2 * i + b) * P:(2 * i + b + 1) * P], sA[0][:, i, b * P:(b + 1) * P], ident)
                    mm.then_inc(S("pT0_ps"), 1)
                    pe.wait_ge(S("qk"), t + 1)
                    pe.wait_ge(S("D"), t + 1)
                    pe.wait_ge(S("egam"), t + 1)
                    for f in range(8):
                        mm = T.transpose(flat(4, 2)[:, f * P:(f + 1) * P], qk[:, f, :], ident)
                    mm.then_inc(S("qkT_ps"), 1)
                    pe.wait_ge(S("pn1"), t + 1)
                    for i in range(GQA):
                        for b in range(2):
                            mm = T.transpose(flat(0, 2)[:, (2 * i + b) * P:(2 * i + b + 1) * P], sA[1][:, i, b * P:(b + 1) * P], ident)
                    mm.then_inc(S("pT1_ps"), 1)
                    pe.wait_ge(S("qkT"), t + 1)
                    pe.wait_ge(S("vtok"), t + 1)
                    for s, h in enumerate(SLOT):
                        kT = qkT[half_of(h), 4 + h // 2, :]
                        mm = T.matmul(flat(6, 2)[:, s * P:(s + 1) * P], kT, kT, start=True, stop=True)
                    mm.then_inc(S("G_ps"), 1)
                    for s, h in enumerate(SLOT):
                        mm = T.matmul(flat(4, 2)[:, s * P:(s + 1) * P], qkT[half_of(h), 4 + h // 2, :], qkT[half_of(h), h // 2, :], start=True, stop=True)
                    mm.then_inc(S("QK_ps"), 1)

                    def values(g):
                        pe.wait_ge(S(f"pT{g}"), t + 1)
                        for i in range(GQA):
                            h = GQA * g + ORD[i]
                            for b in range(2):
                                mm = T.matmul(bank(2)[half_of(h), (h // 2) * P:(h // 2 + 1) * P], vst[:, b * P + g * HD:b * P + g * HD + HD],
                                              pT[:, 2 * i + b, :], start=(b == 0), stop=(b == 1))
                        return mm

                    values(0).then_inc(S("av0_ps"), 1)
                    values(1).then_inc(S("av_ps"), 1)
                    pe.wait_ge(S("mixA"), t + 1)
                    for l in range(LV):
                        if l > 0:
                            for g in range(2):
                                pe.wait_ge(S(f"M{g}"), (LV - 1) * t + l)
                                pe.wait_ge(S("Lo"), LV * t + l + 1)
                                for h in range(4 * g, 4 * g + 4):
                                    mm = T.matmul(bank(2 + g)[:, (h % 4) * P:(h % 4 + 1) * P], Lo[l % 2][:, h, :], M_[:, h, :], start=True, stop=True)
                                mm.then_inc(S(f"X{g}_ps"), 1)
                            for g in range(2):
                                pe.wait_ge(S(f"X{g}"), (LV - 1) * t + l)
                                if l == 1:
                                    pe.wait_ge(S("AT"), t + 1)
                                for h in range(4 * g, 4 * g + 4):
                                    mm = T.matmul(bank(6 + g)[:, (h % 4) * P:(h % 4 + 1) * P], Xs[:, h, :], MT[(l - 1) % 2][:, h, :], start=True, stop=True)
                                mm.then_inc(S(f"PT{g}_ps"), 1)
                        if l < LV - 1:
                            for g in range(2):
                                pe.wait_ge(S(f"MT{g}"), LV * t + l + 1)
                                if l == 0:
                                    pe.wait_ge(S("pT1"), t + 1)
                                for h in range(4 * g, 4 * g + 4):
                                    mm = T.transpose(bank(g)[:, (h % 4) * P:(h % 4 + 1) * P], MT[l % 2][:, h, :], ident)
                                mm.then_inc(S(f"Tr{g}_ps"), 1)
                    pe.wait_ge(S("S"), t + 1)
                    pe.wait_ge(S("QK"), t + 1)
                    for n in range(2):
                        for h in SLOT:
                            mm = T.matmul(kqS_ps[:, h % 2, n, h // 2, :], qkT[half_of(h), 4 - 4 * n + h // 2, :], Sst[half_of(h), h // 2, :], start=True, stop=True)
                    mm.then_inc(S("kS_ps"), 1)
                    pe.wait_ge(S("r"), t + 1)
                    pe.wait_ge(S("MT0"), LV * t + LV)
                    pe.wait_ge(S("MT1"), LV * t + LV)
                    for h in range(NH):
                        mm = T.matmul(bank(2)[:, h * HD:(h + 1) * HD], MT[(LV - 1) % 2][:, h, :], r_[:, h, :], start=True, stop=True)
                    mm.then_inc(S("v_ps"), 1)
                    pe.wait_ge(S("vn"), t + 1)
                    for h in range(NH):
                        mm = T.matmul(bank(3)[:, h * HD:(h + 1) * HD], QK[:, h, :], vn[:, h, :], start=True, stop=True)
                    mm.then_inc(S("o_ps"), 1)
                    pe.wait_ge(S("vn2"), t + 1)
                    for s, h in enumerate(SLOT):
                        mm = T.matmul(bank(6)[half_of(h), (h // 2) * HD:(h // 2 + 1) * HD], qk[:, 4 + h // 2, half_of(h)], vn2[:, s, :], start=True, stop=True)
                    mm.then_inc(S("dS_ps"), 1)
                    pe.wait_ge(S("og"), t + 1)
                    for f in range(4):
                        mm = T.transpose(bank(7)[:, f * P:(f + 1) * P], vn.rearrange("p h d -> p (h d)")[:, f * P:(f + 1) * P], ident)
                    mm.then_inc(S("oT_ps"), 1)
                    pe.wait_ge(S("mixB"), t + 1)
                    pe.wait_ge(S("wout"), 16)
                    out_rows(t, P, mix)
                pe.wait_ge(S("h"), NT)
                out_rows(NT, DEC, mixD)

        stage_ends()
        mem.at = stay
        NTT = NT + 1
        fill = mem.take(MAXB, 4).bitcast(I32)
        gmx, pm, sm, pgs, m1, m2, ex, dn, gate1, gate2 = (mem.take(NTT) for _ in range(10))
        eqg, selg, exg = mem.take(NTT, NG), mem.take(NTT, NG), mem.take(NTT, NG)
        wide, oh1, oh2, slotE, geb = (mem.take(NTT, NE) for _ in range(5))
        mask = mem.take(NTT, NE)
        le, le2, q1, q2, e1h, e2h = (mem.take(NTT, EPG) for _ in range(6))
        cnt, ext, incl, base = (mem.take(NE) for _ in range(4))
        cmp8 = mem.take(NE, 8)
        cmpo, cmpo2, eo = mem.take(XB, NE), mem.take(XB, NE), mem.take(XB + 1)
        dst, dsti = mem.take(2, NTT), mem.take(2, NTT).bitcast(I32)
        pay = mem.take(2, NTT * 4).rearrange("p k (t c) -> p k t c", c=4).bitcast(I32)
        tabrow = mem.take(P, 4)

        def cols(c0, n):
            return cst[:, c0:c0 + n]

        with nc.Block() as block:
            @block.vector
            def _(v):
                V = nc.vector
                tick = [0]

                def chain(ins):
                    tick[0] += 1
                    ins.then_inc(S("dve_route"), 1)
                    v.wait_ge(S("dve_route"), tick[0])

                def first(values, best, prio, marks, out):
                    n = values.shape[2]
                    chain(V.tensor_tensor(marks, values, bc(best, n), ALU.is_ge))
                    chain(V.tensor_tensor(marks, marks, bm(prio, NTT), ALU.mult))
                    chain(V.tensor_reduce(pm, marks, AX.X, ALU.max))
                    chain(V.tensor_tensor(out, marks, bc(pm, n), ALU.is_equal))

                chain(V.memset(fill, 0))
                chain(V.memset(fill[:, :, 1], DUMP))
                V.memset(pay, 0).then_inc(S("fill"), 1)
                G = lg[:, :, 0:NG]
                chain(V.tensor_reduce(gmx, G, AX.X, ALU.max))
                V.tensor_tensor(exg, G, bc(gmx, NG), ALU.subtract).then_inc(S("exg"), 1)
                first(G, gmx, cols(C_GP, NG), eqg, selg)
                w4 = wide.rearrange("p t (g j) -> p t g j", g=NG)
                l4 = lg[:, :, NG:].rearrange("p t (g j) -> p t g j", g=NG)
                s4 = selg.unsqueeze(3).to_broadcast([P, NTT, NG, EPG])
                chain(V.tensor_tensor(w4, l4, s4, ALU.mult))
                chain(V.tensor_reduce(le, wide.rearrange("p t (g j) -> p t j g", g=NG), AX.X, ALU.add))
                chain(V.tensor_reduce(m1, le, AX.X, ALU.max))
                first(le, m1, cols(C_EP, EPG), q1, e1h)
                chain(V.scalar_tensor_tensor(le2, e1h, -BIG, le, ALU.mult, ALU.add))
                chain(V.tensor_reduce(m2, le2, AX.X, ALU.max))
                first(le2, m2, cols(C_EP, EPG), q2, e2h)
                V.tensor_tensor(ex, m2, m1, ALU.subtract).then_inc(S("ex"), 1)
                val = cols(C_VAL, NTT)
                for e_, o in ((e1h, oh1), (e2h, oh2)):
                    o4 = o.rearrange("p t (g j) -> p t g j", g=NG)
                    chain(V.tensor_tensor(o4, s4, e_.unsqueeze(2).to_broadcast([P, NTT, NG, EPG]), ALU.mult))
                    chain(V.tensor_tensor(o, o, bc(val, NE), ALU.mult))
                V.tensor_tensor(mask, oh1, oh2, ALU.add).then_inc(S("mask"), 1)
                v.wait_ge(S("exps"), 1)
                chain(V.tensor_reduce(sm, exg, AX.X, ALU.add))
                chain(V.tensor_scalar(dn, ex, 1.0, None, ALU.add))
                chain(V.tensor_tensor(dn, dn, sm, ALU.mult))
                chain(V.reciprocal(gate1, dn))
                chain(V.tensor_tensor(gate2, gate1, ex, ALU.mult))
                for k, gt in ((0, gate1), (1, gate2)):
                    V.tensor_copy(pay[:, k, :, 0], cols(C_TT, NTT))
                    V.tensor_scalar(pay[:, k, :, 1], cols(C_TT, NTT), float(k * TOK), None, ALU.add)
                    chain(V.tensor_copy(pay[:, k, :, 2], gt.bitcast(I32)))
                v.wait_ge(S("pos"), 1)
                pos = bank(0)[:, 0:NTT * NE].rearrange("p (t e) -> p t e", e=NE)
                chain(V.tensor_copy(cnt, bank(1)[:, 0:NE]))
                chain(V.tensor_tensor(cmp8, bc(cnt, 8), bm(cols(C_THR, 8), NE), ALU.is_gt))
                chain(V.tensor_reduce(ext, cmp8, AX.X, ALU.add))
                chain(V.tensor_tensor_scan(incl, ones[:, 0:NE], ext, 0.0, ALU.mult, ALU.add))
                chain(V.tensor_tensor(base, incl, ext, ALU.subtract))
                chain(V.tensor_tensor(cmpo, bc(cols(C_OV, XB), NE), bm(base, XB), ALU.is_ge))
                chain(V.tensor_scalar(base, base, float(P), float((NE - 1) * P), ALU.mult, ALU.add))
                chain(V.tensor_tensor(base, base, cols(C_E128, NE), ALU.subtract))
                chain(V.tensor_scalar(geb, pos, float(P), None, ALU.is_ge))
                chain(V.tensor_tensor(geb, geb, bm(base, NTT), ALU.mult))
                chain(V.tensor_tensor(slotE, pos, bm(cols(C_E128, NE), NTT), ALU.add))
                chain(V.tensor_tensor(slotE, slotE, geb, ALU.add))
                for k, o in ((0, oh1), (1, oh2)):
                    chain(V.tensor_tensor(wide, slotE, o, ALU.mult))
                    chain(V.tensor_reduce(dst[:, k], wide, AX.X, ALU.add))
                chain(V.tensor_scalar(pm, val, -float(DUMP), float(DUMP), ALU.mult, ALU.add))
                chain(V.tensor_tensor(dst, dst, bm(pm, 2), ALU.add))
                V.tensor_copy(dsti, dst).then_inc(S("dst"), 1)
                chain(V.tensor_tensor(cmpo2, bc(cols(C_OV, XB), NE), bm(incl, XB), ALU.is_lt))
                chain(V.tensor_tensor(cmpo, cmpo, cmpo2, ALU.mult))
                chain(V.tensor_tensor(cmpo, cmpo, bm(cols(C_EI, NE), XB), ALU.mult))
                chain(V.tensor_reduce(eo[:, 0:XB], cmpo, AX.X, ALU.add))
                chain(V.tensor_copy(eo[:, XB:], incl[:, NE - 1:NE]))
                V.tensor_copy(blk[0:1], eo[0:1]).then_inc(S("blk"), 1)
                v.wait_ge(S("tabT"), 1)
                V.tensor_copy(tabI[:, 0:3], bank(2)[:, 0:3 * MAXB].rearrange("p (c b) -> p c b", b=MAXB).bitcast(I32)).then_inc(S("tabI"), 1)

            @block.scalar
            def _(act):
                act.wait_ge(S("exg"), 1)
                nc.scalar.activation(exg, exg, ACT.Exp)
                act.wait_ge(S("ex"), 1)
                nc.scalar.activation(ex, ex, ACT.Exp).then_inc(S("exps"), 1)

            @block.tensor
            def _(pe):
                pe.wait_ge(S("mask"), 1)
                mk = mask.rearrange("p t e -> p (t e)")
                nc.tensor.matmul(bank(0)[:, 0:NTT * NE], cols(C_US, P), mk, start=True, stop=False, skip_group_check=True)
                for s in range(1, NTT):
                    nc.tensor.matmul(bank(0)[:, s * NE:NTT * NE], ones, mk[:, 0:(NTT - s) * NE], start=False, stop=(s == NTT - 1), skip_group_check=True)
                for t in range(NTT):
                    mm = nc.tensor.matmul(bank(1)[:, 0:NE], ones, mask[:, t, :], start=(t == 0), stop=(t == NTT - 1))
                mm.then_inc(S("pos"), 1)
                pe.wait_ge(S("tabrow"), 16)
                for c in range(3):
                    mm = nc.tensor.transpose(bank(2)[:, c * MAXB:(c + 1) * MAXB], tabrow[0:MAXB, :, c], ident[0:MAXB, 0:MAXB])
                mm.then_inc(S("tabT"), 1)

            @block.gpsimd
            def _(g):
                g.wait_ge(S("fill"), 1)
                g.dma_start(tab_d.rearrange("(p b) c -> p b c", b=MAXB), fill).then_inc(S("filled"), 16)
                g.wait_ge(S("filled"), 16)
                g.wait_ge(S("dst"), 1)
                n = 0
                for k in range(2):
                    for t in range(NTT):
                        g.indirect_dma_start(out=tab_d, out_offset=bass.IndirectOffsetOnAxis(ap=dsti[:, k, t:t + 1], axis=0),
                                             in_=pay[:, k, t, :], in_offset=None, bounds_check=MAXB * P - 1, oob_is_err=False).then_inc(S("scat"), 16)
                        n += 16
                g.wait_ge(S("scat"), n)
                g.dma_start(tabrow[0:MAXB].bitcast(I32), tab_d.rearrange("(b s) c -> b s c", s=P)).then_inc(S("tabrow"), 16)
                g.wait_ge(S("tabrow"), 16)

        stage_ends()
        mem.at = stay
        U = 4
        wgu = [mem.take(KD, 2 * DE) for _ in range(U)]
        wd = [mem.take(KE, D) for _ in range(U)]
        xg = [mem.take(D) for _ in range(U)]
        xgT = [mem.take(KD, P) for _ in range(2)]
        sg = [mem.take(DE) for _ in range(2)]
        hm = [mem.take(DE) for _ in range(2)]
        hT = [mem.take(KE, P) for _ in range(2)]
        ye = [mem.take(D) for _ in range(2)]
        it, io = ([mem.take(1).bitcast(I32) for _ in range(U)] for _ in range(2))
        gt = [mem.take(1) for _ in range(U)]

        class Slot:

            def __init__(self, u, n, b, alone=None):
                self.u, self.n, self.b = u, n, b
                self.v = u % 2
                self.m = 2 * n + u // 2 if alone is None else alone
                self.c = b if alone is None else alone
                self.a, self.h = f"{u}", f"{u % 2}h"

        def load_block(sp, s, e):
            sp.wait_ge(S("down" + s.a), s.n)
            for w, lo in (("w_gate", 0), ("w_up", DE)):
                sp.dma_start(wgu[s.u][:, :, lo:lo + DE], I[w][0, bass.ds(e, 1)].rearrange("a (p k) n -> p (a k) n", k=KD)).then_inc(S("wgu" + s.a), 16)
            sp.dma_start(wd[s.u].rearrange("p k n -> p (k n)"), I["w_down"][0, bass.ds(e, 1)].rearrange("a (p k) n -> p (a k n)", k=KE)).then_inc(S("wd" + s.a), 16)

        def gather(g, s):
            g.wait_ge(S("xgT_ps" + s.a), s.n)
            g.wait_ge(S("hm" + s.a), s.n)
            g.tensor_copy(it[s.u], tabI[:, 0, bass.ds(s.b, 1)])
            g.tensor_copy(gt[s.u].bitcast(I32), tabI[:, 2, bass.ds(s.b, 1)]).then_inc(S("idx" + s.a), 1)
            g.wait_ge(S("idx" + s.a), s.n + 1)
            settle(g)
            g.indirect_dma_start(out=xg[s.u], out_offset=None, in_=xs_d,
                                 in_offset=bass.IndirectOffsetOnAxis(ap=it[s.u], axis=0)).then_inc(S("xg" + s.a), 16)

        def scatter(g, s):
            g.wait_ge(S("ye_out" + s.a), 16 * s.n)
            g.tensor_copy(io[s.u], tabI[:, 1, bass.ds(s.b, 1)]).then_inc(S("rows" + s.a), 1)
            g.wait_ge(S("ye" + s.h), s.m + 1)
            g.wait_ge(S("rows" + s.a), s.n + 1)
            settle(g)
            g.indirect_dma_start(out=ye_d, out_offset=bass.IndirectOffsetOnAxis(ap=io[s.u], axis=0), in_=ye[s.v], in_offset=None,
                                 bounds_check=2 * TOK - 1, oob_is_err=False).then_inc(S("ye_out" + s.a), 16)

        def turn_block(pe, s):
            pe.wait_ge(S("xg" + s.a), 16 * s.n + 16)
            pe.wait_ge(S("xgT_all"), s.c)
            for k in range(KD):
                mm = nc.tensor.transpose(flat(0, 2)[:, k * P:(k + 1) * P], xg[s.u].rearrange("p (c k) -> p k c", k=KD)[:, k, :], ident)
            mm.then_inc(S("xgT_ps" + s.a), 1)

        def up_block(pe, s):
            pe.wait_ge(S("xgT" + s.h), s.m + 1)
            pe.wait_ge(S("wgu" + s.a), 32 * s.n + 32)
            pe.wait_ge(S("hm" + s.h), s.m)
            for k in range(KD):
                mm = nc.tensor.matmul(bank(2 + s.v), xgT[s.v][:, k, :], wgu[s.u][:, k, :], start=(k == 0), stop=(k == KD - 1))
            mm.then_inc(S("gu" + s.h), 1)

        def turn_hidden(pe, s):
            pe.wait_ge(S("hm" + s.h), s.m + 1)
            pe.wait_ge(S("hT_all"), s.c)
            for k in range(KE):
                mm = nc.tensor.transpose(bank(4)[:, k * P:(k + 1) * P], hm[s.v].rearrange("p (c k) -> p k c", k=KE)[:, k, :], ident)
            mm.then_inc(S("hT_ps" + s.h), 1)

        def down_block(pe, s):
            pe.wait_ge(S("hT" + s.h), s.m + 1)
            pe.wait_ge(S("wd" + s.a), 16 * s.n + 16)
            pe.wait_ge(S("ye_all"), s.c)
            for n in range(2):
                for k in range(KE):
                    mm = nc.tensor.matmul(bank(6 + n), hT[s.v][:, k, :], wd[s.u][:, k, n * 512:(n + 1) * 512], start=(k == 0), stop=(k == KE - 1))
            mm.then_inc(S("down" + s.a), 1)

        def gain_block(v, s):
            v.wait_ge(S("xgT_ps" + s.a), s.n + 1)
            v.wait_ge(S("gu" + s.h), s.m)
            nc.vector.tensor_tensor(xgT[s.v], flat(0, 2).rearrange("p (k c) -> p k c", c=P), bc(g_ffn, P), ALU.mult).then_inc(S("xgT" + s.h), 1)
            v.wait_ge(S("xgT" + s.h), s.m + 1)
            v.sem_inc(S("xgT_all"), 1)

        def hidden_block(v, s):
            v.wait_ge(S("sg" + s.h), s.m + 1)
            v.wait_ge(S("idx" + s.a), s.n + 1)
            v.wait_ge(S("hT_ps" + s.h), s.m)
            nc.vector.scalar_tensor_tensor(hm[s.v], sg[s.v], gt[s.u], bank(2 + s.v)[:, DE:], ALU.mult, ALU.mult).then_inc(S("hm" + s.h), 1)
            v.wait_ge(S("hm" + s.h), s.m + 1)
            v.sem_inc(S("hm" + s.a), 1)

        def hidden_out(v, s):
            v.wait_ge(S("hT_ps" + s.h), s.m + 1)
            nc.vector.tensor_copy(hT[s.v].rearrange("p k c -> p (k c)"), bank(4)[:, 0:KE * P]).then_inc(S("hT" + s.h), 1)
            v.wait_ge(S("hT" + s.h), s.m + 1)
            v.sem_inc(S("hT_all"), 1)

        def silu_block(act, s):
            act.wait_ge(S("gu" + s.h), s.m + 1)
            act.wait_ge(S("hm" + s.h), s.m)
            nc.scalar.activation(sg[s.v], bank(2 + s.v)[:, 0:DE], ACT.Silu).then_inc(S("sg" + s.h), 1)

        def out_block(act, s, before, scattered):
            act.wait_ge(S("down" + s.a), s.n + 1)
            if before:
                act.wait_ge(S("ye_out" + before.a), scattered)
            nc.scalar.activation(ye[s.v], flat(6, 2), ACT.Copy).then_inc(S("ye" + s.h), 1)
            act.wait_ge(S("ye" + s.h), s.m + 1)
            act.sem_inc(S("ye_all"), 1)

        def slot(n, u):
            if u < 0:
                return slot(n - 1, u + U)
            if u >= U:
                return slot(n + 1, u - U)
            return Slot(u, n, n * U + u)

        def rounds(eng, body):
            for u in range(U):
                body(0, u, u)
            with eng.Fori(1, NE // U) as n:
                for u in range(U):
                    body(n, u, U)

        with nc.Block() as block:
            @block.sync
            def _(sp):
                with sp.Fori(0, NE // U) as n:
                    for u in range(U):
                        load_block(sp, slot(n, u), sp.snap(n * U + u))

            @block.gpsimd
            def _(g):
                def body(n, u, seen, last=False):
                    if not last:
                        gather(g, slot(n, u + 2))
                    if seen >= 2:
                        scatter(g, slot(n, u - 2))

                gather(g, slot(0, 0))
                gather(g, slot(0, 1))
                for u in range(U):
                    body(0, u, u)
                with g.Fori(1, NE // U - 1) as n:
                    for u in range(U):
                        body(n, u, U)
                for u in range(U):
                    body(NE // U - 1, u, U, last=(u >= U - 2))
                scatter(g, slot(NE // U, -2))
                scatter(g, slot(NE // U, -1))
                for u in range(U):
                    g.wait_ge(S(f"ye_out{u}"), 16 * NE // U)

            @block.tensor
            def _(pe):
                turn_block(pe, slot(0, 0))

                def body(n, u, seen, last=False):
                    up_block(pe, slot(n, u))
                    if seen >= 1:
                        turn_hidden(pe, slot(n, u - 1))
                    if not last:
                        turn_block(pe, slot(n, u + 1))
                    if seen >= 1:
                        down_block(pe, slot(n, u - 1))

                for u in range(U):
                    body(0, u, u)
                with pe.Fori(1, NE // U - 1) as n:
                    for u in range(U):
                        body(n, u, U)
                for u in range(U):
                    body(NE // U - 1, u, U, last=(u == U - 1))
                turn_hidden(pe, slot(NE // U, -1))
                down_block(pe, slot(NE // U, -1))

            @block.vector
            def _(v):
                def body(n, u, seen, last=False):
                    if seen >= 1:
                        hidden_out(v, slot(n, u - 1))
                    if not last:
                        gain_block(v, slot(n, u + 1))
                    hidden_block(v, slot(n, u))

                gain_block(v, slot(0, 0))
                for u in range(U):
                    body(0, u, u)
                with v.Fori(1, NE // U - 1) as n:
                    for u in range(U):
                        body(n, u, U)
                for u in range(U):
                    body(NE // U - 1, u, U, last=(u == U - 1))
                hidden_out(v, slot(NE // U, -1))

            @block.scalar
            def _(act):
                def body(n, u, seen):
                    silu_block(act, slot(n, u))
                    if seen >= 1:
                        s, before = slot(n, u - 1), slot(n, u - 3)
                        out_block(act, s, before if seen >= 3 else None, 16 * before.n + 16)

                rounds(act, body)
                out_block(act, slot(NE // U, -1), slot(NE // U, -3), 16 * NE // U)

        stage_ends()
        with nc.Block() as block:
            def blocks(eng, body):
                count = eng.value_load(blk[0:1, XB:XB + 1], min_val=0, max_val=XB)
                with eng.Fori(0, XB) as o:
                    with eng.If(count > o):
                        body(Slot(0, o, eng.snap(o + NE), o))

            @block.sync
            def _(sp):
                blocks(sp, lambda s: load_block(sp, s, sp.value_load(blk[0:1, bass.ds(s.n, 1)], min_val=0, max_val=NE - 1)))

            @block.gpsimd
            def _(g):
                def body(s):
                    gather(g, s)
                    scatter(g, s)
                    g.wait_ge(S("ye_out0"), 16 * s.n + 16)
                    g.sem_inc(S("scattered"), 1)

                blocks(g, body)

            @block.tensor
            def _(pe):
                def body(s):
                    turn_block(pe, s)
                    up_block(pe, s)
                    turn_hidden(pe, s)
                    down_block(pe, s)

                blocks(pe, body)

            @block.vector
            def _(v):
                def body(s):
                    gain_block(v, s)
                    hidden_block(v, s)
                    hidden_out(v, s)

                blocks(v, body)

            @block.scalar
            def _(act):
                def body(s):
                    silu_block(act, s)
                    out_block(act, s, s, 16 * s.n)

                blocks(act, body)

        stage_ends()
        mem.at = stay
        wpg, wpp = mem.take(KD, D), mem.take(KE, D)
        gfB = mem.take(D)
        hf, y0, y1, xf, sgf, of = ([mem.take(D) for _ in range(2)] for _ in range(6))
        xfT = [mem.take(KD, P) for _ in range(2)]
        pf, pfT = [mem.take(PLE) for _ in range(2)], [mem.take(KE, P) for _ in range(2)]
        sc = [[mem.take(1) for _ in range(6)] for _ in range(2)]

        with nc.Block() as block:
            @block.sync
            def _(sp):
                def load(n, u, t):
                    R, rows = (DEC, slice(SEQ, TOK)) if t is None else (P, bass.ds(t * P, P))
                    yrow = [slice(k * TOK + SEQ, k * TOK + TOK) if t is None else bass.ds(t * P + k * TOK, P) for k in range(2)]
                    psrc = I["p_sample"][0, :, 0, :] if t is None else I["p_prompt"][0, 0, rows, :]
                    sp.wait_ge(S(f"h3{u}"), n)
                    sp.wait_ge(S(f"pT_ps{u}"), n)
                    for dst_, src in ((hf[u], h_d[rows, :]), (y0[u], ye_d[yrow[0], :]), (y1[u], ye_d[yrow[1], :]), (pf[u], psrc)):
                        sp.dma_start(dst_[0:R], src).then_inc(S(f"in{u}"), 16)

                load(0, 0, 0)
                sp.dma_start(wpp, I["w_ple_proj"][0].rearrange("(k p) n -> p k n", p=P)).then_inc(S("wpp"), 16)
                sp.dma_start(wpg, I["w_ple_gate"][0].rearrange("(p k) n -> p k n", k=KD)).then_inc(S("wpg"), 16)
                sp.dma_start(gfB, I["norm_final"].partition_broadcast(P)).then_inc(S("gf"), 16)
                load(0, 1, 1)
                with sp.Fori(1, 4) as n:
                    for u in range(2):
                        load(n, u, sp.snap(2 * n + u))
                load(4, 0, None)

            @block.gpsimd
            def _(g):
                def power(n, u, which):
                    g.wait_ge(S(f"ms{which}{u}"), n + 1)
                    g.tensor_tensor(sc[u][3 * which + 2], sc[u][3 * which + 1], half, ALU.pow).then_inc(S(f"rs{which}{u}"), 1)

                power(0, 0, 0)
                with g.Fori(0, 4) as n:
                    power(n, 1, 0)
                    power(n, 0, 1)
                    power(n + 1, 0, 0)
                    power(n, 1, 1)
                power(4, 0, 1)

            @block.vector
            def _(v):
                V = nc.vector

                def sum_in(n, u):
                    v.wait_ge(S(f"in{u}"), 64 * n + 64)
                    V.tensor_tensor(hf[u], hf[u], y0[u], ALU.add).then_inc(S(f"v_h{u}"), 1)
                    v.wait_ge(S(f"v_h{u}"), n + 1)
                    V.tensor_tensor(hf[u], hf[u], y1[u], ALU.add).then_inc(S(f"h2{u}"), 1)
                    v.wait_ge(S(f"ssA{u}"), n + 1)
                    V.tensor_scalar(sc[u][1], sc[u][0], 1.0 / D, EPS, ALU.mult, ALU.add).then_inc(S(f"ms0{u}"), 1)
                    v.wait_ge(S(f"rs0{u}"), n + 1)
                    V.tensor_scalar(xf[u], hf[u], sc[u][2], None, ALU.mult).then_inc(S(f"xf{u}"), 1)

                def gain(n, u):
                    v.wait_ge(S(f"xfT_ps{u}"), n + 1)
                    v.wait_ge(S(f"gate_ps{u}"), n)
                    V.tensor_tensor(xfT[u], flat(0, 2).rearrange("p (k c) -> p k c", c=P), bc(g_ple, P), ALU.mult).then_inc(S(f"xfT{u}"), 1)
                    v.wait_ge(S(f"pT_ps{u}"), n + 1)
                    v.wait_ge(S(f"pp_ps{u}"), n)
                    V.tensor_copy(pfT[u].rearrange("p k c -> p (k c)"), bank(2)[:, 0:KE * P]).then_inc(S(f"pfT{u}"), 1)

                def close(n, u):
                    v.wait_ge(S(f"pp_ps{u}"), n + 1)
                    v.wait_ge(S(f"sgf{u}"), n + 1)
                    V.tensor_tensor(sgf[u], sgf[u], flat(6, 2), ALU.mult).then_inc(S(f"pg{u}"), 1)
                    v.wait_ge(S(f"pg{u}"), n + 1)
                    V.tensor_tensor(sgf[u], sgf[u], hf[u], ALU.add).then_inc(S(f"h3{u}"), 1)
                    v.wait_ge(S(f"ssB{u}"), n + 1)
                    V.tensor_scalar(sc[u][4], sc[u][3], 1.0 / D, EPS, ALU.mult, ALU.add).then_inc(S(f"ms1{u}"), 1)
                    v.wait_ge(S(f"rs1{u}"), n + 1)
                    v.wait_ge(S("gf"), 16)
                    V.scalar_tensor_tensor(of[u], sgf[u], sc[u][5], gfB, ALU.mult, ALU.mult).then_inc(S(f"of{u}"), 1)

                sum_in(0, 0)
                gain(0, 0)
                with v.Fori(0, 4) as n:
                    sum_in(n, 1)
                    gain(n, 1)
                    close(n, 0)
                    sum_in(n + 1, 0)
                    gain(n + 1, 0)
                    close(n, 1)
                close(4, 0)

            @block.scalar
            def _(act):
                A = nc.scalar

                def square_in(n, u):
                    act.wait_ge(S(f"h2{u}"), n + 1)
                    act.wait_ge(S(f"xfT_ps{u}"), n)
                    A.activation(xf[u], hf[u], ACT.Square, accum_out=sc[u][0]).then_inc(S(f"ssA{u}"), 1)

                def sigmoid(n, u):
                    act.wait_ge(S(f"gate_ps{u}"), n + 1)
                    act.wait_ge(S(f"of{u}"), n)
                    A.activation(sgf[u], flat(4, 2), ACT.Sigmoid).then_inc(S(f"sgf{u}"), 1)

                def close(n, u, rows, R):
                    act.wait_ge(S(f"h3{u}"), n + 1)
                    act.wait_ge(S(f"out{u}"), 16 * n)
                    A.activation(of[u], sgf[u], ACT.Square, accum_out=sc[u][3]).then_inc(S(f"ssB{u}"), 1)
                    act.wait_ge(S(f"of{u}"), n + 1)
                    act.dma_start(O["y_prompt"][0, rows, :] if R == P else O["y_sample"][:, 0, :], of[u][0:R]).then_inc(S(f"out{u}"), 16)

                square_in(0, 0)
                with act.Fori(0, 4) as n:
                    square_in(n, 1)
                    sigmoid(n, 0)
                    close(n, 0, bass.ds(n * 2 * P, P), P)
                    square_in(n + 1, 0)
                    sigmoid(n, 1)
                    close(n, 1, bass.ds(n * 2 * P + P, P), P)
                sigmoid(4, 0)
                close(4, 0, None, DEC)
                act.wait_ge(S("out0"), 80)
                act.wait_ge(S("out1"), 64)

            @block.tensor
            def _(pe):
                def turn(n, u, before):
                    pe.wait_ge(S(f"xf{u}"), n + 1)
                    if before is not None:
                        pe.wait_ge(S(f"xfT{1 - u}"), before)
                        pe.wait_ge(S(f"pfT{1 - u}"), before)
                    for k in range(KD):
                        mm = nc.tensor.transpose(flat(0, 2)[:, k * P:(k + 1) * P], xf[u].rearrange("p (c k) -> p k c", k=KD)[:, k, :], ident)
                    mm.then_inc(S(f"xfT_ps{u}"), 1)
                    for k in range(KE):
                        mm = nc.tensor.transpose(bank(2)[:, k * P:(k + 1) * P], pf[u][:, k * P:(k + 1) * P], ident)
                    mm.then_inc(S(f"pT_ps{u}"), 1)

                def products(n, u, before):
                    pe.wait_ge(S(f"xfT{u}"), n + 1)
                    if before is not None:
                        pe.wait_ge(S(f"sgf{1 - u}"), before)
                    pe.wait_ge(S("wpg"), 16)
                    for m in range(2):
                        for k in range(KD):
                            mm = nc.tensor.matmul(bank(4 + m), xfT[u][:, k, :], wpg[:, k, m * 512:(m + 1) * 512], start=(k == 0), stop=(k == KD - 1))
                    mm.then_inc(S(f"gate_ps{u}"), 1)
                    pe.wait_ge(S(f"pfT{u}"), n + 1)
                    if before is not None:
                        pe.wait_ge(S(f"pg{1 - u}"), before)
                    pe.wait_ge(S("wpp"), 16)
                    for m in range(2):
                        for k in range(KE):
                            mm = nc.tensor.matmul(bank(6 + m), pfT[u][:, k, :], wpp[:, k, m * 512:(m + 1) * 512], start=(k == 0), stop=(k == KE - 1))
                    mm.then_inc(S(f"pp_ps{u}"), 1)

                turn(0, 0, None)
                with pe.Fori(0, 4) as n:
                    turn(n, 1, n + 1)
                    products(n, 0, n)
                    turn(n + 1, 0, n + 1)
                    products(n, 1, n + 1)
                products(4, 0, 4)


_INS = ["x_prompt", "x_sample", "p_prompt", "p_sample", "cache_k", "cache_v", "state_conv", "state_S", "rel_bias",
        "norm_mix", "w_in", "att_sink", "conv_w", "dn_A_log", "dn_dt_bias", "dn_norm", "w_out", "norm_ffn",
        "w_router_group", "w_router_expert", "w_gate", "w_up", "w_down", "w_ple_proj", "w_ple_gate", "norm_ple",
        "norm_final"]
_OUTS = [("y_prompt", (1, SEQ, D)), ("y_sample", (DEC, 1, D)),
         ("cache_k_prompt", (1, 1, P, 2, HD)), ("cache_v_prompt", (1, 1, P, 2, HD)),
         ("state_conv_prompt", (1, 1, CW - 1, CCH)), ("state_S_prompt", (1, 1, NH, HD, HD)),
         ("cache_k_sample", (1, DEC, P, 2, HD)), ("cache_v_sample", (1, DEC, P, 2, HD)),
         ("state_conv_sample", (1, DEC, CW - 1, CCH)), ("state_S_sample", (1, DEC, NH, HD, HD))]


def kernel(**inputs):
    import concourse.bacc as _bacc
    from concourse.bass_utils import run_bass_kernel_spmd as _run

    nc = _bacc.Bacc("TRN2", target_bir_lowering=False, num_devices=1)
    arrays = {f"in_{name}": np.ascontiguousarray(inputs[name]) for name in _INS}
    arrays["in_cst"] = constants()
    ins = {name[3:]: nc.dram_tensor(name, a.shape, F32, kind="ExternalInput").ap() for name, a in arrays.items()}
    outs = {name: nc.dram_tensor(f"out_{name}", shape, F32, kind="ExternalOutput").ap() for name, shape in _OUTS}
    program(nc, ins, outs)
    r = _run(nc, [arrays], core_ids=[0])
    return tuple(r.results[0][f"out_{name}"] for name, _ in _OUTS)
```

```python
from contextlib import ExitStack

import numpy as np

import concourse.bass as bass
from concourse import mybir

F32 = mybir.dt.float32
I32 = mybir.dt.int32
ALU = mybir.AluOpType
ACT = mybir.ActivationFunctionType
AX = mybir.AxisListType

P = 128
D = 1024
KD = D // P
SEQ = 1024
NT = SEQ // P
DEC = 8
TOK = SEQ + DEC
AH, HD, GQA = 8, 64, 4
NH = 8
CW = 4
CCH = 3 * NH * HD
FT_DN = CCH // P
A_Q, A_K, A_V, D_Q, D_B = 0, 512, 640, 768, 2304
IN_W = 2832
NG, EPG, NE, DE = 4, 8, 32, 256
PLE = 256
KE = DE // P
EPS = 1e-6
BIG = 1.0e30
XB = (2 * TOK - 1) // P
MAXB = NE + XB
DUMP = 1 << 20

C_ID, C_U, C_NEG, C_LV, C_HOT, C_HOTD, C_US, C_SWAP = 0, 128, 256, 384, 1280, 1664, 1792, 1920
C_TOK, C_GP, C_EP, C_EI, C_E128, C_THR, C_OV, C_FLAG, C_VAL, C_TT, C_END = \
    2048, 2049, 2053, 2061, 2093, 2125, 2133, 2149, 2157, 2166, 2175


def constants():
    c = np.zeros((P, C_END), np.float32)
    i = np.arange(P)
    row, col = i[:, None], i[None, :]
    c[:, C_ID:C_ID + P] = row == col
    c[:, C_U:C_U + P] = row <= col
    c[:, C_NEG:C_NEG + P] = np.where(col >= row, 0.0, -BIG)
    for n in range(7):
        s = 1 << n
        c[:, C_LV + n * P:C_LV + (n + 1) * P] = (row // (2 * s) == col // (2 * s)) & (row // s < col // s)
    c[:, C_US:C_US + P] = row < col
    c[:, C_SWAP:C_SWAP + P] = row == (col + 64) % P

    def bucket(d):
        d = np.maximum(d, 0)
        ratio = np.log(np.maximum(d, 1).astype(np.float32) / 16) / np.log(8.0)
        return np.where(d < 16, d, np.minimum(16 + (ratio * 16).astype(np.int32), 31))

    m = np.arange(3 * P)
    dist = 2 * P - 1 - m
    b = np.where((dist >= 0) & (dist < P), bucket(dist), 32)
    c[b, C_HOT + m] = 1.0
    dist = np.where(i == 0, 0, P - i)
    c[bucket(dist), C_HOTD + i] = 1.0
    c[:, C_TOK] = i
    c[:, C_GP:C_GP + NG] = NG - np.arange(NG)
    c[:, C_EP:C_EP + EPG] = EPG - np.arange(EPG)
    c[:, C_EI:C_EI + NE] = np.arange(NE)
    c[:, C_E128:C_E128 + NE] = np.arange(NE) * P
    c[:, C_THR:C_THR + 8] = (np.arange(8) + 1) * P
    c[:, C_OV:C_OV + XB] = np.arange(XB)
    c[:, C_FLAG] = -BIG
    c[:, C_VAL:C_VAL + NT] = 1.0
    c[:DEC, C_VAL + NT] = 1.0
    c[:, C_TT:C_TT + NT + 1] = i[:, None] + P * np.arange(NT + 1)
    return c


class Layout:

    def __init__(self, tensor):
        self.tensor, self.at = tensor, 0

    def take(self, *shape):
        n = 1
        for s in shape:
            n *= s
        view = self.tensor[:, self.at:self.at + n]
        self.at += n
        assert self.at <= self.tensor.shape[1], self.at
        if len(shape) == 2:
            return view.rearrange("p (a b) -> p a b", b=shape[1])
        if len(shape) == 3:
            return view.rearrange("p (a b c) -> p a b c", b=shape[1], c=shape[2])
        return view


def bc(ap, n):
    return ap.unsqueeze(2).to_broadcast([ap.shape[0], ap.shape[1], n])


def bm(ap, n):
    return ap.unsqueeze(1).to_broadcast([ap.shape[0], n, ap.shape[1]])


def even_odd(x):
    return x.rearrange("p (a f) -> p a f", a=2)


def program(nc, I, O, dbg=None):
    es = ExitStack()
    sems, lasting, stages = {}, {}, []

    def S(name):
        if name not in sems:
            sems[name] = nc.alloc_semaphore(name=f"{name}_{len(stages)}")
        return sems[name]

    def L(name):
        if name not in lasting:
            lasting[name] = nc.alloc_semaphore(name=name)
        return lasting[name]

    def stage_ends():
        nc.clear_and_free_semaphores(list(sems.values()))
        sems.clear()
        stages.append(None)
        nc.all_engine_barrier()

    def settle(eng):
        eng.sem_inc(S(f"settled_{eng.engine}".replace(".", "_")), 1)

    def dram(name, *shape, dt=F32):
        return nc.dram_tensor(name, shape, dt).ap()

    with es:
        mem = Layout(es.enter_context(nc.sbuf_tensor("mem", [P, 50400], F32)))
        psum = es.enter_context(nc.psum_tensor("psum", [P, 8, 512], F32))

        y_d = dram("conv_out_d", P, FT_DN, SEQ)
        ydec_d = dram("conv_dec_d", 3, DEC, NH * HD)
        sz_d = dram("gate_d", TOK, NH * HD)
        h_d = dram("h_d", TOK, D)
        xs_d = dram("xs_d", TOK, D)
        ye_d = dram("ye_d", 2 * TOK, D)
        tab_d = dram("tab_d", MAXB * P, 4, dt=I32)
        bias_d = dram("bias_d", AH, P, 3 * P)
        gbd_d = dram("gbd_d", 2, DEC, NH)
        od_d = dram("od_d", DEC, NH * HD)

        cst = mem.take(C_END)
        ident = cst[:, C_ID:C_ID + P]
        small = mem.take(1024)
        at = [0]

        def col(n):
            at[0] += n
            assert at[0] <= 1024
            return small[:, at[0] - n:at[0]]

        g_mix, g_ffn, g_ple = col(KD), col(KD), col(KD)
        half = col(1)
        normB, sinkB, sinkC, lg_pad = col(HD), col(AH), col(1), col(1)
        ones = mem.take(P)
        lg = mem.take(NT + 1, NG + NE)
        tabI = mem.take(4, MAXB).bitcast(I32)
        blk = mem.take(XB + 1).bitcast(I32)
        after_mix = mem.at
        gb = mem.take(NT + 1, 16)
        qf = mem.take(4, TOK)
        kf = mem.take(P + TOK)
        ksw = mem.take(P + TOK)
        vt = mem.take(NT + 2, P)
        mixD = mem.take(KD, DEC)
        stay = mem.at

        def bank(i, n=1):
            return psum[:, i, :] if n == 1 else psum[:, i:i + n, :]

        TB = TOK // 3

        def thirds(u):
            return psum[:, 3 * u:3 * u + 3, 0:TB]

        def flat(i, n):
            return psum[:, i:i + n, :].rearrange("p a b -> p (a b)")

        hnT = mem.take(KD, TOK)
        xin, xs, xT = mem.take(2, D), mem.take(2, D), mem.take(2, KD, P)
        wtok = mem.take(KD, 144 + 512)
        wf = mem.take(2, KD, P)
        XP = CW - 1 + SEQ + DEC * CW
        xp = mem.take(2, XP + 1)
        yc = mem.take(2, XP + 1)
        ys = mem.take(2, XP + 1)
        tails = mem.take(FT_DN, 27)
        stT = mem.take(FT_DN, 24)
        cwT = mem.take(FT_DN, CW)
        strow = mem.take(CCH)
        cwrow = mem.take(P)
        szt = mem.take(2, 512)
        ydT = mem.take(FT_DN, DEC)
        ydrow = mem.take(CCH)
        dtN, alN, dtB, alB = (col(NH) for _ in range(4))
        small_a, small_b, small_c = (col((NT + 1) * NH) for _ in range(3))
        rr = [(col(1), col(1), col(1)) for _ in range(2)]
        w_in = I["w_in"][0].rearrange("(p k) n -> p k n", k=KD)
        NV = XP - CW + 1

        with nc.Block() as block:
            @block.sync
            def _(sp):
                sp.dma_start(cst, I["cst"]).then_inc(S("cst"), 16)
                for v, name in ((g_mix, "norm_mix"), (g_ffn, "norm_ffn"), (g_ple, "norm_ple")):
                    sp.dma_start(v, I[name][0].rearrange("(p k) -> p k", k=KD)).then_inc(S("gains"), 16)
                sp.dma_start(dtN, I["dn_dt_bias"][0].partition_broadcast(P)).then_inc(S("gains"), 16)
                sp.dma_start(alN, I["dn_A_log"][0].partition_broadcast(P)).then_inc(S("gains"), 16)
                sp.dma_start(normB, I["dn_norm"][0].partition_broadcast(P)).then_inc(S("gains"), 16)

                def load_x(n, u, t):
                    sp.wait_ge(S(f"xs{u}"), n)
                    if t is None:
                        sp.dma_start(xin[0:DEC, u, :], I["x_sample"][:, 0, :]).then_inc(S(f"x{u}"), 16)
                    else:
                        sp.dma_start(xin[:, u, :], I["x_prompt"][0, bass.ds(t * P, P), :]).then_inc(S(f"x{u}"), 16)

                load_x(0, 0, 0)
                load_x(0, 1, 1)
                sp.dma_start(wtok[:, :, 0:P], w_in[:, :, A_V:A_V + P]).then_inc(S("wtok"), 16)
                sp.dma_start(wtok[:, :, P:], w_in[:, :, D_B:IN_W]).then_inc(S("wtok"), 16)
                sp.dma_start(strow[0:24, :], I["state_conv"][0].rearrange("b j c -> (b j) c")).then_inc(S("small"), 16)
                sp.dma_start(cwrow[0:48, :], I["conv_w"][0].rearrange("j (f c) -> (j f) c", c=P)).then_inc(S("small"), 16)
                with sp.Fori(1, 4) as n:
                    for u in range(2):
                        load_x(n, u, 2 * n + u)
                load_x(4, 0, None)

                def load_w(n, u, c0):
                    sp.wait_ge(S(f"f_psum{u}"), n)
                    sp.dma_start(wf[:, u], w_in[:, :, bass.ds(c0, P)]).then_inc(S(f"wf{u}"), 16)

                with sp.Fori(0, FT_DN // 2) as n:
                    for u in range(2):
                        load_w(n, u, D_Q + (2 * n + u) * P)
                for a in range(5):
                    load_w(6 + a // 2, a % 2, a * P)

                sp.wait_ge(S("tok_out0"), 5)
                sp.wait_ge(S("tok_out1"), 4)
                sp.dma_start(O["cache_v_prompt"][0, 0].rearrange("t h d -> t (h d)"), vt[:, NT, :]).then_inc(S("o1"), 16)
                sp.dma_start(O["cache_v_sample"][0, :, P - 1].rearrange("b h d -> b (h d)"), vt[0:DEC, NT + 1, :]).then_inc(S("o1"), 16)
                for new, old in (("cache_k_sample", "cache_k"), ("cache_v_sample", "cache_v")):
                    sp.dma_start(O[new][0, :, 0:P - 1].rearrange("b t h d -> b t (h d)"),
                                 I[old][0, :, 1:P].rearrange("b t h d -> b t (h d)")).then_inc(S("o1"), 16)
                sp.wait_ge(S("tails_row"), 1)
                sp.dma_start(O["state_conv_prompt"][0, 0], strow[0:3, :]).then_inc(S("o1"), 16)
                sp.dma_start(O["state_conv_sample"][0].rearrange("b j c -> (b j) c"), strow[3:27, :]).then_inc(S("o1"), 16)
                sp.wait_ge(S("ydrow"), 1)
                sp.dma_start(ydec_d.rearrange("i b c -> b i c"), ydrow[0:DEC, :].rearrange("b (i c) -> b i c", i=3)).then_inc(S("o1"), 16)
                sp.wait_ge(S("krow"), 1)
                sp.dma_start(O["cache_k_prompt"][0, 0].rearrange("t h d -> t (h d)"), cwrow).then_inc(S("o1"), 16)
                sp.wait_ge(S("krow"), 2)
                sp.dma_start(O["cache_k_sample"][0, :, P - 1].rearrange("b h d -> b (h d)"), yc[0:DEC, 0, 0:P]).then_inc(S("o1"), 16)
                sp.wait_ge(S("o1"), 16 * 9)

            @block.gpsimd
            def _(g):
                g.memset(half, -0.5).then_inc(S("half"), 1)
                g.memset(ones, 1.0).then_inc(S("ones"), 1)
                g.memset(kf[:, 0:P], 0.0).then_inc(S("zeros"), 1)
                g.memset(ksw[:, 0:P], 0.0).then_inc(S("zeros"), 1)
                g.memset(vt[:, 0, :], 0.0).then_inc(S("zeros"), 1)
                g.memset(vt[:, NT + 1, :], 0.0).then_inc(S("zeros"), 1)
                g.memset(gb[:, NT, :], 0.0).then_inc(S("zeros"), 1)
                g.memset(lg[:, NT, :], 0.0).then_inc(S("zeros"), 1)
                g.memset(xp[:, :, 0:CW - 1], 0.0).then_inc(S("zeros"), 1)
                g.wait_ge(S("half"), 1)

                def rstd(n, u):
                    g.wait_ge(S(f"var{u}"), n + 1)
                    g.tensor_tensor(rr[u][2], rr[u][1], half, ALU.pow).then_inc(S(f"rstd{u}"), 1)

                with g.Fori(0, 4) as n:
                    for u in range(2):
                        rstd(n, u)
                rstd(4, 0)

            @block.vector
            def _(v):
                def scale(n, u):
                    v.wait_ge(S(f"ss{u}"), n + 1)
                    nc.vector.tensor_scalar(rr[u][1], rr[u][0], 1.0 / D, EPS, ALU.mult, ALU.add).then_inc(S(f"var{u}"), 1)
                    v.wait_ge(S(f"rstd{u}"), n + 1)
                    nc.vector.tensor_scalar(xs[:, u, :], xin[:, u, :], rr[u][2], None, ALU.mult).then_inc(S(f"xs{u}"), 1)

                def gain(n, u):
                    v.wait_ge(S(f"xT_psum{u}"), n + 1)
                    v.wait_ge(S(f"tok_psum{u}"), n)
                    v.wait_ge(S(f"hnT{u}"), n)
                    nc.vector.tensor_tensor(xT[:, u], flat(2 * u, 2).rearrange("p (k c) -> p k c", c=P),
                                            bc(g_mix, P), ALU.mult).then_inc(S(f"xT{u}"), 1)

                v.wait_ge(S("gains"), 96)
                nc.vector.tensor_copy(even_odd(dtB), dtN.rearrange("p (f a) -> p a f", a=2)).then_inc(S("dtB"), 1)
                scale(0, 0)
                with v.Fori(0, 4) as n:
                    scale(n, 1)
                    gain(n, 0)
                    scale(n + 1, 0)
                    gain(n, 1)
                gain(4, 0)

                v.wait_ge(S("st_psum"), 1)
                nc.vector.tensor_copy(stT, bank(6)[:, 0:24 * FT_DN].rearrange("p (f c) -> p f c", c=24)).then_inc(S("stT"), 1)
                nc.vector.tensor_copy(cwT, bank(7)[:, 0:48].rearrange("p (j f) -> p f j", f=FT_DN)).then_inc(S("stT"), 1)
                v.wait_ge(S("stT"), 2)

                def conv(n, u, ft):
                    dec = xp[:, u, CW - 1 + SEQ:XP].rearrange("p (b j) -> p b j", j=CW)
                    v.wait_ge(S(f"tails{u}"), n)
                    nc.vector.tensor_copy(dec[:, :, 0:CW - 1], stT[:, ft, :].rearrange("p (b j) -> p b j", j=CW - 1)).then_inc(S(f"xp_dec{u}"), 1)
                    v.wait_ge(S(f"xp_dec{u}"), n + 1)
                    v.wait_ge(S(f"xp{u}"), n + 1)
                    v.wait_ge(S(f"silu{u}"), n)
                    nc.vector.tensor_scalar(yc[:, u, 0:NV], xp[:, u, 0:NV], cwT[:, ft, 0:1], None,
                                            ALU.mult).then_inc(S(f"conv{u}"), 1)
                    for j in range(1, CW):
                        v.wait_ge(S(f"conv{u}"), CW * n + j)
                        nc.vector.scalar_tensor_tensor(yc[:, u, 0:NV], xp[:, u, j:j + NV], cwT[:, ft, j:j + 1],
                                                       yc[:, u, 0:NV], ALU.mult, ALU.add).then_inc(S(f"conv{u}"), 1)
                    nc.vector.tensor_copy(tails[:, ft, 0:3], xp[:, u, SEQ:SEQ + 3])
                    nc.vector.tensor_copy(tails[:, ft, 3:27].rearrange("p (b j) -> p b j", j=3),
                                          dec[:, :, 1:CW]).then_inc(S(f"tails{u}"), 1)

                v.wait_ge(S("zeros"), 7)
                with v.Fori(0, FT_DN // 2) as n:
                    for u in range(2):
                        conv(n, u, 2 * n + u)
                v.wait_ge(S("tails_psum"), 1)
                nc.vector.tensor_copy(strow[0:27, :], flat(3, 3)[0:27, :]).then_inc(S("tails_row"), 1)
                v.wait_ge(S("yd_psum"), 1)
                nc.vector.tensor_copy(ydrow[0:DEC, :], flat(3, 3)[0:DEC, :]).then_inc(S("ydrow"), 1)
                v.wait_ge(S("ksw_psum"), 1)
                nc.vector.tensor_copy(ksw[:, P:].rearrange("p (b c) -> p b c", c=TB), thirds(0)).then_inc(S("ksw"), 1)
                v.wait_ge(S("krow_psum"), 1)
                nc.vector.tensor_copy(cwrow, bank(6)[:, 0:P]).then_inc(S("krow"), 1)
                nc.vector.tensor_copy(yc[0:DEC, 0, 0:P], bank(6)[0:DEC, P:2 * P]).then_inc(S("krow"), 1)

                v.wait_ge(S("sig"), 1)
                nc.vector.tensor_scalar(small_a, small_a, 1.0, None, ALU.add).then_inc(S("gbc"), 1)
                v.wait_ge(S("gbc"), 1)
                nc.vector.reciprocal(gb[:, :, 0:NH], small_a.rearrange("p (t h) -> p t h", h=NH)).then_inc(S("gbc"), 1)
                da = gb[:, :, NH:2 * NH]
                v.wait_ge(S("dtB"), 1)
                nc.vector.tensor_tensor(da, da, bm(dtB, NT + 1), ALU.add).then_inc(S("gbc"), 1)
                v.wait_ge(S("gbc"), 3)
                nc.vector.tensor_scalar(small_b.rearrange("p (t h) -> p t h", h=NH), da, 0.0, None, ALU.max).then_inc(S("gbc"), 1)
                v.wait_ge(S("gbc"), 4)
                nc.vector.scalar_tensor_tensor(small_c.rearrange("p (t h) -> p t h", h=NH), small_b.rearrange("p (t h) -> p t h", h=NH), -2.0, da,
                                               ALU.mult, ALU.add).then_inc(S("negabs"), 1)
                v.wait_ge(S("sp"), 1)
                nc.vector.tensor_tensor(small_b, small_b, small_c, ALU.add).then_inc(S("gbc"), 1)
                v.wait_ge(S("gbc"), 5)
                nc.vector.scalar_tensor_tensor(da, small_b.rearrange("p (t h) -> p t h", h=NH), -1.0, bm(alB, NT + 1),
                                               ALU.mult, ALU.mult).then_inc(S("gbc"), 1)

            @block.scalar
            def _(act):
                def square(n, u):
                    act.wait_ge(S(f"x{u}"), 16 * n + 16)
                    act.wait_ge(S(f"xT_psum{u}"), n)
                    nc.scalar.activation(xs[:, u, :], xin[:, u, :], ACT.Square, accum_out=rr[u][0]).then_inc(S(f"ss{u}"), 1)

                def keep_hnT(n, u, cols, m):
                    act.wait_ge(S(f"xT{u}"), n + 1)
                    nc.scalar.activation(hnT[:, :, cols], xT[:, u, :, 0:m], ACT.Copy).then_inc(S(f"hnT{u}"), 1)

                def keep_tok(n, u, t, R):
                    act.wait_ge(S(f"tok_psum{u}"), n + 1)
                    act.wait_ge(S(f"sz_out{u}"), 16 * n)
                    nc.scalar.activation(vt[0:R, t + 1, :], bank(4 + 2 * u)[0:R, 0:P], ACT.Copy)
                    nc.scalar.activation(gb[0:R, t, :].rearrange("p (i a f) -> p i a f", i=2, a=2),
                                         bank(4 + 2 * u)[0:R, P:P + 16].rearrange("p (i f a) -> p i a f", i=2, a=2), ACT.Copy)
                    nc.scalar.activation(szt[0:R, u, :], bank(5 + 2 * u)[0:R, :], ACT.Silu).then_inc(S(f"tok_out{u}"), 1)
                    act.wait_ge(S(f"tok_out{u}"), n + 1)
                    dst = sz_d[SEQ:TOK, :] if R == DEC else sz_d[bass.ds(t * P, P), :]
                    act.dma_start(dst, szt[0:R, u, :]).then_inc(S(f"sz_out{u}"), 16)

                act.wait_ge(S("zeros"), 7)
                square(0, 0)
                square(0, 1)

                def pair(n, last=False):
                    keep_hnT(n, 0, bass.ds(2 * n * P, P), P)
                    square(n + 1, 0)
                    keep_hnT(n, 1, bass.ds((2 * n + 1) * P, P), P)
                    keep_tok(n, 0, 2 * n, P)
                    if not last:
                        square(n + 1, 1)
                    keep_tok(n, 1, 2 * n + 1, P)

                with act.Fori(0, 3) as n:
                    pair(n)
                pair(3, last=True)
                keep_hnT(4, 0, slice(SEQ, TOK), DEC)
                keep_tok(4, 0, NT, DEC)

                def conv_in(n, u):
                    act.wait_ge(S(f"f_psum{u}"), n + 1)
                    act.wait_ge(S(f"tails{u}"), n)
                    nc.scalar.activation(xp[:, u, CW - 1:CW - 1 + 2 * TB].rearrange("p (b c) -> p b c", c=TB), thirds(u)[:, 0:2], ACT.Copy)
                    nc.scalar.activation(xp[:, u, CW - 1 + 2 * TB:CW - 1 + SEQ], thirds(u)[:, 2, 0:TB - DEC], ACT.Copy)
                    dec = xp[:, u, CW - 1 + SEQ:XP].rearrange("p (b j) -> p b j", j=CW)
                    nc.scalar.activation(dec[:, :, CW - 1], thirds(u)[:, 2, TB - DEC:TB], ACT.Copy).then_inc(S(f"xp{u}"), 1)

                def silu(n, u, ft):
                    act.wait_ge(S(f"conv{u}"), CW * n + CW)
                    act.wait_ge(S(f"y_out{u}"), 16 * n)
                    nc.scalar.activation(ys[:, u, 0:NV], yc[:, u, 0:NV], ACT.Silu).then_inc(S(f"silu{u}"), 1)
                    act.wait_ge(S(f"silu{u}"), n + 1)
                    act.dma_start(y_d[:, ft, :], ys[:, u, 0:SEQ]).then_inc(S(f"y_out{u}"), 16)
                    nc.scalar.activation(ydT[:, ft, :],
                                         ys[:, u, CW - 1 + SEQ:CW - 1 + SEQ + DEC * CW].rearrange("p (b j) -> p b j", j=CW)[:, :, 0],
                                         ACT.Copy).then_inc(S("ydT"), 1)

                with act.Fori(0, FT_DN // 2) as n:
                    conv_in(n, 0)
                    conv_in(n, 1)
                    silu(n, 0, 2 * n)
                    silu(n, 1, 2 * n + 1)
                for a in range(5):
                    n, u = 6 + a // 2, a % 2
                    act.wait_ge(S(f"f_psum{u}"), n + 1)
                    dst = qf[:, a, :] if a < 4 else kf[:, P:]
                    nc.scalar.activation(dst.rearrange("p (b c) -> p b c", c=TB), thirds(u), ACT.Copy).then_inc(S(f"att_out{u}"), 1)
                nc.scalar.activation(small_a.rearrange("p (t h) -> p t h", h=NH), gb[:, :, 0:NH], ACT.Exp, scale=-1.0).then_inc(S("sig"), 1)
                act.wait_ge(S("gains"), 96)
                nc.scalar.activation(even_odd(alB), alN.rearrange("p (f a) -> p a f", a=2), ACT.Exp)
                act.wait_ge(S("negabs"), 1)
                nc.scalar.activation(small_c, small_c, ACT.Exp).then_inc(S("spc"), 1)
                act.wait_ge(S("spc"), 1)
                nc.scalar.activation(small_c, small_c, ACT.Ln, bias=1.0).then_inc(S("sp"), 1)
                act.wait_ge(S("sz_out0"), 80)
                act.wait_ge(S("sz_out1"), 64)
                act.wait_ge(S("y_out0"), 96)
                act.wait_ge(S("y_out1"), 96)

            @block.tensor
            def _(pe):
                def turn(n, u):
                    pe.wait_ge(S(f"xs{u}"), n + 1)
                    pe.wait_ge(S(f"xT{u}"), n)
                    for k in range(KD):
                        mm = nc.tensor.transpose(flat(2 * u, 2)[:, k * P:(k + 1) * P],
                                                 xs[:, u, :].rearrange("p (c k) -> p k c", k=KD)[:, k, :], ident)
                    mm.then_inc(S(f"xT_psum{u}"), 1)

                def project(n, u):
                    pe.wait_ge(S(f"xT{u}"), n + 1)
                    pe.wait_ge(S(f"tok_out{u}"), n)
                    for k in range(KD):
                        nc.tensor.matmul(bank(4 + 2 * u)[:, 0:144], xT[:, u, k, :], wtok[:, k, 0:144], start=(k == 0), stop=(k == KD - 1))
                    for k in range(KD):
                        mm = nc.tensor.matmul(bank(5 + 2 * u), xT[:, u, k, :], wtok[:, k, 144:], start=(k == 0), stop=(k == KD - 1))
                    mm.then_inc(S(f"tok_psum{u}"), 1)

                pe.wait_ge(S("cst"), 16)
                turn(0, 0)
                pe.wait_ge(S("wtok"), 32)
                with pe.Fori(0, 4) as n:
                    turn(n, 1)
                    project(n, 0)
                    turn(n + 1, 0)
                    project(n, 1)
                project(4, 0)
                pe.wait_ge(S("small"), 32)
                pe.wait_ge(S("tok_out1"), 4)
                for f in range(FT_DN):
                    nc.tensor.transpose(bank(6)[:, 24 * f:24 * f + 24], strow[0:24, f * P:(f + 1) * P], ident[0:24, 0:24])
                nc.tensor.transpose(bank(7)[:, 0:48], cwrow[0:48, :], ident[0:48, 0:48]).then_inc(S("st_psum"), 1)
                pe.wait_ge(S("hnT0"), 5)
                pe.wait_ge(S("hnT1"), 4)
                pe.wait_ge(S("tok_out0"), 5)

                def features(n, u, att=False):
                    pe.wait_ge(S(f"wf{u}"), 16 * n + 16)
                    if not att or n == 6:
                        pe.wait_ge(S(f"xp{u}"), n if not att else 6)
                    else:
                        pe.wait_ge(S(f"att_out{u}"), n - 6)
                    for b in range(3):
                        for k in range(KD):
                            mm = nc.tensor.matmul(thirds(u)[:, b], wf[:, u, k, :], hnT[:, k, b * TB:(b + 1) * TB],
                                                  start=(k == 0), stop=(k == KD - 1))
                    mm.then_inc(S(f"f_psum{u}"), 1)

                with pe.Fori(0, FT_DN // 2) as n:
                    for u in range(2):
                        features(n, u)
                for a in range(5):
                    features(6 + a // 2, a % 2, True)
                pe.wait_ge(S("att_out1"), 2)
                pe.wait_ge(S("tails0"), 6)
                pe.wait_ge(S("tails1"), 6)
                for f in range(FT_DN):
                    mm = nc.tensor.transpose(flat(3, 3)[0:27, f * P:(f + 1) * P], tails[:, f, :], ident)
                mm.then_inc(S("tails_psum"), 1)
                pe.wait_ge(S("tails_row"), 1)
                pe.wait_ge(S("ydT"), FT_DN)
                for f in range(FT_DN):
                    mm = nc.tensor.transpose(flat(3, 3)[0:DEC, f * P:(f + 1) * P], ydT[:, f, :], ident)
                mm.then_inc(S("yd_psum"), 1)
                pe.wait_ge(S("att_out0"), 3)
                swap = cst[:, C_SWAP:C_SWAP + P]
                for b in range(3):
                    mm = nc.tensor.matmul(thirds(0)[:, b], swap, kf[:, P + b * TB:P + (b + 1) * TB], start=True, stop=True)
                mm.then_inc(S("ksw_psum"), 1)
                pe.wait_ge(S("stT"), 2)
                nc.tensor.transpose(bank(6)[:, 0:P], kf[:, SEQ:SEQ + P], ident)
                nc.tensor.transpose(bank(6)[0:DEC, P:2 * P], kf[:, P + SEQ:P + TOK], ident).then_inc(S("krow_psum"), 1)

        stage_ends()
        mem.at = stay
        biasS = mem.take(AH, 2 * P)
        mixer = mem.at
        kc, vc, kcT = mem.take(DEC, P), mem.take(DEC, P), mem.take(DEC, P)
        sinkN = mem.take(AH)
        relb, relw = mem.take(AH), mem.take(AH, P)
        toep = mem.take(2, 3 * P)
        qblk = mem.take(DEC, AH)
        biasD = mem.take(P)
        sD, pTD = mem.take(DEC, P), mem.take(DEC, AH)
        oD = mem.take(DEC, AH)
        mD, eD, dD, rD = (mem.take(DEC) for _ in range(4))
        odr = mem.take(NH * HD)
        S0, prod, prodq = (mem.take(HD, HD) for _ in range(3))
        qkv = mem.take(3, HD)
        szd = mem.take(HD)
        sqd = mem.take(3, HD)
        kS, qS, vn1, o1, o2 = (mem.take(HD) for _ in range(5))
        bD, gD, egD, qkD, n1, m1, r1 = (mem.take(1) for _ in range(7))
        n2, m2, r2 = (mem.take(2) for _ in range(3))
        PR = DEC * NH

        with nc.Block() as block:
            @block.sync
            def _(sp):
                sp.dma_start(relb[0:32, :], I["rel_bias"]).then_inc(S("d_rel"), 16)
                for i in range(2):
                    for a in range(2):
                        sp.dma_start(gbd_d[i, :, a::2], gb[0:DEC, NT, NH * i + 4 * a:NH * i + 4 * a + 4], allow_slow_non_contiguous=True).then_inc(S("gbd"), 16)
                sp.dma_start(S0[0:PR], I["state_S"][0].rearrange("b h d e -> (b h) d e")).then_inc(S("S0"), 16)
                for i in range(3):
                    sp.dma_start(qkv[0:PR, i, :], ydec_d[i].rearrange("b (h d) -> (b h) d", d=HD)).then_inc(S("qkv"), 16)
                sp.dma_start(szd[0:PR], sz_d[SEQ:TOK].rearrange("b (h d) -> (b h) d", d=HD)).then_inc(S("qkv"), 16)
                sp.wait_ge(S("gbd"), 64)
                sp.dma_start(bD[0:PR], gbd_d[0].rearrange("b (h o) -> (b h) o", o=1)).then_inc(S("bg"), 16)
                sp.dma_start(gD[0:PR], gbd_d[1].rearrange("b (h o) -> (b h) o", o=1)).then_inc(S("bg"), 16)
                sp.dma_start(kc, I["cache_k"][0].rearrange("b t h d -> t b (h d)")).then_inc(S("kc"), 16)
                sp.dma_start(vc[1:P], I["cache_v"][0, :, 1:P].rearrange("b t h d -> t b (h d)")).then_inc(S("vc"), 16)
                sp.dma_start(vc[0:1], O["cache_v_sample"][0, :, P - 1].rearrange("b h d -> b (h d)").unsqueeze(0)).then_inc(S("vc"), 16)
                sp.dma_start(sinkN, I["att_sink"][0].partition_broadcast(P)).then_inc(S("sinks"), 16)
                sp.dma_start(sinkC[0:AH], I["att_sink"][0].unsqueeze(1)).then_inc(S("sinks"), 16)
                for h in range(AH):
                    sp.wait_ge(S("toep"), h + 1)
                    sp.dma_start(bias_d[h], toep[:, h % 2, :]).then_inc(S(f"toep_out{h % 2}"), 16)
                sp.wait_ge(S("toep_out0"), 64)
                sp.wait_ge(S("toep_out1"), 64)
                skew = bias_d.rearrange("h p m -> h (p m)")[:, P - 1:P - 1 + P * (3 * P - 1)].rearrange("h (p m) -> p h m", m=3 * P - 1)
                for g in range(2):
                    for a in range(2):
                        sp.dma_start(biasS[:, 4 * g + 2 * a:4 * g + 2 * a + 2], skew[:, 4 * g + a:4 * g + a + 3:2, 0:2 * P]).then_inc(S("biasS"), 16)
                sp.wait_ge(S("S1"), 1)
                sp.dma_start(O["state_S_sample"][0].rearrange("b h d e -> (b h) d e"), S0[0:PR]).then_inc(S("o2"), 16)
                sp.wait_ge(S("o_dn"), 1)
                sp.dma_start(od_d.rearrange("b (h d) -> (b h) d", d=HD), o2[0:PR]).then_inc(S("od"), 16)
                sp.wait_ge(S("od"), 16)
                sp.dma_start(odr[0:DEC, :], od_d).then_inc(S("odr"), 16)
                sp.wait_ge(S("biasS"), 64)
                sp.wait_ge(S("o2"), 16)
                sp.wait_ge(S("odr"), 16)
                sp.wait_ge(S("sinks"), 32)

            @block.gpsimd
            def _(g):
                g.memset(qblk, 0.0).then_inc(S("qblk0"), 1)
                g.wait_ge(S("n2"), 1)
                g.tensor_tensor(r2[0:PR], m2[0:PR], half[0:PR].to_broadcast([PR, 2]), ALU.pow).then_inc(S("r2"), 1)
                g.wait_ge(S("qk_n"), 1)
                g.wait_ge(S("S0"), 16)
                g.tensor_tensor(prodq[0:PR], S0[0:PR].rearrange("p d e -> p e d"), bm(qkv[0:PR, 0, :], HD), ALU.mult).then_inc(S("qS"), 1)
                g.wait_ge(S("n1"), 1)
                g.tensor_tensor(r1[0:PR], m1[0:PR], half[0:PR], ALU.pow).then_inc(S("r1"), 1)

            @block.scalar
            def _(act):
                act.wait_ge(S("bg"), 32)
                nc.scalar.activation(egD[0:PR], gD[0:PR], ACT.Exp).then_inc(S("egD"), 1)
                for h in range(AH):
                    act.wait_ge(S("toep_ps"), h + 1)
                    act.wait_ge(S(f"toep_out{h % 2}"), 16 * (h // 2))
                    nc.scalar.activation(toep[:, h % 2, :], bank(h % 2)[:, 0:3 * P], ACT.Copy).then_inc(S("toep"), 1)
                act.wait_ge(S("xD"), 1)
                nc.scalar.activation(sD[0:AH], sD[0:AH], ACT.Exp)
                nc.scalar.activation(eD[0:AH], eD[0:AH], ACT.Exp).then_inc(S("eD"), 1)

            @block.tensor
            def _(pe):
                pe.wait_ge(S("relw"), 1)
                for h in range(AH):
                    pe.wait_ge(S("toep"), h - 1) if h > 1 else None
                    nc.tensor.matmul(bank(h % 2)[:, 0:3 * P], relw[0:33, h, :], cst[0:33, C_HOT:C_HOT + 3 * P], start=True, stop=True).then_inc(S("toep_ps"), 1)
                nc.tensor.matmul(bank(4)[0:AH, 0:P], relb[0:33, :], cst[0:33, C_HOTD:C_HOTD + P], start=True, stop=True)
                nc.tensor.matmul(bank(4)[:, P:P + 4 * DEC], cst[:, C_SWAP:C_SWAP + P], qf[:, :, SEQ:TOK], start=True, stop=True)
                pe.wait_ge(S("kc"), 16)
                for b in range(DEC):
                    mm = nc.tensor.transpose(flat(2, 2)[:, b * P:(b + 1) * P], kc[:, b, :], ident)
                mm.then_inc(S("kcT_ps"), 1)
                pe.wait_ge(S("kcT"), 1)
                for b in range(DEC):
                    mm = nc.tensor.matmul(flat(5, 2)[0:AH, b * P:(b + 1) * P], qblk[:, b, :], kcT[:, b, :], start=True, stop=True)
                mm.then_inc(S("sD_ps"), 1)
                pe.wait_ge(S("pD"), 1)
                for b in range(DEC):
                    mm = nc.tensor.transpose(bank(7)[:, b * AH:(b + 1) * AH], sD[0:AH, b, :], ident[0:AH, 0:AH])
                mm.then_inc(S("pTD_ps"), 1)
                pe.wait_ge(S("pTD"), 1)
                pe.wait_ge(S("vc"), 32)
                for b in range(DEC):
                    mm = nc.tensor.matmul(bank(2)[:, b * AH:(b + 1) * AH], vc[:, b, :], pTD[:, b, :], start=True, stop=True)
                mm.then_inc(S("oD_ps"), 1)
                pe.wait_ge(S("oD"), 1)
                nc.tensor.matmul(bank(3)[:, 0:DEC * AH], cst[:, C_SWAP:C_SWAP + P], oD.rearrange("p b h -> p (b h)"), start=True, stop=True).then_inc(S("osw"), 1)
                pe.wait_ge(S("odr"), 16)
                for k in range(4):
                    mm = nc.tensor.transpose(bank(7)[:, k * DEC:(k + 1) * DEC], odr[0:DEC, k * P:(k + 1) * P], ident[0:DEC, 0:DEC])
                mm.then_inc(S("odT"), 1)

            @block.vector
            def _(v):
                tick = [0]

                def chain(ins):
                    tick[0] += 1
                    ins.then_inc(S("dve_decode"), 1)
                    v.wait_ge(S("dve_decode"), tick[0])

                chain(nc.vector.memset(relb[32:33, :], -BIG))
                v.wait_ge(S("d_rel"), 16)
                nc.vector.tensor_copy(relw[0:33], bc(relb[0:33], P)).then_inc(S("relw"), 1)
                v.wait_ge(S("qkv"), 64)
                v.wait_ge(S("bg"), 32)
                chain(nc.vector.tensor_tensor(sqd[0:PR, 0:2], qkv[0:PR, 0:2], qkv[0:PR, 0:2], ALU.mult))
                chain(nc.vector.tensor_reduce(n2[0:PR], sqd[0:PR, 0:2], AX.X, ALU.add))
                nc.vector.tensor_scalar(m2[0:PR, 0:1], n2[0:PR, 0:1], float(HD), HD * EPS, ALU.mult, ALU.add)
                nc.vector.tensor_scalar(m2[0:PR, 1:2], n2[0:PR, 1:2], 1.0, EPS, ALU.mult, ALU.add).then_inc(S("n2"), 1)
                v.wait_ge(S("r2"), 1)
                nc.vector.tensor_tensor(qkv[0:PR, 0:2], qkv[0:PR, 0:2], bc(r2[0:PR], HD), ALU.mult).then_inc(S("qk_n"), 1)
                v.wait_ge(S("qk_n"), 1)
                q_, k_, v_ = (qkv[0:PR, i, :] for i in range(3))
                v.wait_ge(S("S0"), 16)
                S0e = S0[0:PR].rearrange("p d e -> p e d")
                chain(nc.vector.tensor_tensor(prod[0:PR], S0e, bm(k_, HD), ALU.mult))
                chain(nc.vector.tensor_reduce(kS[0:PR], prod[0:PR], AX.X, ALU.add))
                v.wait_ge(S("qS"), 1)
                chain(nc.vector.tensor_reduce(qS[0:PR], prodq[0:PR], AX.X, ALU.add))
                chain(nc.vector.tensor_tensor(sqd[0:PR, 2], q_, k_, ALU.mult))
                chain(nc.vector.tensor_reduce(qkD[0:PR], sqd[0:PR, 2], AX.X, ALU.add))
                v.wait_ge(S("egD"), 1)
                chain(nc.vector.tensor_scalar(kS[0:PR], kS[0:PR], egD[0:PR], None, ALU.mult))
                chain(nc.vector.tensor_tensor(vn1[0:PR], v_, kS[0:PR], ALU.subtract))
                chain(nc.vector.tensor_scalar(vn1[0:PR], vn1[0:PR], bD[0:PR], None, ALU.mult))
                chain(nc.vector.tensor_scalar(o1[0:PR], qS[0:PR], egD[0:PR], None, ALU.mult))
                chain(nc.vector.scalar_tensor_tensor(o1[0:PR], vn1[0:PR], qkD[0:PR], o1[0:PR], ALU.mult, ALU.add))
                chain(nc.vector.tensor_tensor(prod[0:PR], bc(k_, HD), bm(vn1[0:PR], HD), ALU.mult))
                nc.vector.scalar_tensor_tensor(S0[0:PR], S0[0:PR], egD[0:PR], prod[0:PR], ALU.mult, ALU.add).then_inc(S("S1"), 1)
                chain(nc.vector.tensor_tensor(sqd[0:PR, 0], o1[0:PR], o1[0:PR], ALU.mult))
                chain(nc.vector.tensor_reduce(n1[0:PR], sqd[0:PR, 0], AX.X, ALU.add))
                nc.vector.tensor_scalar(m1[0:PR], n1[0:PR], 1.0 / HD, EPS, ALU.mult, ALU.add).then_inc(S("n1"), 1)
                v.wait_ge(S("r1"), 1)
                chain(nc.vector.scalar_tensor_tensor(o2[0:PR], o1[0:PR], r1[0:PR], normB[0:PR], ALU.mult, ALU.mult))
                nc.vector.tensor_tensor(o2[0:PR], o2[0:PR], szd[0:PR], ALU.mult).then_inc(S("o_dn"), 1)

                v.wait_ge(S("kcT_ps"), 1)
                v.wait_ge(S("qblk0"), 1)
                chain(nc.vector.tensor_copy(kcT, flat(2, 2).rearrange("p (b j) -> p b j", j=P)))
                nc.vector.tensor_copy(kcT[:, :, 0], kf[:, P + SEQ:])
                qsw = bank(4)[:, P:P + 4 * DEC].rearrange("p (i b) -> p i b", b=DEC)
                for h in range(AH):
                    lo = (h // GQA) * HD
                    src = qf[lo:lo + HD, h // 2, SEQ:TOK] if (h % 2) * HD == lo else qsw[lo:lo + HD, h // 2, :]
                    nc.vector.tensor_copy(qblk[lo:lo + HD, :, h], src)
                nc.vector.tensor_copy(biasD[0:AH], bank(4)[0:AH, 0:P]).then_inc(S("kcT"), 1)
                v.wait_ge(S("kcT"), 1)
                v.wait_ge(S("sD_ps"), 1)
                v.wait_ge(S("sinks"), 32)
                nc.vector.tensor_copy(sinkB.rearrange("p (g a f) -> p g a f", g=2, a=2), sinkN.rearrange("p (g f a) -> p g a f", g=2, a=2))
                sp_ = flat(5, 2)[0:AH].rearrange("p (b j) -> p b j", j=P)
                chain(nc.vector.scalar_tensor_tensor(sD[0:AH], sp_, HD ** -0.5, bm(biasD[0:AH], DEC), ALU.mult, ALU.add))
                chain(nc.vector.tensor_reduce(mD[0:AH], sD[0:AH], AX.X, ALU.max))
                chain(nc.vector.tensor_scalar(mD[0:AH], mD[0:AH], sinkC[0:AH], None, ALU.max))
                nc.vector.tensor_tensor(sD[0:AH], sD[0:AH], bc(mD[0:AH], P), ALU.subtract)
                nc.vector.tensor_scalar(eD[0:AH], mD[0:AH], sinkC[0:AH], -1.0, ALU.subtract, ALU.mult).then_inc(S("xD"), 1)

                v.wait_ge(S("eD"), 1)
                chain(nc.vector.tensor_reduce(dD[0:AH], sD[0:AH], AX.X, ALU.add))
                chain(nc.vector.tensor_tensor(dD[0:AH], dD[0:AH], eD[0:AH], ALU.add))
                chain(nc.vector.reciprocal(rD[0:AH], dD[0:AH]))
                nc.vector.tensor_tensor(sD[0:AH], sD[0:AH], bc(rD[0:AH], P), ALU.mult).then_inc(S("pD"), 1)
                v.wait_ge(S("pTD_ps"), 1)
                nc.vector.tensor_copy(pTD, bank(7)[:, 0:DEC * AH].rearrange("p (b h) -> p b h", h=AH)).then_inc(S("pTD"), 1)
                v.wait_ge(S("oD_ps"), 1)
                nc.vector.tensor_copy(oD, bank(2)[:, 0:DEC * AH].rearrange("p (b h) -> p b h", h=AH)).then_inc(S("oD"), 1)
                v.wait_ge(S("oD"), 1)
                v.wait_ge(S("osw"), 1)
                oS = bank(3)[:, 0:DEC * AH].rearrange("p (b h) -> p b h", h=AH)
                for h in range(AH):
                    lo = (h % 2) * HD
                    src = oD if (h // GQA) * HD == lo else oS
                    nc.vector.tensor_copy(mixD[lo:lo + HD, h // 2, :], src[lo:lo + HD, :, h])
                v.wait_ge(S("odT"), 1)
                nc.vector.tensor_copy(mixD[:, 4:8, :], bank(7)[:, 0:4 * DEC].rearrange("p (k b) -> p k b", b=DEC)).then_inc(S("mixD"), 1)

        stage_ends()
        mem.at = mixer
        qst, kst, kswst, vst = mem.take(4, P), mem.take(2 * P), mem.take(2 * P), mem.take(2 * P)
        yst = mem.take(FT_DN, P)
        szst = mem.take(NH * HD)
        sA = [mem.take(GQA, 2 * P) for _ in range(2)]
        pT = mem.take(2 * GQA, P)
        mix = mem.take(KD, P)
        qk = mem.take(KD, P)
        qkT = mem.take(KD, P)
        vtok = mem.take(NH, HD)
        E_ = mem.take(NH, P)
        gU = mem.take(NH, P)
        AT = mem.take(NH, P)
        QK = mem.take(NH, P)
        Lo = [mem.take(NH, P) for _ in range(2)]
        Xs = mem.take(NH, P)
        sq = Xs.rearrange("p h i -> p (h i)")
        MT = [mem.take(NH, P) for _ in range(2)]
        M_ = mem.take(NH, P)
        r_, vn, vn2, tmp, o_ = (mem.take(NH, HD) for _ in range(5))
        Sst = mem.take(4, HD)
        xres, hh_, xs2 = mem.take(D), mem.take(D), mem.take(D)
        xT2 = mem.take(KD, P)
        wout = mem.take(KD, D)
        wr = mem.take(KD, NG + NE)
        ss16, m16, r16 = mem.take(16), mem.take(16), mem.take(16)
        ss8, m8, r8, egam, kdec, eglS, gam8 = (mem.take(NH) for _ in range(7))
        mx, mm_, nm_, es_, den, rcp = ([mem.take(GQA) for _ in range(2)] for _ in range(6))
        ssx, msx, rsx = mem.take(1), mem.take(1), mem.take(1)
        LV = 7

        ORD = (0, 2, 1, 3)
        SLOT = (0, 2, 4, 6, 1, 3, 5, 7)

        kqS_ps = flat(4, 2).rearrange("p (a n f e) -> p a n f e", a=2, n=2, f=4)

        def slots(x):
            return x.rearrange("p (a f) d -> p a f d", a=2)

        def natural(x):
            return x.rearrange("p (f a d) -> p a f d", a=2, d=HD)

        def scores_ps(g):
            return flat(2 * g, 2).rearrange("p (h j) -> p h j", h=GQA)

        with nc.Block() as block:
            @block.sync
            def _(sp):
                sp.dma_start(wout, I["w_out"][0].rearrange("(k p) n -> p k n", p=P)).then_inc(S("wout"), 16)
                sp.dma_start(wr[:, :, 0:NG], I["w_router_group"][0].rearrange("(p k) n -> p k n", k=KD)).then_inc(S("wr"), 16)
                sp.dma_start(wr[:, :, NG:], I["w_router_expert"][0].rearrange("(p k) n -> p k n", k=KD)).then_inc(S("wr"), 16)

                def load_tile(t, xrows, first=False):
                    rows = t * P if first else sp.snap(t * P)
                    if not first:
                        sp.wait_ge(S("tokv_ps"), t)
                        settle(sp)
                    sp.dma_start(yst, y_d[:, :, bass.ds(rows, P)]).then_inc(S("y_in"), 16)
                    if not first:
                        sp.wait_ge(S("av_ps"), t)
                    sp.dma_start(qst, qf[:, :, bass.ds(rows, P)]).then_inc(S("att_in"), 16)
                    sp.dma_start(kst, kf[:, bass.ds(rows, 2 * P)]).then_inc(S("att_in"), 16)
                    sp.dma_start(kswst, ksw[:, bass.ds(rows, 2 * P)]).then_inc(S("att_in"), 16)
                    sp.dma_start(vst.rearrange("p (a b) -> p a b", b=P), vt[:, bass.ds(t, 2), :]).then_inc(S("att_in"), 16)
                    if not first:
                        sp.wait_ge(S("h"), t)
                    sp.dma_start(xres[0:xrows.shape[0]], xrows).then_inc(S("xres"), 16)
                    if not first:
                        sp.wait_ge(S("og"), t)
                    sp.dma_start(szst, sz_d[bass.ds(rows, P), :]).then_inc(S("sz_in"), 16)

                load_tile(0, I["x_sample"][:, 0, :], first=True)
                with sp.Fori(1, NT) as t:
                    load_tile(t, I["x_prompt"][0, bass.ds(sp.snap(t * P - P), P), :])
                sp.wait_ge(S("h"), NT)
                sp.dma_start(xres, I["x_prompt"][0, SEQ - P:SEQ, :]).then_inc(S("xres"), 16)
                sp.wait_ge(S("S"), NT + 1)
                for hp in range(2):
                    sp.dma_start(O["state_S_prompt"][0, 0, hp::2].rearrange("h d e -> d h e"), Sst[hp * HD:(hp + 1) * HD]).then_inc(S("o3"), 16)
                sp.wait_ge(S("o3"), 32)

            @block.gpsimd
            def _(g):
                g.memset(Sst, 0.0).then_inc(S("S"), 1)
                g.wait_ge(S("S"), 1)

                def rms_pow(name, out, in_, n, t):
                    g.wait_ge(S("m_" + name), t + 1)
                    g.tensor_tensor(out, in_, half[0:out.shape[0]].to_broadcast([out.shape[0], n]), ALU.pow).then_inc(S("r_" + name), 1)

                def tile(t, first=False):
                    if not first:
                        g.wait_ge(S("gam_ps"), t)
                    g.tensor_tensor(gU, bm(cst[:, C_U:C_U + P], NH), bc(gb[:, t, NH:2 * NH], P), ALU.mult).then_inc(S("gU"), 1)
                    if not first:
                        rms_pow("o", r8, m8, NH, t - 1)
                    rms_pow("qk", r16, m16, 16, t)
                    R = DEC if first else P
                    rms_pow("x", rsx[0:R], msx[0:R], 1, t)
                    for l in range(LV):
                        if l == 0:
                            g.wait_ge(S("AT"), t + 1)
                            g.wait_ge(S("X1_ps"), (LV - 1) * t)
                        elif l >= 3:
                            g.wait_ge(S("X1_ps"), (LV - 1) * t + l - 2)
                        elif l == 2:
                            g.wait_ge(S("MT1"), LV * t + 1)
                        g.tensor_tensor(Lo[l % 2], AT, bm(cst[:, C_LV + l * P:C_LV + (l + 1) * P], NH), ALU.mult).then_inc(S("Lo"), 1)

                tile(0, first=True)
                with g.Fori(1, NT) as t:
                    tile(t)
                rms_pow("o", r8, m8, NH, NT - 1)
                rms_pow("x", rsx, msx, 1, NT)

            @block.vector
            def _(v):
                V = nc.vector

                def residual(t, R):
                    v.wait_ge(S("proj_ps"), t + 1)
                    v.wait_ge(S("xres"), 16 * t + 16)
                    v.wait_ge(S("h_out"), 16 * t)
                    V.tensor_tensor(hh_[0:R], xres[0:R], flat(2, 2)[0:R], ALU.add).then_inc(S("h"), 1)

                def normed(t, R):
                    v.wait_ge(S("ssx"), t + 1)
                    V.tensor_scalar(msx[0:R], ssx[0:R], 1.0 / D, EPS, ALU.mult, ALU.add).then_inc(S("m_x"), 1)
                    v.wait_ge(S("r_x"), t + 1)
                    V.tensor_scalar(xs2[0:R], hh_[0:R], rsx[0:R], None, ALU.mult).then_inc(S("xs2"), 1)

                def gain(t, R):
                    v.wait_ge(S("xT2_ps"), t + 1)
                    V.tensor_tensor(xT2[:, :, 0:R], flat(0, 2).rearrange("p (k c) -> p k c", c=P)[:, :, 0:R], bc(g_ffn, R), ALU.mult).then_inc(S("xT2"), 1)

                def logits(t, R, dst):
                    v.wait_ge(S("lg_ps"), t + 1)
                    V.tensor_copy(dst, bank(3)[0:R, 0:NG + NE]).then_inc(S("lg"), 1)

                def gated(t):
                    v.wait_ge(S("osq"), t + 1)
                    V.tensor_reduce(ss8, tmp, AX.X, ALU.add).then_inc(S("v_ss8"), 1)
                    v.wait_ge(S("v_ss8"), t + 1)
                    V.tensor_scalar(m8, ss8, 1.0 / HD, EPS, ALU.mult, ALU.add).then_inc(S("m_o"), 1)
                    v.wait_ge(S("sz_in"), 16 * t + 16)
                    V.tensor_tensor(slots(r_), natural(szst), slots(bm(normB, NH)), ALU.mult).then_inc(S("v_sz"), 1)
                    v.wait_ge(S("r_o"), t + 1)
                    V.tensor_tensor(o_, o_, bc(r8, HD), ALU.mult).then_inc(S("v_on"), 1)
                    v.wait_ge(S("v_on"), t + 1)
                    V.tensor_tensor(natural(vn.rearrange("p h d -> p (h d)")), slots(o_), slots(r_), ALU.mult).then_inc(S("og"), 1)

                def tile(t, R, dst, first=False):
                    if not first:
                        gated(t - 1)
                    for g in range(2):
                        v.wait_ge(S(f"sc{g}"), t + 1)
                        V.scalar_tensor_tensor(sA[g], scores_ps(g), HD ** -0.5, biasS[:, GQA * g:GQA * g + GQA, :], ALU.mult, ALU.add).then_inc(S(f"s{g}"), 1)
                    for g in range(2):
                        v.wait_ge(S(f"s{g}"), t + 1)
                        V.tensor_scalar(sA[g][:, :, 0:P], sA[g][:, :, 0:P], cst[:, bass.ds(C_FLAG + t, 1)], None, ALU.add).then_inc(S(f"sf{g}"), 1)
                    v.wait_ge(S("gam_ps"), t + 1)
                    gB = flat(4, 2).rearrange("p (h i) -> p h i", i=P)
                    gL = gB[:, :, P - 1]
                    V.tensor_copy(gam8, bank(6)[:, 0:NH]).then_inc(S("v_gC"), 1)
                    v.wait_ge(S("v_gC"), t + 1)
                    V.tensor_tensor(E_, gB, bc(gam8, P), ALU.subtract).then_inc(S("v_D"), 1)
                    V.tensor_tensor(kdec, gL, gam8, ALU.subtract).then_inc(S("kd_in"), 1)
                    v.wait_ge(S("v_D"), t + 1)
                    V.tensor_tensor(E_, E_, bm(cst[:, C_NEG:C_NEG + P], NH), ALU.add).then_inc(S("D"), 1)
                    for g in range(2):
                        v.wait_ge(S(f"sf{g}"), t + 1)
                        V.tensor_reduce(mx[g], sA[g], AX.X, ALU.max).then_inc(S(f"v_mx{g}"), 1)
                        v.wait_ge(S(f"v_mx{g}"), t + 1)
                        V.tensor_tensor(mm_[g], mx[g], sinkB[:, GQA * g:GQA * g + GQA], ALU.max).then_inc(S(f"v_mm{g}"), 1)
                        v.wait_ge(S(f"v_mm{g}"), t + 1)
                        V.tensor_scalar(nm_[g], mm_[g], -1.0, None, ALU.mult)
                        V.tensor_tensor(es_[g], sinkB[:, GQA * g:GQA * g + GQA], mm_[g], ALU.subtract).then_inc(S(f"nm{g}"), 1)
                    v.wait_ge(S("sq"), t + 1)
                    V.tensor_reduce(ss16, sq.rearrange("p (h d) -> p h d", d=HD), AX.X, ALU.add).then_inc(S("v_ss"), 1)
                    v.wait_ge(S("v_ss"), t + 1)
                    V.tensor_scalar(m16[:, 0:NH], ss16[:, 0:NH], float(HD), HD * EPS, ALU.mult, ALU.add)
                    V.tensor_scalar(m16[:, NH:], ss16[:, NH:], 1.0, EPS, ALU.mult, ALU.add).then_inc(S("m_qk"), 1)
                    for g in range(2):
                        v.wait_ge(S(f"p{g}"), t + 1)
                        V.tensor_tensor(den[g], den[g], es_[g], ALU.add).then_inc(S(f"v_den{g}"), 1)
                        v.wait_ge(S(f"v_den{g}"), t + 1)
                        V.reciprocal(rcp[g], den[g]).then_inc(S(f"v_rcp{g}"), 1)
                        v.wait_ge(S(f"v_rcp{g}"), t + 1)
                        V.tensor_tensor(sA[g], sA[g], bc(rcp[g], 2 * P), ALU.mult).then_inc(S(f"pn{g}"), 1)
                        if g == 0:
                            v.wait_ge(S("r_qk"), t + 1)
                            V.tensor_tensor(qk.rearrange("p f (a d) -> p (f a) d", d=HD), flat(0, 2).rearrange("p (h d) -> p h d", d=HD),
                                            bc(r16, HD), ALU.mult).then_inc(S("qk"), 1)
                    residual(t, R)
                    normed(t, R)
                    v.wait_ge(S("G_ps"), t + 1)
                    v.wait_ge(S("E"), t + 1)
                    v.wait_ge(S("Lo"), LV * t)
                    V.tensor_tensor(AT, flat(6, 2).rearrange("p (h i) -> p h i", i=P), E_, ALU.mult).then_inc(S("v_AT"), 1)
                    v.wait_ge(S("v_AT"), t + 1)
                    V.tensor_tensor(AT, AT, bc(gb[:, t, 0:NH], P), ALU.mult).then_inc(S("AT"), 1)
                    gain(t, R)
                    v.wait_ge(S("Lo"), LV * t + 1)
                    for g in range(2):
                        hs = slice(4 * g, 4 * g + 4)
                        V.tensor_tensor(MT[0][:, hs], bm(ident, 4), Lo[0][:, hs], ALU.subtract).then_inc(S(f"MT{g}"), 1)
                    v.wait_ge(S("QK_ps"), t + 1)
                    V.tensor_tensor(QK, flat(4, 2).rearrange("p (h i) -> p h i", i=P), E_, ALU.mult).then_inc(S("QK"), 1)
                    logits(t, R, dst)
                    for l in range(1, LV):
                        for g in range(2):
                            hs = slice(4 * g, 4 * g + 4)
                            v.wait_ge(S(f"PT{g}_ps"), (LV - 1) * t + l)
                            V.tensor_tensor(MT[l % 2][:, hs], MT[(l - 1) % 2][:, hs], bank(6 + g).rearrange("p (h i) -> p h i", i=P),
                                            ALU.subtract).then_inc(S(f"MT{g}"), 1)
                        if l == 2:
                            v.wait_ge(S("egam"), t + 1)
                            v.wait_ge(S("kS_ps"), t + 1)
                            V.tensor_tensor(slots(tmp), kqS_ps[:, :, 0], slots(bc(egam, HD)), ALU.mult).then_inc(S("v_kS"), 1)
                        if l == 3:
                            v.wait_ge(S("v_kS"), t + 1)
                            V.tensor_tensor(r_, vtok, tmp, ALU.subtract).then_inc(S("r"), 1)
                        if l == 4:
                            v.wait_ge(S("r"), t + 1)
                            V.tensor_tensor(slots(tmp), kqS_ps[:, :, 1], slots(bc(egam, HD)), ALU.mult).then_inc(S("v_qS"), 1)
                            V.tensor_tensor(Sst, Sst, bc(eglS[:, 0:4], HD), ALU.mult).then_inc(S("v_S"), 1)
                    for g in range(2):
                        hs = slice(4 * g, 4 * g + 4)
                        v.wait_ge(S(f"v{g}_ps"), t + 1)
                        V.tensor_tensor(vn[:, hs], bank(2 * (1 - g))[:, 0:4 * HD].rearrange("p (h d) -> p h d", d=HD), bc(gb[:, t, 4 * g:4 * g + 4], HD),
                                        ALU.mult).then_inc(S(f"vn{g}"), 1)
                    v.wait_ge(S("vn1"), t + 1)
                    V.tensor_tensor(vn2, vn, bc(kdec, HD), ALU.mult).then_inc(S("vn2"), 1)
                    for g in range(2):
                        hs = slice(4 * g, 4 * g + 4)
                        v.wait_ge(S(f"o{g}_ps"), t + 1)
                        V.tensor_tensor(o_[:, hs], bank(3 - 2 * g)[:, 0:4 * HD].rearrange("p (h d) -> p h d", d=HD), tmp[:, hs], ALU.add).then_inc(S("o"), 1)
                    v.wait_ge(S("v_S"), t + 1)
                    v.wait_ge(S("dS_ps"), t + 1)
                    V.tensor_tensor(Sst, Sst, bank(6)[:, 0:4 * HD].rearrange("p (f e) -> p f e", e=HD), ALU.add).then_inc(S("S"), 1)

                tile(0, DEC, lg[0:DEC, NT, :], first=True)
                with v.Fori(1, NT) as t:
                    tile(t, P, lg[:, bass.ds(t - 1, 1), :].rearrange("p a n -> p (a n)"))
                gated(NT - 1)
                residual(NT, P)
                normed(NT, P)
                gain(NT, P)
                logits(NT, P, lg[:, NT - 1, :])

            @block.scalar
            def _(act):
                A = nc.scalar

                def norm_rows(t, R, rows):
                    act.wait_ge(S("h"), t + 1)
                    act.wait_ge(S("xT2_ps"), t)
                    act.wait_ge(S("xs_out"), 16 * t)
                    A.activation(xs2[0:R], hh_[0:R], ACT.Square, accum_out=ssx[0:R]).then_inc(S("ssx"), 1)
                    act.dma_start(h_d[rows, :], hh_[0:R]).then_inc(S("h_out"), 16)

                def store_rows(t, R, rows):
                    act.wait_ge(S("xs2"), t + 1)
                    act.dma_start(xs_d[rows, :], xs2[0:R]).then_inc(S("xs_out"), 16)

                def mix_rows(t):
                    act.wait_ge(S("oT_ps"), t + 1)
                    A.activation(mix[:, 4:8, :], bank(7).rearrange("p (f q) -> p f q", q=P), ACT.Copy).then_inc(S("mixB"), 1)

                def tile(t, R, rows, first=False):
                    act.wait_ge(S("tok_ps"), t + 1)
                    A.activation(sq, flat(0, 2), ACT.Square).then_inc(S("sq"), 1)
                    if not first:
                        mix_rows(t - 1)
                    act.wait_ge(S("D"), t + 1)
                    act.wait_ge(S("kd_in"), t + 1)
                    A.activation(E_, E_, ACT.Exp).then_inc(S("E"), 1)
                    A.activation(kdec, kdec, ACT.Exp)
                    A.activation(egam, bank(6)[:, 0:NH], ACT.Exp)
                    gL = flat(4, 2).rearrange("p (h i) -> p h i", i=P)[:, :, P - 1]
                    A.activation(eglS[0:HD, 0:4], gL[0:HD, 0:4], ACT.Exp)
                    A.activation(eglS[HD:P, 0:4], gL[HD:P, 4:8], ACT.Exp).then_inc(S("egam"), 1)
                    act.wait_ge(S("tokv_ps"), t + 1)
                    A.activation(slots(vtok), natural(bank(7)), ACT.Copy).then_inc(S("vtok"), 1)
                    for g in range(2):
                        act.wait_ge(S(f"nm{g}"), t + 1)
                        for i in range(GQA):
                            A.activation(sA[g][:, i, :], sA[g][:, i, :], ACT.Exp, bias=nm_[g][:, i:i + 1], accum_out=den[g][:, i:i + 1])
                        A.activation(es_[g], es_[g], ACT.Exp).then_inc(S(f"p{g}"), 1)
                    act.wait_ge(S("qkT_ps"), t + 1)
                    A.activation(qkT, flat(4, 2).rearrange("p (a q) -> p a q", q=P), ACT.Copy).then_inc(S("qkT"), 1)
                    act.wait_ge(S("pT0_ps"), t + 1)
                    A.activation(pT, flat(2, 2).rearrange("p (a q) -> p a q", q=P), ACT.Copy).then_inc(S("pT0"), 1)
                    norm_rows(t, R, rows)
                    act.wait_ge(S("pT1_ps"), t + 1)
                    act.wait_ge(S("av0_ps"), t + 1)
                    A.activation(pT, flat(0, 2).rearrange("p (a q) -> p a q", q=P), ACT.Copy).then_inc(S("pT1"), 1)
                    act.wait_ge(S("av_ps"), t + 1)
                    A.activation(mix[:, 0:4, :], bank(2).rearrange("p (f q) -> p f q", q=P), ACT.Copy).then_inc(S("mixA"), 1)
                    store_rows(t, R, rows)
                    for l in range(LV):
                        for g in range(2):
                            hs = slice(4 * g, 4 * g + 4)
                            if l > 0:
                                act.wait_ge(S(f"X{g}_ps"), (LV - 1) * t + l)
                                A.activation(Xs[:, hs], bank(2 + g).rearrange("p (h i) -> p h i", i=P), ACT.Copy).then_inc(S(f"X{g}"), 1)
                        for g in range(2):
                            hs = slice(4 * g, 4 * g + 4)
                            if l < LV - 1:
                                act.wait_ge(S(f"Tr{g}_ps"), (LV - 1) * t + l + 1)
                                A.activation(M_[:, hs], bank(g).rearrange("p (h i) -> p h i", i=P), ACT.Copy).then_inc(S(f"M{g}"), 1)
                    act.wait_ge(S("o"), 2 * t + 2)
                    A.activation(tmp, o_, ACT.Square).then_inc(S("osq"), 1)

                tile(0, DEC, slice(SEQ, TOK), first=True)
                with act.Fori(1, NT) as t:
                    tile(t, P, bass.ds(act.snap(t * P - P), P))
                mix_rows(NT - 1)
                norm_rows(NT, P, slice(SEQ - P, SEQ))
                store_rows(NT, P, slice(SEQ - P, SEQ))
                act.wait_ge(S("h_out"), 16 * (NT + 1))
                act.wait_ge(S("xs_out"), 16 * (NT + 1))

            @block.tensor
            def _(pe):
                T = nc.tensor

                def half_of(h):
                    return slice((h % 2) * HD, (h % 2) * HD + HD)

                def turn_out(t):
                    pe.wait_ge(S("og"), t + 1)
                    for f in range(4):
                        mm = T.transpose(bank(7)[:, f * P:(f + 1) * P], vn.rearrange("p h d -> p (h d)")[:, f * P:(f + 1) * P], ident)
                    mm.then_inc(S("oT_ps"), 1)

                def project(t, R, src, n):
                    for k in range(KD):
                        mm = T.matmul(bank(2 + n)[0:R], src[:, k, :], wout[:, k, n * 512:(n + 1) * 512], start=(k == 0), stop=(k == KD - 1))
                    return mm

                def turn_rows(t, R):
                    pe.wait_ge(S("xs2"), t + 1)
                    for k in range(KD):
                        mm = T.transpose(flat(0, 2)[:, k * P:k * P + R], xs2[0:R].rearrange("p (c k) -> p k c", k=KD)[:, k, :], ident[0:R, 0:R])
                    mm.then_inc(S("xT2_ps"), 1)

                def route(t, R):
                    pe.wait_ge(S("xT2"), t + 1)
                    pe.wait_ge(S("wr"), 32)
                    for k in range(KD):
                        mm = T.matmul(bank(3)[0:R, 0:NG + NE], xT2[:, k, 0:R], wr[:, k, :], start=(k == 0), stop=(k == KD - 1))
                    mm.then_inc(S("lg_ps"), 1)

                def tile(t, R, src, first=False):
                    pe.wait_ge(S("att_in"), 64 * t + 64)
                    pe.wait_ge(S("o"), 2 * t)
                    for g in range(2):
                        for i in range(GQA):
                            h = GQA * g + ORD[i]
                            ks = kst if h % 2 == g else kswst
                            mm = T.matmul(scores_ps(g)[:, i, :], qst[half_of(h), h // 2, :], ks[half_of(h), :], start=True, stop=True)
                        mm.then_inc(S(f"sc{g}"), 1)
                    pe.wait_ge(S("gU"), t + 1)
                    pe.wait_ge(S("S"), t + 1)
                    T.matmul(bank(6)[:, 0:NH], cst[:, C_U:C_U + P], gb[:, t, NH:2 * NH], start=True, stop=True)
                    for n in range(2):
                        mm = T.matmul(bank(4 + n), ones, gU[:, 4 * n:4 * n + 4].rearrange("p h i -> p (h i)"), start=True, stop=True)
                    mm.then_inc(S("gam_ps"), 1)
                    pe.wait_ge(S("y_in"), 16 * t + 16)
                    pe.wait_ge(S("s0"), t + 1)
                    for f in range(8):
                        mm = T.transpose(flat(0, 2)[:, f * P:(f + 1) * P], yst[:, f, :], ident)
                    mm.then_inc(S("tok_ps"), 1)
                    if not first:
                        turn_out(t - 1)
                        pe.wait_ge(S("mixB"), t)
                    pe.wait_ge(S("wout"), 16)
                    pe.wait_ge(S("s1"), t + 1)
                    project(t, R, src, 0)
                    for f in range(4):
                        mm = T.transpose(bank(7)[:, f * P:(f + 1) * P], yst[:, 8 + f, :], ident)
                    mm.then_inc(S("tokv_ps"), 1)
                    project(t, R, src, 1).then_inc(S("proj_ps"), 1)
                    pe.wait_ge(S("qk"), t + 1)
                    pe.wait_ge(S("D"), t + 1)
                    pe.wait_ge(S("egam"), t + 1)
                    for f in range(8):
                        mm = T.transpose(flat(4, 2)[:, f * P:(f + 1) * P], qk[:, f, :], ident)
                    mm.then_inc(S("qkT_ps"), 1)
                    for g in range(2):
                        pe.wait_ge(S(f"pn{g}"), t + 1)
                        if g == 0:
                            pe.wait_ge(S("h"), t + 1)
                        for i in range(GQA):
                            for b in range(2):
                                mm = T.transpose(flat(2 - 2 * g, 2)[:, (2 * i + b) * P:(2 * i + b + 1) * P], sA[g][:, i, b * P:(b + 1) * P], ident)
                        mm.then_inc(S(f"pT{g}_ps"), 1)
                    pe.wait_ge(S("qkT"), t + 1)
                    pe.wait_ge(S("vtok"), t + 1)
                    for s, h in enumerate(SLOT):
                        kT = qkT[half_of(h), 4 + h // 2, :]
                        mm = T.matmul(flat(6, 2)[:, s * P:(s + 1) * P], kT, kT, start=True, stop=True)
                    mm.then_inc(S("G_ps"), 1)

                    def values(g):
                        pe.wait_ge(S(f"pT{g}"), t + 1)
                        for i in range(GQA):
                            h = GQA * g + ORD[i]
                            for b in range(2):
                                mm = T.matmul(bank(2)[half_of(h), (h // 2) * P:(h // 2 + 1) * P], vst[:, b * P + g * HD:b * P + g * HD + HD],
                                              pT[:, 2 * i + b, :], start=(b == 0), stop=(b == 1))
                        return mm

                    values(0).then_inc(S("av0_ps"), 1)
                    for s, h in enumerate(SLOT):
                        mm = T.matmul(flat(4, 2)[:, s * P:(s + 1) * P], qkT[half_of(h), 4 + h // 2, :], qkT[half_of(h), h // 2, :], start=True, stop=True)
                    mm.then_inc(S("QK_ps"), 1)
                    pe.wait_ge(S("pT1"), t + 1)
                    turn_rows(t, R)
                    values(1).then_inc(S("av_ps"), 1)
                    route(t, R)
                    pe.wait_ge(S("lg"), t + 1)
                    pe.wait_ge(S("mixA"), t + 1)
                    for l in range(LV):
                        if l > 0:
                            for g in range(2):
                                pe.wait_ge(S(f"M{g}"), (LV - 1) * t + l)
                                pe.wait_ge(S("Lo"), LV * t + l + 1)
                                for h in range(4 * g, 4 * g + 4):
                                    mm = T.matmul(bank(2 + g)[:, (h % 4) * P:(h % 4 + 1) * P], Lo[l % 2][:, h, :], M_[:, h, :], start=True, stop=True)
                                mm.then_inc(S(f"X{g}_ps"), 1)
                            if l == 2:
                                pe.wait_ge(S("QK"), t + 1)
                                for n in range(2):
                                    for h in SLOT:
                                        mm = T.matmul(kqS_ps[:, h % 2, n, h // 2, :], qkT[half_of(h), 4 - 4 * n + h // 2, :], Sst[half_of(h), h // 2, :], start=True, stop=True)
                                mm.then_inc(S("kS_ps"), 1)
                            for g in range(2):
                                pe.wait_ge(S(f"X{g}"), (LV - 1) * t + l)
                                if l == 1:
                                    pe.wait_ge(S("AT"), t + 1)
                                for h in range(4 * g, 4 * g + 4):
                                    mm = T.matmul(bank(6 + g)[:, (h % 4) * P:(h % 4 + 1) * P], Xs[:, h, :], MT[(l - 1) % 2][:, h, :], start=True, stop=True)
                                mm.then_inc(S(f"PT{g}_ps"), 1)
                        if l < LV - 1:
                            for g in range(2):
                                pe.wait_ge(S(f"MT{g}"), LV * t + l + 1)
                                for h in range(4 * g, 4 * g + 4):
                                    mm = T.transpose(bank(g)[:, (h % 4) * P:(h % 4 + 1) * P], MT[l % 2][:, h, :], ident)
                                mm.then_inc(S(f"Tr{g}_ps"), 1)
                    pe.wait_ge(S("r"), t + 1)
                    for g in range(2):
                        pe.wait_ge(S(f"MT{g}"), LV * t + LV)
                        for h in range(4 * g, 4 * g + 4):
                            mm = T.matmul(bank(2 * (1 - g))[:, (h % 4) * HD:(h % 4 + 1) * HD], MT[(LV - 1) % 2][:, h, :], r_[:, h, :], start=True, stop=True)
                        mm.then_inc(S(f"v{g}_ps"), 1)
                    for g in range(2):
                        pe.wait_ge(S(f"vn{g}"), t + 1)
                        for h in range(4 * g, 4 * g + 4):
                            mm = T.matmul(bank(3 - 2 * g)[:, (h % 4) * HD:(h % 4 + 1) * HD], QK[:, h, :], vn[:, h, :], start=True, stop=True)
                        mm.then_inc(S(f"o{g}_ps"), 1)
                    pe.wait_ge(S("vn2"), t + 1)
                    for s, h in enumerate(SLOT):
                        mm = T.matmul(bank(6)[half_of(h), (h // 2) * HD:(h // 2 + 1) * HD], qk[:, 4 + h // 2, half_of(h)], vn2[:, s, :], start=True, stop=True)
                    mm.then_inc(S("dS_ps"), 1)

                tile(0, DEC, mixD, first=True)
                with pe.Fori(1, NT) as t:
                    tile(t, P, mix)
                turn_out(NT - 1)
                pe.wait_ge(S("mixB"), NT)
                project(NT, P, mix, 0)
                project(NT, P, mix, 1).then_inc(S("proj_ps"), 1)
                turn_rows(NT, P)
                route(NT, P)

        stage_ends()
        mem.at = after_mix
        U = 4
        wgu = [mem.take(KD, 2 * DE) for _ in range(U)]
        wd = [mem.take(KE, D) for _ in range(U)]
        after_weights = mem.at
        NTT = NT + 1
        fill = mem.take(MAXB, 4).bitcast(I32)
        gmx, pm, sm, pgs, m1, m2, ex, dn, gate1, gate2 = (mem.take(NTT) for _ in range(10))
        eqg, selg, exg = mem.take(NTT, NG), mem.take(NTT, NG), mem.take(NTT, NG)
        wide, oh1, oh2, slotE, geb = (mem.take(NTT, NE) for _ in range(5))
        mask = mem.take(NTT, NE)
        le, le2, q1, q2, e1h, e2h = (mem.take(NTT, EPG) for _ in range(6))
        cnt, ext, incl, base = (mem.take(NE) for _ in range(4))
        cmp8 = mem.take(NE, 8)
        cmpo, cmpo2, eo = mem.take(XB, NE), mem.take(XB, NE), mem.take(XB + 1)
        dst, dsti = mem.take(2, NTT), mem.take(2, NTT).bitcast(I32)
        pay = mem.take(2, NTT * 4).rearrange("p k (t c) -> p k t c", c=4).bitcast(I32)
        tabrow = mem.take(P, 4)

        def cols(c0, n):
            return cst[:, c0:c0 + n]

        def load_expert(sp, u, e, gate_up, down):
            for w, lo in (("w_gate", 0), ("w_up", DE)):
                sp.dma_start(wgu[u][:, :, lo:lo + DE], I[w][0, bass.ds(e, 1)].rearrange("a (p k) n -> p (a k) n", k=KD)).then_inc(gate_up, 16)
            sp.dma_start(wd[u].rearrange("p k n -> p (k n)"), I["w_down"][0, bass.ds(e, 1)].rearrange("a (p k) n -> p (a k n)", k=KE)).then_inc(down, 16)

        with nc.Block() as block:
            @block.sync
            def _(sp):
                for u in range(U):
                    load_expert(sp, u, u, L(f"wgu{u}"), L(f"wd{u}"))

            @block.vector
            def _(v):
                V = nc.vector
                tick = [0]

                def chain(ins):
                    tick[0] += 1
                    ins.then_inc(S("dve_route"), 1)
                    v.wait_ge(S("dve_route"), tick[0])

                def first(values, best, prio, marks, out):
                    n = values.shape[2]
                    chain(V.tensor_tensor(marks, values, bc(best, n), ALU.is_ge))
                    chain(V.tensor_tensor(marks, marks, bm(prio, NTT), ALU.mult))
                    chain(V.tensor_reduce(pm, marks, AX.X, ALU.max))
                    chain(V.tensor_tensor(out, marks, bc(pm, n), ALU.is_equal))

                chain(V.memset(fill, 0))
                chain(V.memset(fill[:, :, 1], DUMP))
                V.memset(pay, 0).then_inc(S("fill"), 1)
                G = lg[:, :, 0:NG]
                chain(V.tensor_reduce(gmx, G, AX.X, ALU.max))
                V.tensor_tensor(exg, G, bc(gmx, NG), ALU.subtract).then_inc(S("exg"), 1)
                first(G, gmx, cols(C_GP, NG), eqg, selg)
                w4 = wide.rearrange("p t (g j) -> p t g j", g=NG)
                l4 = lg[:, :, NG:].rearrange("p t (g j) -> p t g j", g=NG)
                s4 = selg.unsqueeze(3).to_broadcast([P, NTT, NG, EPG])
                chain(V.tensor_tensor(w4, l4, s4, ALU.mult))
                chain(V.tensor_reduce(le, wide.rearrange("p t (g j) -> p t j g", g=NG), AX.X, ALU.add))
                chain(V.tensor_reduce(m1, le, AX.X, ALU.max))
                first(le, m1, cols(C_EP, EPG), q1, e1h)
                chain(V.scalar_tensor_tensor(le2, e1h, -BIG, le, ALU.mult, ALU.add))
                chain(V.tensor_reduce(m2, le2, AX.X, ALU.max))
                first(le2, m2, cols(C_EP, EPG), q2, e2h)
                V.tensor_tensor(ex, m2, m1, ALU.subtract).then_inc(S("ex"), 1)
                val = cols(C_VAL, NTT)
                for e_, o in ((e1h, oh1), (e2h, oh2)):
                    o4 = o.rearrange("p t (g j) -> p t g j", g=NG)
                    chain(V.tensor_tensor(o4, s4, e_.unsqueeze(2).to_broadcast([P, NTT, NG, EPG]), ALU.mult))
                    chain(V.tensor_tensor(o, o, bc(val, NE), ALU.mult))
                V.tensor_tensor(mask, oh1, oh2, ALU.add).then_inc(S("mask"), 1)
                v.wait_ge(S("exps"), 1)
                chain(V.tensor_reduce(sm, exg, AX.X, ALU.add))
                chain(V.tensor_scalar(dn, ex, 1.0, None, ALU.add))
                chain(V.tensor_tensor(dn, dn, sm, ALU.mult))
                chain(V.reciprocal(gate1, dn))
                chain(V.tensor_tensor(gate2, gate1, ex, ALU.mult))
                for k, gt in ((0, gate1), (1, gate2)):
                    V.tensor_copy(pay[:, k, :, 0], cols(C_TT, NTT))
                    V.tensor_scalar(pay[:, k, :, 1], cols(C_TT, NTT), float(k * TOK), None, ALU.add)
                    chain(V.tensor_copy(pay[:, k, :, 2], gt.bitcast(I32)))
                v.wait_ge(S("pos"), 1)
                pos = bank(0)[:, 0:NTT * NE].rearrange("p (t e) -> p t e", e=NE)
                chain(V.tensor_copy(cnt, bank(1)[:, 0:NE]))
                chain(V.tensor_tensor(cmp8, bc(cnt, 8), bm(cols(C_THR, 8), NE), ALU.is_gt))
                chain(V.tensor_reduce(ext, cmp8, AX.X, ALU.add))
                chain(V.tensor_tensor_scan(incl, ones[:, 0:NE], ext, 0.0, ALU.mult, ALU.add))
                chain(V.tensor_tensor(base, incl, ext, ALU.subtract))
                chain(V.tensor_tensor(cmpo, bc(cols(C_OV, XB), NE), bm(base, XB), ALU.is_ge))
                chain(V.tensor_scalar(base, base, float(P), float((NE - 1) * P), ALU.mult, ALU.add))
                chain(V.tensor_tensor(base, base, cols(C_E128, NE), ALU.subtract))
                chain(V.tensor_scalar(geb, pos, float(P), None, ALU.is_ge))
                chain(V.tensor_tensor(geb, geb, bm(base, NTT), ALU.mult))
                chain(V.tensor_tensor(slotE, pos, bm(cols(C_E128, NE), NTT), ALU.add))
                chain(V.tensor_tensor(slotE, slotE, geb, ALU.add))
                for k, o in ((0, oh1), (1, oh2)):
                    chain(V.tensor_tensor(wide, slotE, o, ALU.mult))
                    chain(V.tensor_reduce(dst[:, k], wide, AX.X, ALU.add))
                chain(V.tensor_scalar(pm, val, -float(DUMP), float(DUMP), ALU.mult, ALU.add))
                chain(V.tensor_tensor(dst, dst, bm(pm, 2), ALU.add))
                V.tensor_copy(dsti, dst).then_inc(S("dst"), 1)
                chain(V.tensor_tensor(cmpo2, bc(cols(C_OV, XB), NE), bm(incl, XB), ALU.is_lt))
                chain(V.tensor_tensor(cmpo, cmpo, cmpo2, ALU.mult))
                chain(V.tensor_tensor(cmpo, cmpo, bm(cols(C_EI, NE), XB), ALU.mult))
                chain(V.tensor_reduce(eo[:, 0:XB], cmpo, AX.X, ALU.add))
                chain(V.tensor_copy(eo[:, XB:], incl[:, NE - 1:NE]))
                V.tensor_copy(blk[0:1], eo[0:1]).then_inc(S("blk"), 1)
                v.wait_ge(S("tabT"), 1)
                V.tensor_copy(tabI[:, 0:3], bank(2)[:, 0:3 * MAXB].rearrange("p (c b) -> p c b", b=MAXB).bitcast(I32)).then_inc(S("tabI"), 1)

            @block.scalar
            def _(act):
                act.wait_ge(S("exg"), 1)
                nc.scalar.activation(exg, exg, ACT.Exp)
                act.wait_ge(S("ex"), 1)
                nc.scalar.activation(ex, ex, ACT.Exp).then_inc(S("exps"), 1)

            @block.tensor
            def _(pe):
                pe.wait_ge(S("mask"), 1)
                mk = mask.rearrange("p t e -> p (t e)")
                nc.tensor.matmul(bank(0)[:, 0:NTT * NE], cols(C_US, P), mk, start=True, stop=False, skip_group_check=True)
                for s in range(1, NTT):
                    nc.tensor.matmul(bank(0)[:, s * NE:NTT * NE], ones, mk[:, 0:(NTT - s) * NE], start=False, stop=(s == NTT - 1), skip_group_check=True)
                for t in range(NTT):
                    mm = nc.tensor.matmul(bank(1)[:, 0:NE], ones, mask[:, t, :], start=(t == 0), stop=(t == NTT - 1))
                mm.then_inc(S("pos"), 1)
                pe.wait_ge(S("tabrow"), 16)
                for c in range(3):
                    mm = nc.tensor.transpose(bank(2)[:, c * MAXB:(c + 1) * MAXB], tabrow[0:MAXB, :, c], ident[0:MAXB, 0:MAXB])
                mm.then_inc(S("tabT"), 1)

            @block.gpsimd
            def _(g):
                g.wait_ge(S("fill"), 1)
                g.dma_start(tab_d.rearrange("(p b) c -> p b c", b=MAXB), fill).then_inc(S("filled"), 16)
                g.wait_ge(S("filled"), 16)
                g.wait_ge(S("dst"), 1)
                n = 0
                for k in range(2):
                    for t in range(NTT):
                        g.indirect_dma_start(out=tab_d, out_offset=bass.IndirectOffsetOnAxis(ap=dsti[:, k, t:t + 1], axis=0),
                                             in_=pay[:, k, t, :], in_offset=None, bounds_check=MAXB * P - 1, oob_is_err=False).then_inc(S("scat"), 16)
                        n += 16
                g.wait_ge(S("scat"), n)
                g.dma_start(tabrow[0:MAXB].bitcast(I32), tab_d.rearrange("(b s) c -> b s c", s=P)).then_inc(S("tabrow"), 16)
                g.wait_ge(S("tabrow"), 16)

        stage_ends()
        mem.at = after_weights
        xg = [mem.take(D) for _ in range(U)]
        xgT = [mem.take(KD, P) for _ in range(2)]
        sg = [mem.take(DE) for _ in range(2)]
        hm = [mem.take(DE) for _ in range(2)]
        hT = [mem.take(KE, P) for _ in range(2)]
        ye = [mem.take(D) for _ in range(2)]
        it, io = ([mem.take(1).bitcast(I32) for _ in range(U)] for _ in range(2))
        gt = [mem.take(1) for _ in range(U)]
        wpg, wpp, gfB = mem.take(KD, D), mem.take(KE, D), mem.take(D)

        class Slot:

            def __init__(self, u, n, b, alone=None):
                self.u, self.n, self.b = u, n, b
                self.w = n if alone is None else n + NE // U + 1
                self.v = u % 2
                self.m = 2 * n + u // 2 if alone is None else alone
                self.c = b if alone is None else alone
                self.a, self.h = f"{u}", f"{u % 2}h"

        def load_block(sp, s, e):
            sp.wait_ge(S("down" + s.a), s.n)
            load_expert(sp, s.u, e, L(f"wgu{s.u}"), L(f"wd{s.u}"))

        def gather(g, s):
            g.wait_ge(S("xgT_ps" + s.a), s.n)
            g.wait_ge(S("hm" + s.a), s.n)
            g.tensor_copy(it[s.u], tabI[:, 0, bass.ds(s.b, 1)])
            g.tensor_copy(gt[s.u].bitcast(I32), tabI[:, 2, bass.ds(s.b, 1)]).then_inc(S("idx" + s.a), 1)
            g.wait_ge(S("idx" + s.a), s.n + 1)
            settle(g)
            g.indirect_dma_start(out=xg[s.u], out_offset=None, in_=xs_d,
                                 in_offset=bass.IndirectOffsetOnAxis(ap=it[s.u], axis=0)).then_inc(S("xg" + s.a), 16)

        def scatter(g, s):
            g.wait_ge(S("ye_out" + s.a), 16 * s.n)
            g.tensor_copy(io[s.u], tabI[:, 1, bass.ds(s.b, 1)]).then_inc(S("rows" + s.a), 1)
            g.wait_ge(S("ye" + s.h), s.m + 1)
            g.wait_ge(S("rows" + s.a), s.n + 1)
            settle(g)
            g.indirect_dma_start(out=ye_d, out_offset=bass.IndirectOffsetOnAxis(ap=io[s.u], axis=0), in_=ye[s.v], in_offset=None,
                                 bounds_check=2 * TOK - 1, oob_is_err=False).then_inc(S("ye_out" + s.a), 16)

        def turn_block(pe, s):
            pe.wait_ge(S("xg" + s.a), 16 * s.n + 16)
            pe.wait_ge(S("xgT_all"), s.c)
            for k in range(KD):
                mm = nc.tensor.transpose(flat(0, 2)[:, k * P:(k + 1) * P], xg[s.u].rearrange("p (c k) -> p k c", k=KD)[:, k, :], ident)
            mm.then_inc(S("xgT_ps" + s.a), 1)

        def up_block(pe, s):
            pe.wait_ge(S("xgT" + s.h), s.m + 1)
            pe.wait_ge(L(f"wgu{s.u}"), 32 * s.w + 32)
            pe.wait_ge(S("hm" + s.h), s.m)
            for k in range(KD):
                mm = nc.tensor.matmul(bank(2 + s.v), xgT[s.v][:, k, :], wgu[s.u][:, k, :], start=(k == 0), stop=(k == KD - 1))
            mm.then_inc(S("gu" + s.h), 1)

        def turn_hidden(pe, s):
            pe.wait_ge(S("hm" + s.h), s.m + 1)
            pe.wait_ge(S("hT_all"), s.c)
            for k in range(KE):
                mm = nc.tensor.transpose(bank(4)[:, k * P:(k + 1) * P], hm[s.v].rearrange("p (c k) -> p k c", k=KE)[:, k, :], ident)
            mm.then_inc(S("hT_ps" + s.h), 1)

        def down_block(pe, s):
            pe.wait_ge(S("hT" + s.h), s.m + 1)
            pe.wait_ge(L(f"wd{s.u}"), 16 * s.w + 16)
            pe.wait_ge(S("ye_all"), s.c)
            for n in range(2):
                for k in range(KE):
                    mm = nc.tensor.matmul(bank(6 + n), hT[s.v][:, k, :], wd[s.u][:, k, n * 512:(n + 1) * 512], start=(k == 0), stop=(k == KE - 1))
            mm.then_inc(S("down" + s.a), 1)

        def gain_block(v, s):
            v.wait_ge(S("xgT_ps" + s.a), s.n + 1)
            v.wait_ge(S("gu" + s.h), s.m)
            nc.vector.tensor_tensor(xgT[s.v], flat(0, 2).rearrange("p (k c) -> p k c", c=P), bc(g_ffn, P), ALU.mult).then_inc(S("xgT" + s.h), 1)
            v.wait_ge(S("xgT" + s.h), s.m + 1)
            v.sem_inc(S("xgT_all"), 1)

        def hidden_block(v, s):
            v.wait_ge(S("sg" + s.h), s.m + 1)
            v.wait_ge(S("idx" + s.a), s.n + 1)
            v.wait_ge(S("hT_ps" + s.h), s.m)
            nc.vector.scalar_tensor_tensor(hm[s.v], sg[s.v], gt[s.u], bank(2 + s.v)[:, DE:], ALU.mult, ALU.mult).then_inc(S("hm" + s.h), 1)
            v.wait_ge(S("hm" + s.h), s.m + 1)
            v.sem_inc(S("hm" + s.a), 1)

        def hidden_out(v, s):
            v.wait_ge(S("hT_ps" + s.h), s.m + 1)
            nc.vector.tensor_copy(hT[s.v].rearrange("p k c -> p (k c)"), bank(4)[:, 0:KE * P]).then_inc(S("hT" + s.h), 1)
            v.wait_ge(S("hT" + s.h), s.m + 1)
            v.sem_inc(S("hT_all"), 1)

        def silu_block(act, s):
            act.wait_ge(S("gu" + s.h), s.m + 1)
            act.wait_ge(S("hm" + s.h), s.m)
            nc.scalar.activation(sg[s.v], bank(2 + s.v)[:, 0:DE], ACT.Silu).then_inc(S("sg" + s.h), 1)

        def out_block(act, s, before, scattered):
            act.wait_ge(S("down" + s.a), s.n + 1)
            if before:
                act.wait_ge(S("ye_out" + before.a), scattered)
            nc.scalar.activation(ye[s.v], flat(6, 2), ACT.Copy).then_inc(S("ye" + s.h), 1)
            act.wait_ge(S("ye" + s.h), s.m + 1)
            act.sem_inc(S("ye_all"), 1)

        def slot(n, u):
            if u < 0:
                return slot(n - 1, u + U)
            if u >= U:
                return slot(n + 1, u - U)
            return Slot(u, n, n * U + u)

        def rounds(eng, body):
            for u in range(U):
                body(0, u, u)
            with eng.Fori(1, NE // U) as n:
                for u in range(U):
                    body(n, u, U)

        with nc.Block() as block:
            @block.sync
            def _(sp):
                with sp.Fori(1, NE // U) as n:
                    for u in range(U):
                        load_block(sp, slot(n, u), sp.snap(n * U + u))
                load_block(sp, slot(NE // U, 0), sp.value_load(blk[0:1, 0:1], min_val=0, max_val=NE - 1))
                sp.dma_start(wpp, I["w_ple_proj"][0].rearrange("(k p) n -> p k n", p=P)).then_inc(L("wpp"), 16)
                sp.dma_start(wpg, I["w_ple_gate"][0].rearrange("(p k) n -> p k n", k=KD)).then_inc(L("wpg"), 16)
                sp.dma_start(gfB, I["norm_final"].partition_broadcast(P)).then_inc(L("gf"), 16)

            @block.gpsimd
            def _(g):
                def body(n, u, seen, last=False):
                    if not last:
                        gather(g, slot(n, u + 2))
                    if seen >= 2:
                        scatter(g, slot(n, u - 2))

                gather(g, slot(0, 0))
                gather(g, slot(0, 1))
                for u in range(U):
                    body(0, u, u)
                with g.Fori(1, NE // U - 1) as n:
                    for u in range(U):
                        body(n, u, U)
                for u in range(U + 1):
                    body(NE // U - 1, u, U, last=(u >= U - 1))
                scatter(g, slot(NE // U, -1))
                scatter(g, slot(NE // U, 0))
                for u in range(U):
                    g.wait_ge(S(f"ye_out{u}"), 16 * (NE // U + (u == 0)))

            @block.tensor
            def _(pe):
                turn_block(pe, slot(0, 0))

                def body(n, u, seen, last=False):
                    up_block(pe, slot(n, u))
                    if seen >= 1:
                        turn_hidden(pe, slot(n, u - 1))
                    if not last:
                        turn_block(pe, slot(n, u + 1))
                    if seen >= 1:
                        down_block(pe, slot(n, u - 1))

                for u in range(U):
                    body(0, u, u)
                with pe.Fori(1, NE // U - 1) as n:
                    for u in range(U):
                        body(n, u, U)
                for u in range(U + 1):
                    body(NE // U - 1, u, U, last=(u == U))
                turn_hidden(pe, slot(NE // U, 0))
                down_block(pe, slot(NE // U, 0))

            @block.vector
            def _(v):
                def body(n, u, seen, last=False):
                    if seen >= 1:
                        hidden_out(v, slot(n, u - 1))
                    if not last:
                        gain_block(v, slot(n, u + 1))
                    hidden_block(v, slot(n, u))

                gain_block(v, slot(0, 0))
                for u in range(U):
                    body(0, u, u)
                with v.Fori(1, NE // U - 1) as n:
                    for u in range(U):
                        body(n, u, U)
                for u in range(U + 1):
                    body(NE // U - 1, u, U, last=(u == U))
                hidden_out(v, slot(NE // U, 0))

            @block.scalar
            def _(act):
                def body(n, u, seen):
                    silu_block(act, slot(n, u))
                    if seen >= 1:
                        s, before = slot(n, u - 1), slot(n, u - 3)
                        out_block(act, s, before if seen >= 3 else None, 16 * before.n + 16)

                rounds(act, body)
                body(NE // U, 0, U)
                out_block(act, slot(NE // U, 0), slot(NE // U, -2), 16 * NE // U)

        stage_ends()
        with nc.Block() as block:
            def blocks(eng, body):
                count = eng.value_load(blk[0:1, XB:XB + 1], min_val=0, max_val=XB)
                with eng.If(count > 1):
                    with eng.Fori(0, XB - 1) as o:
                        with eng.If(count > o + 1):
                            body(Slot(0, o, eng.snap(o + NE + 1), o))

            @block.sync
            def _(sp):
                blocks(sp, lambda s: load_block(sp, s, sp.value_load(blk[0:1, bass.ds(s.n + 1, 1)], min_val=0, max_val=NE - 1)))

            @block.gpsimd
            def _(g):
                def body(s):
                    gather(g, s)
                    scatter(g, s)
                    g.wait_ge(S("ye_out0"), 16 * s.n + 16)
                    g.sem_inc(S("scattered"), 1)

                blocks(g, body)

            @block.tensor
            def _(pe):
                def body(s):
                    turn_block(pe, s)
                    up_block(pe, s)
                    turn_hidden(pe, s)
                    down_block(pe, s)

                blocks(pe, body)

            @block.vector
            def _(v):
                def body(s):
                    gain_block(v, s)
                    hidden_block(v, s)
                    hidden_out(v, s)

                blocks(v, body)

            @block.scalar
            def _(act):
                def body(s):
                    silu_block(act, s)
                    out_block(act, s, s, 16 * s.n)

                blocks(act, body)

        stage_ends()
        mem.at = after_mix
        F = 3
        hf, y0, y1, xf, sgf, of = ([mem.take(D) for _ in range(F)] for _ in range(6))
        xfT = [mem.take(KD, P) for _ in range(F)]
        pf, pfT = [mem.take(PLE) for _ in range(F)], [mem.take(KE, P) for _ in range(F)]
        sc = [[mem.take(1) for _ in range(6)] for _ in range(F)]

        def nth(n, u):
            return (n, u) if u < F else (n + 1, u - F)

        def steps(eng, step):
            with eng.Fori(0, NT // F) as n:
                for u in range(F):
                    step(n, u, F)
            for u in range(F):
                step(NT // F, u, F - 1 - u)

        def before(name, n, u):
            return (S(f"{name}{u - 1}"), n + 1) if u else (S(f"{name}{F - 1}"), n)

        with nc.Block() as block:
            @block.sync
            def _(sp):
                def load(n, u, t):
                    R, rows = (DEC, slice(SEQ, TOK)) if t is None else (P, bass.ds(t * P, P))
                    yrow = [slice(k * TOK + SEQ, k * TOK + TOK) if t is None else bass.ds(t * P + k * TOK, P) for k in range(2)]
                    psrc = I["p_sample"][0, :, 0, :] if t is None else I["p_prompt"][0, 0, rows, :]
                    sp.wait_ge(S(f"h3{u}"), n)
                    sp.wait_ge(S(f"pT_ps{u}"), n)
                    for dst_, src in ((hf[u], h_d[rows, :]), (y0[u], ye_d[yrow[0], :]), (y1[u], ye_d[yrow[1], :]), (pf[u], psrc)):
                        sp.dma_start(dst_[0:R], src).then_inc(S(f"in{u}"), 16)

                with sp.Fori(0, NT // F) as n:
                    for u in range(F):
                        load(n, u, sp.snap(F * n + u))
                for t in range(NT - NT % F, NT):
                    load(NT // F, t % F, t)
                load(NT // F, NT % F, None)

            @block.gpsimd
            def _(g):
                def power(n, u, which):
                    g.wait_ge(S(f"ms{which}{u}"), n + 1)
                    g.tensor_tensor(sc[u][3 * which + 2], sc[u][3 * which + 1], half, ALU.pow).then_inc(S(f"rs{which}{u}"), 1)

                power(0, 0, 0)
                power(0, 1, 0)

                def step(n, u, left):
                    if left > 1:
                        power(*nth(n, u + 2), 0)
                    power(n, u, 1)

                steps(g, step)

            @block.vector
            def _(v):
                V = nc.vector

                def sum_in(n, u):
                    v.wait_ge(S(f"in{u}"), 64 * n + 64)
                    V.tensor_tensor(hf[u], hf[u], y0[u], ALU.add).then_inc(S(f"v_h{u}"), 1)
                    v.wait_ge(S(f"v_h{u}"), n + 1)
                    V.tensor_tensor(hf[u], hf[u], y1[u], ALU.add).then_inc(S(f"h2{u}"), 1)
                    v.wait_ge(S(f"ssA{u}"), n + 1)
                    V.tensor_scalar(sc[u][1], sc[u][0], 1.0 / D, EPS, ALU.mult, ALU.add).then_inc(S(f"ms0{u}"), 1)
                    v.wait_ge(S(f"rs0{u}"), n + 1)
                    V.tensor_scalar(xf[u], hf[u], sc[u][2], None, ALU.mult).then_inc(S(f"xf{u}"), 1)

                def gain(n, u):
                    v.wait_ge(S(f"xfT_ps{u}"), n + 1)
                    v.wait_ge(S(f"gate_ps{u}"), n)
                    V.tensor_tensor(xfT[u], flat(0, 2).rearrange("p (k c) -> p k c", c=P), bc(g_ple, P), ALU.mult).then_inc(S(f"xfT{u}"), 1)
                    v.wait_ge(S(f"pT_ps{u}"), n + 1)
                    v.wait_ge(S(f"pp_ps{u}"), n)
                    V.tensor_copy(pfT[u].rearrange("p k c -> p (k c)"), bank(2)[:, 0:KE * P]).then_inc(S(f"pfT{u}"), 1)

                def close(n, u):
                    v.wait_ge(S(f"pp_ps{u}"), n + 1)
                    v.wait_ge(S(f"sgf{u}"), n + 1)
                    V.tensor_tensor(sgf[u], sgf[u], flat(6, 2), ALU.mult).then_inc(S(f"pg{u}"), 1)
                    v.wait_ge(S(f"pg{u}"), n + 1)
                    V.tensor_tensor(sgf[u], sgf[u], hf[u], ALU.add).then_inc(S(f"h3{u}"), 1)
                    v.wait_ge(S(f"ssB{u}"), n + 1)
                    V.tensor_scalar(sc[u][4], sc[u][3], 1.0 / D, EPS, ALU.mult, ALU.add).then_inc(S(f"ms1{u}"), 1)
                    v.wait_ge(S(f"rs1{u}"), n + 1)
                    v.wait_ge(L("gf"), 16)
                    V.scalar_tensor_tensor(of[u], sgf[u], sc[u][5], gfB, ALU.mult, ALU.mult).then_inc(S(f"of{u}"), 1)

                sum_in(0, 0)
                sum_in(0, 1)
                gain(0, 0)

                def step(n, u, left):
                    if left > 1:
                        sum_in(*nth(n, u + 2))
                    if left > 0:
                        gain(*nth(n, u + 1))
                    close(n, u)

                steps(v, step)

            @block.scalar
            def _(act):
                A = nc.scalar

                def square_in(n, u):
                    act.wait_ge(S(f"h2{u}"), n + 1)
                    act.wait_ge(S(f"xfT_ps{u}"), n)
                    A.activation(xf[u], hf[u], ACT.Square, accum_out=sc[u][0]).then_inc(S(f"ssA{u}"), 1)

                def sigmoid(n, u):
                    act.wait_ge(S(f"gate_ps{u}"), n + 1)
                    act.wait_ge(S(f"of{u}"), n)
                    A.activation(sgf[u], flat(4, 2), ACT.Sigmoid).then_inc(S(f"sgf{u}"), 1)

                def close(n, u, rows, R):
                    act.wait_ge(S(f"h3{u}"), n + 1)
                    act.wait_ge(S(f"out{u}"), 16 * n)
                    A.activation(of[u], sgf[u], ACT.Square, accum_out=sc[u][3]).then_inc(S(f"ssB{u}"), 1)
                    act.wait_ge(S(f"of{u}"), n + 1)
                    act.dma_start(O["y_prompt"][0, rows, :] if R == P else O["y_sample"][:, 0, :], of[u][0:R]).then_inc(S(f"out{u}"), 16)

                square_in(0, 0)
                square_in(0, 1)

                def step(n, u, left):
                    if left > 1:
                        square_in(*nth(n, u + 2))
                    sigmoid(n, u)
                    if left:
                        rows = bass.ds(act.snap((F * n + u) * P), P) if left == F else slice((NT - left) * P, (NT - left + 1) * P)
                        close(n, u, rows, P)
                    else:
                        close(n, u, None, DEC)

                steps(act, step)
                for u in range(F):
                    act.wait_ge(S(f"out{u}"), 16 * 3)

            @block.tensor
            def _(pe):
                def turn(n, u):
                    pe.wait_ge(S(f"xf{u}"), n + 1)
                    pe.wait_ge(*before("xfT", n, u))
                    pe.wait_ge(*before("pfT", n, u))
                    for k in range(KD):
                        mm = nc.tensor.transpose(flat(0, 2)[:, k * P:(k + 1) * P], xf[u].rearrange("p (c k) -> p k c", k=KD)[:, k, :], ident)
                    mm.then_inc(S(f"xfT_ps{u}"), 1)
                    for k in range(KE):
                        mm = nc.tensor.transpose(bank(2)[:, k * P:(k + 1) * P], pf[u][:, k * P:(k + 1) * P], ident)
                    mm.then_inc(S(f"pT_ps{u}"), 1)

                def products(n, u):
                    pe.wait_ge(S(f"xfT{u}"), n + 1)
                    pe.wait_ge(*before("sgf", n, u))
                    pe.wait_ge(L("wpg"), 16)
                    for m in range(2):
                        for k in range(KD):
                            mm = nc.tensor.matmul(bank(4 + m), xfT[u][:, k, :], wpg[:, k, m * 512:(m + 1) * 512], start=(k == 0), stop=(k == KD - 1))
                    mm.then_inc(S(f"gate_ps{u}"), 1)
                    pe.wait_ge(S(f"pfT{u}"), n + 1)
                    pe.wait_ge(*before("pg", n, u))
                    pe.wait_ge(L("wpp"), 16)
                    for m in range(2):
                        for k in range(KE):
                            mm = nc.tensor.matmul(bank(6 + m), pfT[u][:, k, :], wpp[:, k, m * 512:(m + 1) * 512], start=(k == 0), stop=(k == KE - 1))
                    mm.then_inc(S(f"pp_ps{u}"), 1)

                turn(0, 0)

                def step(n, u, left):
                    if left > 0:
                        turn(*nth(n, u + 1))
                    products(n, u)

                steps(pe, step)




_INS = ["x_prompt", "x_sample", "p_prompt", "p_sample", "cache_k", "cache_v", "state_conv", "state_S", "rel_bias",
        "norm_mix", "w_in", "att_sink", "conv_w", "dn_A_log", "dn_dt_bias", "dn_norm", "w_out", "norm_ffn",
        "w_router_group", "w_router_expert", "w_gate", "w_up", "w_down", "w_ple_proj", "w_ple_gate", "norm_ple",
        "norm_final"]
_OUTS = [("y_prompt", (1, SEQ, D)), ("y_sample", (DEC, 1, D)),
         ("cache_k_prompt", (1, 1, P, 2, HD)), ("cache_v_prompt", (1, 1, P, 2, HD)),
         ("state_conv_prompt", (1, 1, CW - 1, CCH)), ("state_S_prompt", (1, 1, NH, HD, HD)),
         ("cache_k_sample", (1, DEC, P, 2, HD)), ("cache_v_sample", (1, DEC, P, 2, HD)),
         ("state_conv_sample", (1, DEC, CW - 1, CCH)), ("state_S_sample", (1, DEC, NH, HD, HD))]


def kernel(**inputs):
    import concourse.bacc as _bacc
    from concourse.bass_utils import run_bass_kernel_spmd as _run

    nc = _bacc.Bacc("TRN2", target_bir_lowering=False, num_devices=1)
    arrays = {f"in_{name}": np.ascontiguousarray(inputs[name]) for name in _INS}
    arrays["in_cst"] = constants()
    ins = {name[3:]: nc.dram_tensor(name, a.shape, F32, kind="ExternalInput").ap() for name, a in arrays.items()}
    outs = {name: nc.dram_tensor(f"out_{name}", shape, F32, kind="ExternalOutput").ap() for name, shape in _OUTS}
    program(nc, ins, outs)
    r = _run(nc, [arrays], core_ids=[0])
    return tuple(r.results[0][f"out_{name}"] for name, _ in _OUTS)
```

```python
from contextlib import ExitStack

import numpy as np

import concourse.bass as bass
from concourse import mybir

F32 = mybir.dt.float32
F32R = mybir.dt.float32r
I32 = mybir.dt.int32
ALU = mybir.AluOpType
ACT = mybir.ActivationFunctionType
AX = mybir.AxisListType

P = 128
D = 1024
KD = D // P
SEQ = 1024
NT = SEQ // P
DEC = 8
TOK = SEQ + DEC
AH, HD, GQA = 8, 64, 4
NH = 8
CW = 4
CCH = 3 * NH * HD
FT_DN = CCH // P
A_Q, A_K, A_V, D_Q, D_B = 0, 512, 640, 768, 2304
IN_W = 2832
NG, EPG, NE, DE = 4, 8, 32, 256
PLE = 256
KE = DE // P
EPS = 1e-6
BIG = 1.0e30
XB = (2 * TOK - 1) // P
MAXB = NE + XB
DUMP = 1 << 20

C_ID, C_U, C_NEG, C_LV, C_HOT, C_HOTD, C_US, C_SWAP = 0, 128, 256, 384, 1280, 1664, 1792, 1920
C_TOK, C_GP, C_EP, C_EI, C_E128, C_THR, C_OV, C_FLAG, C_VAL, C_TT, C_END = \
    2048, 2049, 2053, 2061, 2093, 2125, 2133, 2149, 2157, 2166, 2175


def constants():
    c = np.zeros((P, C_END), np.float32)
    i = np.arange(P)
    row, col = i[:, None], i[None, :]
    c[:, C_ID:C_ID + P] = row == col
    c[:, C_U:C_U + P] = row <= col
    c[:, C_NEG:C_NEG + P] = np.where(col >= row, 0.0, -BIG)
    for n in range(7):
        s = 1 << n
        c[:, C_LV + n * P:C_LV + (n + 1) * P] = (row // (2 * s) == col // (2 * s)) & (row // s < col // s)
    c[:, C_US:C_US + P] = row < col
    c[:, C_SWAP:C_SWAP + P] = row == (col + 64) % P

    def bucket(d):
        d = np.maximum(d, 0)
        ratio = np.log(np.maximum(d, 1).astype(np.float32) / 16) / np.log(8.0)
        return np.where(d < 16, d, np.minimum(16 + (ratio * 16).astype(np.int32), 31))

    m = np.arange(3 * P)
    dist = 2 * P - 1 - m
    b = np.where((dist >= 0) & (dist < P), bucket(dist), 32)
    c[b, C_HOT + m] = 1.0
    dist = np.where(i == 0, 0, P - i)
    c[bucket(dist), C_HOTD + i] = 1.0
    c[:, C_TOK] = i
    c[:, C_GP:C_GP + NG] = NG - np.arange(NG)
    c[:, C_EP:C_EP + EPG] = EPG - np.arange(EPG)
    c[:, C_EI:C_EI + NE] = np.arange(NE)
    c[:, C_E128:C_E128 + NE] = np.arange(NE) * P
    c[:, C_THR:C_THR + 8] = (np.arange(8) + 1) * P
    c[:, C_OV:C_OV + XB] = np.arange(XB)
    c[:, C_FLAG] = -BIG
    c[:, C_VAL:C_VAL + NT] = 1.0
    c[:DEC, C_VAL + NT] = 1.0
    c[:, C_TT:C_TT + NT + 1] = i[:, None] + P * np.arange(NT + 1)
    return c


class Layout:

    def __init__(self, tensor):
        self.tensor, self.at = tensor, 0

    def take(self, *shape):
        n = 1
        for s in shape:
            n *= s
        view = self.tensor[:, self.at:self.at + n]
        self.at += n
        assert self.at <= self.tensor.shape[1], self.at
        if len(shape) == 2:
            return view.rearrange("p (a b) -> p a b", b=shape[1])
        if len(shape) == 3:
            return view.rearrange("p (a b c) -> p a b c", b=shape[1], c=shape[2])
        return view


def bc(ap, n):
    return ap.unsqueeze(2).to_broadcast([ap.shape[0], ap.shape[1], n])


def bm(ap, n):
    return ap.unsqueeze(1).to_broadcast([ap.shape[0], n, ap.shape[1]])


def even_odd(x):
    return x.rearrange("p (a f) -> p a f", a=2)


def program(nc, I, O, dbg=None):
    es = ExitStack()
    sems, lasting, stages = {}, {}, []

    def S(name):
        if name not in sems:
            sems[name] = nc.alloc_semaphore(name=f"{name}_{len(stages)}")
        return sems[name]

    def L(name):
        if name not in lasting:
            lasting[name] = nc.alloc_semaphore(name=name)
        return lasting[name]

    def stage_ends():
        nc.clear_and_free_semaphores(list(sems.values()))
        sems.clear()
        stages.append(None)
        nc.all_engine_barrier()

    def settle(eng):
        eng.sem_inc(S(f"settled_{eng.engine}".replace(".", "_")), 1)

    def dram(name, *shape, dt=F32):
        return nc.dram_tensor(name, shape, dt).ap()

    with es:
        def room(name, words, stack, dt=F32):
            return Layout(stack.enter_context(nc.sbuf_tensor(name, [P, words], dt)))

        WORDS, ALL, MIX = 50400, 3352, 7936
        mem = room("lasting", ALL, es)
        psum = es.enter_context(nc.psum_tensor("psum", [P, 8, 512], F32))

        y_d = dram("conv_out_d", P, FT_DN, SEQ)
        ydec_d = dram("conv_dec_d", 3, DEC, NH * HD)
        sz_d = dram("gate_d", TOK, NH * HD)
        h_d = dram("h_d", TOK, D)
        xs_d = dram("xs_d", TOK, D)
        ye_d = dram("ye_d", 2 * TOK, D)
        tab_d = dram("tab_d", MAXB * P, 4, dt=I32)
        bias_d = dram("bias_d", AH, P, 3 * P)
        gbd_d = dram("gbd_d", 2, DEC, NH)

        cst = mem.take(C_END)
        ident = cst[:, C_ID:C_ID + P]
        small = mem.take(512)
        at = [0]

        def col(n):
            at[0] += n
            assert at[0] <= 512
            return small[:, at[0] - n:at[0]]

        g_mix, g_ffn, g_ple = col(KD), col(KD), col(KD)
        half = col(1)
        normB, sinkB, sinkC, lg_pad = col(HD), col(AH), col(1), col(1)
        ones = mem.take(P)
        lg = mem.take(NT + 1, NG + NE)
        tabI = mem.take(4, MAXB).bitcast(I32)
        blk = mem.take(XB + 1).bitcast(I32)
        until_mixed = ExitStack()
        mem = room("until_mixed", MIX, until_mixed)
        gb = mem.take(NT + 1, 16)
        q_room = mem.take(4 * TOK)
        qf = q_room.rearrange("p (f t) -> p f t", f=4)
        kf = mem.take(P + TOK)
        ksw = mem.take(P + TOK)
        vt = mem.take(NT + 2, P)
        mixD = mem.take(KD, DEC)

        def bank(i, n=1):
            return psum[:, i, :] if n == 1 else psum[:, i:i + n, :]

        TB = TOK // 3

        def thirds(u):
            return psum[:, 3 * u:3 * u + 3, 0:TB]

        def flat(i, n):
            return psum[:, i:i + n, :].rearrange("p a b -> p (a b)")

        own = ExitStack()
        SPLIT = 2 * KD * TOK + 4 * KD * P
        parts = room("split_parts", SPLIT, own, F32R)
        hnH, hnL = parts.take(KD, TOK), parts.take(KD, TOK)
        wfH, wfL = parts.take(2, KD, P), parts.take(2, KD, P)
        mem = room("project", WORDS - ALL - MIX - SPLIT, own)
        wf = mem.take(2, KD, P)
        XP = CW - 1 + SEQ + DEC * CW
        tails = mem.take(FT_DN, 27)
        stT = mem.take(FT_DN, 24)
        cwT = mem.take(FT_DN, CW)
        strow = mem.take(CCH)
        cwrow = mem.take(P)
        szt = mem.take(2, 512)
        ydT = mem.take(FT_DN, DEC)
        xp = mem.take(2, XP + 1)
        xin = q_room[:, 0:2 * D].rearrange("p (u d) -> p u d", u=2)
        xs = q_room[:, 2 * D:4 * D].rearrange("p (u d) -> p u d", u=2)
        shared = mem.at
        xT = mem.take(2, KD, P)
        wtok = mem.take(KD, 144 + 512)
        mem.at = shared
        yc = mem.take(2, XP + 1)
        ys = mem.take(2, XP + 1)
        ydrow = mem.take(CCH)
        dtN, alN, dtB, alB = (col(NH) for _ in range(4))
        small_a, small_b, small_c = (col((NT + 1) * NH) for _ in range(3))
        rr = [(col(1), col(1), col(1)) for _ in range(2)]
        w_in = I["w_in"][0].rearrange("(p k) n -> p k n", k=KD)
        NV = XP - CW + 1

        with nc.Block() as block:
            @block.sync
            def _(sp):
                sp.dma_start(cst, I["cst"]).then_inc(S("cst"), 16)
                for v, name in ((g_mix, "norm_mix"), (g_ffn, "norm_ffn"), (g_ple, "norm_ple")):
                    sp.dma_start(v, I[name][0].rearrange("(p k) -> p k", k=KD)).then_inc(S("gains"), 16)
                sp.dma_start(dtN, I["dn_dt_bias"][0].partition_broadcast(P)).then_inc(S("gains"), 16)
                sp.dma_start(alN, I["dn_A_log"][0].partition_broadcast(P)).then_inc(S("gains"), 16)
                sp.dma_start(normB, I["dn_norm"][0].partition_broadcast(P)).then_inc(S("gains"), 16)

                def load_x(n, u, t):
                    sp.wait_ge(S(f"xs{u}"), n)
                    if t is None:
                        sp.dma_start(xin[0:DEC, u, :], I["x_sample"][:, 0, :]).then_inc(S(f"x{u}"), 16)
                    else:
                        sp.dma_start(xin[:, u, :], I["x_prompt"][0, bass.ds(t * P, P), :]).then_inc(S(f"x{u}"), 16)

                load_x(0, 0, 0)
                load_x(0, 1, 1)
                sp.dma_start(wtok[:, :, 0:P], w_in[:, :, A_V:A_V + P]).then_inc(S("wtok"), 16)
                sp.dma_start(wtok[:, :, P:], w_in[:, :, D_B:IN_W]).then_inc(S("wtok"), 16)
                sp.dma_start(strow[0:24, :], I["state_conv"][0].rearrange("b j c -> (b j) c")).then_inc(S("small"), 16)
                sp.dma_start(cwrow[0:48, :], I["conv_w"][0].rearrange("j (f c) -> (j f) c", c=P)).then_inc(S("small"), 16)
                with sp.Fori(1, 4) as n:
                    for u in range(2):
                        load_x(n, u, 2 * n + u)
                load_x(4, 0, None)

                def load_w(n, u, c0):
                    sp.wait_ge(S(f"wfL{u}"), n)
                    sp.dma_start(wf[:, u], w_in[:, :, bass.ds(c0, P)]).then_inc(S(f"wf{u}"), 16)

                for u in range(2):
                    load_w(0, u, D_Q + u * P)
                with sp.Fori(1, FT_DN // 2) as n:
                    for u in range(2):
                        load_w(n, u, D_Q + (2 * n + u) * P)
                for a in range(5):
                    load_w(6 + a // 2, a % 2, a * P)

                sp.wait_ge(S("tok_out0"), 5)
                sp.wait_ge(S("tok_out1"), 4)
                sp.dma_start(O["cache_v_prompt"][0, 0].rearrange("t h d -> t (h d)"), vt[:, NT, :]).then_inc(S("o1"), 16)
                sp.dma_start(O["cache_v_sample"][0, :, P - 1].rearrange("b h d -> b (h d)"), vt[0:DEC, NT + 1, :]).then_inc(S("o1"), 16)
                for new, old in (("cache_k_sample", "cache_k"), ("cache_v_sample", "cache_v")):
                    sp.dma_start(O[new][0, :, 0:P - 1].rearrange("b t h d -> b t (h d)"),
                                 I[old][0, :, 1:P].rearrange("b t h d -> b t (h d)")).then_inc(S("o1"), 16)
                sp.wait_ge(S("tails_row"), 1)
                sp.dma_start(O["state_conv_prompt"][0, 0], strow[0:3, :]).then_inc(S("o1"), 16)
                sp.dma_start(O["state_conv_sample"][0].rearrange("b j c -> (b j) c"), strow[3:27, :]).then_inc(S("o1"), 16)
                sp.wait_ge(S("ydrow"), 1)
                sp.dma_start(ydec_d.rearrange("i b c -> b i c"), ydrow[0:DEC, :].rearrange("b (i c) -> b i c", i=3)).then_inc(S("o1"), 16)
                sp.wait_ge(S("krow"), 1)
                sp.dma_start(O["cache_k_prompt"][0, 0].rearrange("t h d -> t (h d)"), cwrow).then_inc(S("o1"), 16)
                sp.wait_ge(S("krow"), 2)
                sp.dma_start(O["cache_k_sample"][0, :, P - 1].rearrange("b h d -> b (h d)"), yc[0:DEC, 0, 0:P]).then_inc(S("o1"), 16)
                sp.wait_ge(S("o1"), 16 * 9)

            @block.gpsimd
            def _(g):
                g.memset(half, -0.5).then_inc(S("half"), 1)
                g.memset(ones, 1.0).then_inc(S("ones"), 1)
                g.memset(kf[:, 0:P], 0.0).then_inc(S("zeros"), 1)
                g.memset(ksw[:, 0:P], 0.0).then_inc(S("zeros"), 1)
                g.memset(vt[:, 0, :], 0.0).then_inc(S("zeros"), 1)
                g.memset(vt[:, NT + 1, :], 0.0).then_inc(S("zeros"), 1)
                g.memset(gb[:, NT, :], 0.0).then_inc(S("zeros"), 1)
                g.memset(lg[:, NT, :], 0.0).then_inc(S("zeros"), 1)
                g.memset(xp[:, :, 0:CW - 1], 0.0).then_inc(S("zeros"), 1)
                g.wait_ge(S("half"), 1)

                def rstd(n, u):
                    g.wait_ge(S(f"var{u}"), n + 1)
                    g.tensor_tensor(rr[u][2], rr[u][1], half, ALU.pow).then_inc(S(f"rstd{u}"), 1)

                with g.Fori(0, 4) as n:
                    for u in range(2):
                        rstd(n, u)
                rstd(4, 0)

            @block.vector
            def _(v):
                def scale(n, u):
                    v.wait_ge(S(f"ss{u}"), n + 1)
                    nc.vector.tensor_scalar(rr[u][1], rr[u][0], 1.0 / D, EPS, ALU.mult, ALU.add).then_inc(S(f"var{u}"), 1)
                    v.wait_ge(S(f"rstd{u}"), n + 1)
                    nc.vector.tensor_scalar(xs[:, u, :], xin[:, u, :], rr[u][2], None, ALU.mult).then_inc(S(f"xs{u}"), 1)

                def gain(n, u):
                    v.wait_ge(S(f"xT_psum{u}"), n + 1)
                    v.wait_ge(S(f"tok_psum{u}"), n)
                    v.wait_ge(S(f"hnL{u}"), n)
                    nc.vector.tensor_tensor(xT[:, u], flat(2 * u, 2).rearrange("p (k c) -> p k c", c=P),
                                            bc(g_mix, P), ALU.mult).then_inc(S(f"xT{u}"), 1)

                def low(n, u, cols, m):
                    v.wait_ge(S(f"hnH{u}"), n + 1)
                    nc.vector.tensor_tensor(hnL[:, :, cols], xT[:, u, :, 0:m], hnH[:, :, cols].bitcast(F32), ALU.subtract).then_inc(S(f"hnL{u}"), 1)

                def weights_low(n, u):
                    v.wait_ge(S(f"wfH{u}"), n + 1)
                    nc.vector.tensor_tensor(wfL[:, u], wf[:, u], wfH[:, u].bitcast(F32), ALU.subtract).then_inc(S(f"wfL{u}"), 1)

                v.wait_ge(S("gains"), 96)
                nc.vector.tensor_copy(even_odd(dtB), dtN.rearrange("p (f a) -> p a f", a=2)).then_inc(S("dtB"), 1)
                def pair(n, cols0, cols1):
                    scale(n, 1)
                    gain(n, 0)
                    scale(n + 1, 0)
                    gain(n, 1)
                    low(n, 0, bass.ds(cols0, P), P)
                    low(n, 1, bass.ds(cols1, P), P)

                scale(0, 0)
                pair(0, 0, P)
                with v.Fori(1, 4) as n:
                    pair(n, v.snap(2 * n * P), v.snap((2 * n + 1) * P))
                gain(4, 0)
                low(4, 0, slice(SEQ, TOK), DEC)
                for u in range(2):
                    weights_low(0, u)

                v.wait_ge(S("st_psum"), 1)
                nc.vector.tensor_copy(stT, bank(6)[:, 0:24 * FT_DN].rearrange("p (f c) -> p f c", c=24)).then_inc(S("stT"), 1)
                nc.vector.tensor_copy(cwT, bank(7)[:, 0:48].rearrange("p (j f) -> p f j", f=FT_DN)).then_inc(S("stT"), 1)
                v.wait_ge(S("stT"), 2)

                def conv(n, u, ft):
                    dec = xp[:, u, CW - 1 + SEQ:XP].rearrange("p (b j) -> p b j", j=CW)
                    v.wait_ge(S(f"tails{u}"), n)
                    nc.vector.tensor_copy(dec[:, :, 0:CW - 1], stT[:, ft, :].rearrange("p (b j) -> p b j", j=CW - 1)).then_inc(S(f"xp_dec{u}"), 1)
                    v.wait_ge(S(f"xp_dec{u}"), n + 1)
                    v.wait_ge(S(f"xp{u}"), n + 1)
                    v.wait_ge(S(f"silu{u}"), n)
                    nc.vector.tensor_scalar(yc[:, u, 0:NV], xp[:, u, 0:NV], cwT[:, ft, 0:1], None,
                                            ALU.mult).then_inc(S(f"conv{u}"), 1)
                    for j in range(1, CW):
                        v.wait_ge(S(f"conv{u}"), CW * n + j)
                        nc.vector.scalar_tensor_tensor(yc[:, u, 0:NV], xp[:, u, j:j + NV], cwT[:, ft, j:j + 1],
                                                       yc[:, u, 0:NV], ALU.mult, ALU.add).then_inc(S(f"conv{u}"), 1)
                    nc.vector.tensor_copy(tails[:, ft, 0:3], xp[:, u, SEQ:SEQ + 3])
                    nc.vector.tensor_copy(tails[:, ft, 3:27].rearrange("p (b j) -> p b j", j=3),
                                          dec[:, :, 1:CW]).then_inc(S(f"tails{u}"), 1)

                v.wait_ge(S("zeros"), 7)
                def conv_pair(n):
                    for u in range(2):
                        conv(n, u, 2 * n + u)
                        weights_low(n + 1, u)

                conv_pair(0)
                with v.Fori(1, FT_DN // 2) as n:
                    conv_pair(n)
                for a in range(3):
                    weights_low(7 + a // 2, a % 2)
                v.wait_ge(S("tails_psum"), 1)
                nc.vector.tensor_copy(strow[0:27, :], flat(3, 3)[0:27, :]).then_inc(S("tails_row"), 1)
                v.wait_ge(S("yd_psum"), 1)
                nc.vector.tensor_copy(ydrow[0:DEC, :], flat(3, 3)[0:DEC, :]).then_inc(S("ydrow"), 1)
                v.wait_ge(S("ksw_psum"), 1)
                nc.vector.tensor_copy(ksw[:, P:].rearrange("p (b c) -> p b c", c=TB), thirds(0)).then_inc(S("ksw"), 1)
                v.wait_ge(S("krow_psum"), 1)
                nc.vector.tensor_copy(cwrow, bank(6)[:, 0:P]).then_inc(S("krow"), 1)
                nc.vector.tensor_copy(yc[0:DEC, 0, 0:P], bank(6)[0:DEC, P:2 * P]).then_inc(S("krow"), 1)

                v.wait_ge(S("sig"), 1)
                nc.vector.tensor_scalar(small_a, small_a, 1.0, None, ALU.add).then_inc(S("gbc"), 1)
                v.wait_ge(S("gbc"), 1)
                nc.vector.reciprocal(gb[:, :, 0:NH], small_a.rearrange("p (t h) -> p t h", h=NH)).then_inc(S("gbc"), 1)
                da = gb[:, :, NH:2 * NH]
                v.wait_ge(S("dtB"), 1)
                nc.vector.tensor_tensor(da, da, bm(dtB, NT + 1), ALU.add).then_inc(S("gbc"), 1)
                v.wait_ge(S("gbc"), 3)
                nc.vector.tensor_scalar(small_b.rearrange("p (t h) -> p t h", h=NH), da, 0.0, None, ALU.max).then_inc(S("gbc"), 1)
                v.wait_ge(S("gbc"), 4)
                nc.vector.scalar_tensor_tensor(small_c.rearrange("p (t h) -> p t h", h=NH), small_b.rearrange("p (t h) -> p t h", h=NH), -2.0, da,
                                               ALU.mult, ALU.add).then_inc(S("negabs"), 1)
                v.wait_ge(S("sp"), 1)
                nc.vector.tensor_tensor(small_b, small_b, small_c, ALU.add).then_inc(S("gbc"), 1)
                v.wait_ge(S("gbc"), 5)
                nc.vector.scalar_tensor_tensor(da, small_b.rearrange("p (t h) -> p t h", h=NH), -1.0, bm(alB, NT + 1),
                                               ALU.mult, ALU.mult).then_inc(S("gbc"), 1)

            @block.scalar
            def _(act):
                def square(n, u):
                    act.wait_ge(S(f"x{u}"), 16 * n + 16)
                    act.wait_ge(S(f"xT_psum{u}"), n)
                    nc.scalar.activation(xs[:, u, :], xin[:, u, :], ACT.Square, accum_out=rr[u][0]).then_inc(S(f"ss{u}"), 1)

                def high(n, u, cols, m):
                    act.wait_ge(S(f"xT{u}"), n + 1)
                    nc.scalar.activation(hnH[:, :, cols], xT[:, u, :, 0:m], ACT.Copy).then_inc(S(f"hnH{u}"), 1)

                def weights_high(n, u):
                    act.wait_ge(S(f"wf{u}"), 16 * n + 16)
                    act.wait_ge(S(f"f_psum{u}"), n)
                    nc.scalar.activation(wfH[:, u], wf[:, u], ACT.Copy).then_inc(S(f"wfH{u}"), 1)

                def keep_tok(n, u, t, R):
                    act.wait_ge(S(f"tok_psum{u}"), n + 1)
                    act.wait_ge(S(f"sz_out{u}"), 16 * n)
                    nc.scalar.activation(vt[0:R, t + 1, :], bank(4 + 2 * u)[0:R, 0:P], ACT.Copy)
                    nc.scalar.activation(gb[0:R, t, :].rearrange("p (i a f) -> p i a f", i=2, a=2),
                                         bank(4 + 2 * u)[0:R, P:P + 16].rearrange("p (i f a) -> p i a f", i=2, a=2), ACT.Copy)
                    nc.scalar.activation(szt[0:R, u, :], bank(5 + 2 * u)[0:R, :], ACT.Silu).then_inc(S(f"tok_out{u}"), 1)
                    act.wait_ge(S(f"tok_out{u}"), n + 1)
                    dst = sz_d[SEQ:TOK, :] if R == DEC else sz_d[bass.ds(t * P, P), :]
                    act.dma_start(dst, szt[0:R, u, :]).then_inc(S(f"sz_out{u}"), 16)

                act.wait_ge(S("zeros"), 7)
                square(0, 0)
                square(0, 1)

                def pair(n, last=False):
                    high(n, 0, bass.ds(2 * n * P, P), P)
                    square(n + 1, 0)
                    high(n, 1, bass.ds((2 * n + 1) * P, P), P)
                    keep_tok(n, 0, 2 * n, P)
                    if not last:
                        square(n + 1, 1)
                    keep_tok(n, 1, 2 * n + 1, P)

                pair(0)
                with act.Fori(1, 3) as n:
                    pair(n)
                pair(3, last=True)
                high(4, 0, slice(SEQ, TOK), DEC)
                for u in range(2):
                    weights_high(0, u)
                keep_tok(4, 0, NT, DEC)

                def conv_in(n, u):
                    act.wait_ge(S(f"f_psum{u}"), n + 1)
                    act.wait_ge(S(f"tails{u}"), n)
                    nc.scalar.activation(xp[:, u, CW - 1:CW - 1 + 2 * TB].rearrange("p (b c) -> p b c", c=TB), thirds(u)[:, 0:2], ACT.Copy)
                    nc.scalar.activation(xp[:, u, CW - 1 + 2 * TB:CW - 1 + SEQ], thirds(u)[:, 2, 0:TB - DEC], ACT.Copy)
                    dec = xp[:, u, CW - 1 + SEQ:XP].rearrange("p (b j) -> p b j", j=CW)
                    nc.scalar.activation(dec[:, :, CW - 1], thirds(u)[:, 2, TB - DEC:TB], ACT.Copy).then_inc(S(f"xp{u}"), 1)

                def silu(n, u, ft):
                    act.wait_ge(S(f"conv{u}"), CW * n + CW)
                    act.wait_ge(S(f"y_out{u}"), 16 * n)
                    nc.scalar.activation(ys[:, u, 0:NV], yc[:, u, 0:NV], ACT.Silu).then_inc(S(f"silu{u}"), 1)
                    act.wait_ge(S(f"silu{u}"), n + 1)
                    act.dma_start(y_d[:, ft, :], ys[:, u, 0:SEQ]).then_inc(S(f"y_out{u}"), 16)
                    nc.scalar.activation(ydT[:, ft, :],
                                         ys[:, u, CW - 1 + SEQ:CW - 1 + SEQ + DEC * CW].rearrange("p (b j) -> p b j", j=CW)[:, :, 0],
                                         ACT.Copy).then_inc(S("ydT"), 1)

                def conv_pair(n):
                    for u in range(2):
                        conv_in(n, u)
                        weights_high(n + 1, u)
                        silu(n, u, 2 * n + u)

                conv_pair(0)
                with act.Fori(1, FT_DN // 2) as n:
                    conv_pair(n)
                for a in range(5):
                    n, u = 6 + a // 2, a % 2
                    act.wait_ge(S(f"f_psum{u}"), n + 1)
                    dst = qf[:, a, :] if a < 4 else kf[:, P:]
                    nc.scalar.activation(dst.rearrange("p (b c) -> p b c", c=TB), thirds(u), ACT.Copy).then_inc(S(f"att_out{u}"), 1)
                    if a < 3:
                        weights_high(n + 1, u)
                nc.scalar.activation(small_a.rearrange("p (t h) -> p t h", h=NH), gb[:, :, 0:NH], ACT.Exp, scale=-1.0).then_inc(S("sig"), 1)
                act.wait_ge(S("gains"), 96)
                nc.scalar.activation(even_odd(alB), alN.rearrange("p (f a) -> p a f", a=2), ACT.Exp)
                act.wait_ge(S("negabs"), 1)
                nc.scalar.activation(small_c, small_c, ACT.Exp).then_inc(S("spc"), 1)
                act.wait_ge(S("spc"), 1)
                nc.scalar.activation(small_c, small_c, ACT.Ln, bias=1.0).then_inc(S("sp"), 1)
                act.wait_ge(S("sz_out0"), 80)
                act.wait_ge(S("sz_out1"), 64)
                act.wait_ge(S("y_out0"), 96)
                act.wait_ge(S("y_out1"), 96)

            @block.tensor
            def _(pe):
                def turn(n, u):
                    pe.wait_ge(S(f"xs{u}"), n + 1)
                    pe.wait_ge(S(f"xT{u}"), n)
                    for k in range(KD):
                        mm = nc.tensor.transpose(flat(2 * u, 2)[:, k * P:(k + 1) * P],
                                                 xs[:, u, :].rearrange("p (c k) -> p k c", k=KD)[:, k, :], ident)
                    mm.then_inc(S(f"xT_psum{u}"), 1)

                def project(n, u):
                    pe.wait_ge(S(f"xT{u}"), n + 1)
                    pe.wait_ge(S(f"tok_out{u}"), n)
                    for k in range(KD):
                        nc.tensor.matmul(bank(4 + 2 * u)[:, 0:144], xT[:, u, k, :], wtok[:, k, 0:144], start=(k == 0), stop=(k == KD - 1))
                    for k in range(KD):
                        mm = nc.tensor.matmul(bank(5 + 2 * u), xT[:, u, k, :], wtok[:, k, 144:], start=(k == 0), stop=(k == KD - 1))
                    mm.then_inc(S(f"tok_psum{u}"), 1)

                pe.wait_ge(S("cst"), 16)
                turn(0, 0)
                pe.wait_ge(S("wtok"), 32)
                def pair(n):
                    turn(n, 1)
                    project(n, 0)
                    turn(n + 1, 0)
                    project(n, 1)

                pair(0)
                with pe.Fori(1, 4) as n:
                    pair(n)
                project(4, 0)
                pe.wait_ge(S("small"), 32)
                pe.wait_ge(S("tok_out1"), 4)
                for f in range(FT_DN):
                    nc.tensor.transpose(bank(6)[:, 24 * f:24 * f + 24], strow[0:24, f * P:(f + 1) * P], ident[0:24, 0:24])
                nc.tensor.transpose(bank(7)[:, 0:48], cwrow[0:48, :], ident[0:48, 0:48]).then_inc(S("st_psum"), 1)
                pe.wait_ge(S("hnL0"), 5)
                pe.wait_ge(S("hnL1"), 4)
                pe.wait_ge(S("tok_out0"), 5)

                def features(n, u, att=False):
                    pe.wait_ge(S(f"wfL{u}"), n + 1)
                    if not att or n == 6:
                        pe.wait_ge(S(f"xp{u}"), n if not att else 6)
                    else:
                        pe.wait_ge(S(f"att_out{u}"), n - 6)
                    for b in range(3):
                        for i, (w, x) in enumerate(((wfH, hnH), (wfH, hnL), (wfL, hnH))):
                            for k in range(KD):
                                mm = nc.tensor.matmul(thirds(u)[:, b], w[:, u, k, :], x[:, k, b * TB:(b + 1) * TB],
                                                      start=(i == 0 and k == 0), stop=(i == 2 and k == KD - 1))
                    mm.then_inc(S(f"f_psum{u}"), 1)

                for u in range(2):
                    features(0, u)
                with pe.Fori(1, FT_DN // 2) as n:
                    for u in range(2):
                        features(n, u)
                for a in range(5):
                    features(6 + a // 2, a % 2, True)
                pe.wait_ge(S("att_out1"), 2)
                pe.wait_ge(S("tails0"), 6)
                pe.wait_ge(S("tails1"), 6)
                for f in range(FT_DN):
                    mm = nc.tensor.transpose(flat(3, 3)[0:27, f * P:(f + 1) * P], tails[:, f, :], ident)
                mm.then_inc(S("tails_psum"), 1)
                pe.wait_ge(S("tails_row"), 1)
                pe.wait_ge(S("ydT"), FT_DN)
                for f in range(FT_DN):
                    mm = nc.tensor.transpose(flat(3, 3)[0:DEC, f * P:(f + 1) * P], ydT[:, f, :], ident)
                mm.then_inc(S("yd_psum"), 1)
                pe.wait_ge(S("att_out0"), 3)
                swap = cst[:, C_SWAP:C_SWAP + P]
                for b in range(3):
                    mm = nc.tensor.matmul(thirds(0)[:, b], swap, kf[:, P + b * TB:P + (b + 1) * TB], start=True, stop=True)
                mm.then_inc(S("ksw_psum"), 1)
                pe.wait_ge(S("stT"), 2)
                nc.tensor.transpose(bank(6)[:, 0:P], kf[:, SEQ:SEQ + P], ident)
                nc.tensor.transpose(bank(6)[0:DEC, P:2 * P], kf[:, P + SEQ:P + TOK], ident).then_inc(S("krow_psum"), 1)

        stage_ends()
        own.close()
        mem = room("decode_and_mix", WORDS - ALL - MIX, until_mixed)
        biasS = mem.take(AH, 2 * P)
        wout = mem.take(KD, D)
        wr = mem.take(KD, NG + NE)
        mixer = mem.at
        kc, vc, kcT = mem.take(DEC, P), mem.take(DEC, P), mem.take(DEC, P)
        sinkN = mem.take(AH)
        relb, relw = mem.take(AH), mem.take(AH, P)
        toep = mem.take(AH, 3 * P)
        qblk = mem.take(DEC, AH)
        biasD = mem.take(P)
        sD, pTD = mem.take(DEC, P), mem.take(DEC, AH)
        oD = mem.take(DEC, AH)
        mD, eD, dD, rD = (mem.take(DEC) for _ in range(4))
        HH = HD // 2
        S0 = mem.take(HH, HD)
        prod, prodq = mem.take(HD, HH), mem.take(HD, HH)
        qkv = mem.take(3, HD)
        qkh = mem.take(2, HH)
        szd = mem.take(HD)
        sqd = mem.take(3, HD)
        kqS = mem.take(2, HD)
        o2 = mem.take(2, HD)
        kS, vn1, o1 = (mem.take(HD) for _ in range(3))
        bgD = mem.take(2)
        bD, gD = bgD[:, 0:1], bgD[:, 1:2]
        egD, qkD, n1, m1, r1 = (mem.take(1) for _ in range(5))
        n2, m2, r2 = (mem.take(2) for _ in range(3))
        PR = DEC * NH

        def state_rows(x, a):
            return x[0].rearrange("b h (a d) e -> a (b h) d e", a=2)[a]

        with nc.Block() as block:
            @block.sync
            def _(sp):
                for i in range(2):
                    for a in range(2):
                        sp.dma_start(gbd_d[i, :, a::2], gb[0:DEC, NT, NH * i + 4 * a:NH * i + 4 * a + 4], allow_slow_non_contiguous=True).then_inc(S("gbd"), 16)
                for a in range(2):
                    sp.dma_start(qkv[a * PR:(a + 1) * PR], ydec_d.rearrange("i b (h d) -> (b h) i d", d=HD)).then_inc(S("qkv"), 16)
                for a in range(2):
                    sp.dma_start(S0[a * PR:(a + 1) * PR], state_rows(I["state_S"], a)).then_inc(S("S0"), 16)
                sp.wait_ge(S("gbd"), 64)
                for a in range(2):
                    sp.dma_start(bgD[a * PR:(a + 1) * PR].unsqueeze(2), gbd_d.rearrange("i b (h o) -> (b h) i o", o=1), allow_slow_non_contiguous=True).then_inc(S("bg"), 16)
                sp.dma_start(szd[0:PR], sz_d[SEQ:TOK].rearrange("b (h d) -> (b h) d", d=HD)).then_inc(S("szd"), 16)
                sp.dma_start(wout, I["w_out"][0].rearrange("(k p) n -> p k n", p=P)).then_inc(L("wout"), 16)
                sp.dma_start(wr[:, :, 0:NG], I["w_router_group"][0].rearrange("(p k) n -> p k n", k=KD)).then_inc(L("wr"), 16)
                sp.dma_start(wr[:, :, NG:], I["w_router_expert"][0].rearrange("(p k) n -> p k n", k=KD)).then_inc(L("wr"), 16)
                for i in range(2):
                    sp.wait_ge(S("toep"), 4 * (i + 1))
                    sp.dma_start(bias_d[4 * i:4 * i + 4].rearrange("h p m -> p h m"), toep[:, 4 * i:4 * i + 4, :]).then_inc(S("toep_out"), 16)
                sp.wait_ge(S("toep_out"), 32)
                skew = bias_d.rearrange("h p m -> h (p m)")[:, P - 1:P - 1 + P * (3 * P - 1)].rearrange("h (p m) -> p h m", m=3 * P - 1)
                for g in range(2):
                    for a in range(2):
                        sp.dma_start(biasS[:, 4 * g + 2 * a:4 * g + 2 * a + 2], skew[:, 4 * g + a:4 * g + a + 3:2, 0:2 * P]).then_inc(S("biasS"), 16)
                sp.wait_ge(S("S1"), 1)
                for a in range(2):
                    sp.dma_start(state_rows(O["state_S_sample"], a), S0[a * PR:(a + 1) * PR]).then_inc(S("states_out"), 16)
                sp.wait_ge(S("biasS"), 64)
                sp.wait_ge(S("states_out"), 32)

            @block.gpsimd
            def _(g):
                g.memset(qblk, 0.0).then_inc(S("qblk0"), 1)
                g.wait_ge(S("n2"), 1)
                g.tensor_tensor(r2, m2, half.to_broadcast([P, 2]), ALU.pow).then_inc(S("r2"), 1)
                g.wait_ge(S("qk_n"), 1)
                g.wait_ge(S("S0"), 32)
                g.tensor_tensor(prodq, S0.rearrange("p d e -> p e d"), bm(qkh[:, 0], HD), ALU.mult).then_inc(S("qS"), 1)
                g.wait_ge(S("n1"), 1)
                g.tensor_tensor(r1[0:PR], m1[0:PR], half[0:PR], ALU.pow).then_inc(S("r1"), 1)

            @block.scalar
            def _(act):
                act.dma_start(kc, I["cache_k"][0].rearrange("b t h d -> t b (h d)")).then_inc(S("kc"), 16)
                act.dma_start(relb[0:32, :], I["rel_bias"]).then_inc(S("d_rel"), 16)
                act.dma_start(vc[1:P], I["cache_v"][0, :, 1:P].rearrange("b t h d -> t b (h d)")).then_inc(S("vc"), 16)
                act.dma_start(vc[0:1], O["cache_v_sample"][0, :, P - 1].rearrange("b h d -> b (h d)").unsqueeze(0)).then_inc(S("vc"), 16)
                act.dma_start(sinkN, I["att_sink"][0].partition_broadcast(P)).then_inc(S("sinks"), 16)
                act.dma_start(sinkC[0:AH], I["att_sink"][0].unsqueeze(1)).then_inc(S("sinks"), 16)
                act.wait_ge(S("kcT_ps"), 1)
                nc.scalar.activation(kcT[:, :, 1:], flat(2, 2).rearrange("p (b j) -> p b j", j=P)[:, :, 1:], ACT.Copy).then_inc(S("kcT"), 1)
                for h in range(AH):
                    act.wait_ge(S("toep_ps"), h + 1)
                    nc.scalar.activation(toep[:, h, :], bank(h % 2)[:, 0:3 * P], ACT.Copy).then_inc(S("toep"), 1)
                    if h == 3:
                        act.wait_ge(S("bg"), 32)
                        nc.scalar.activation(egD, gD, ACT.Exp).then_inc(S("egD"), 1)
                act.wait_ge(S("xD"), 1)
                nc.scalar.activation(sD[0:AH], sD[0:AH], ACT.Exp)
                nc.scalar.activation(eD[0:AH], eD[0:AH], ACT.Exp).then_inc(S("eD"), 1)

            @block.tensor
            def _(pe):
                def toeplitz(h):
                    if h > 1:
                        pe.wait_ge(S("toep"), h - 1)
                    nc.tensor.matmul(bank(h % 2)[:, 0:3 * P], relw[0:33, h, :], cst[0:33, C_HOT:C_HOT + 3 * P], start=True, stop=True).then_inc(S("toep_ps"), 1)

                nc.tensor.matmul(bank(4)[:, P:P + 4 * DEC], cst[:, C_SWAP:C_SWAP + P], qf[:, :, SEQ:TOK], start=True, stop=True).then_inc(S("q_sw"), 1)
                pe.wait_ge(S("kc"), 16)
                for b in range(DEC):
                    mm = nc.tensor.transpose(flat(2, 2)[:, b * P:(b + 1) * P], kc[:, b, :], ident)
                mm.then_inc(S("kcT_ps"), 1)
                pe.wait_ge(S("relw"), 1)
                pe.wait_ge(S("qblk"), 1)
                nc.tensor.matmul(bank(4)[0:AH, 0:P], relb[0:33, :], cst[0:33, C_HOTD:C_HOTD + P], start=True, stop=True).then_inc(S("biasD_ps"), 1)
                pe.wait_ge(S("kcT"), 1)
                for b in range(DEC):
                    mm = nc.tensor.matmul(flat(5, 2)[0:AH, b * P:(b + 1) * P], qblk[:, b, :], kcT[:, b, :], start=True, stop=True)
                mm.then_inc(S("sD_ps"), 1)
                for h in range(AH):
                    toeplitz(h)
                pe.wait_ge(S("kqS"), 2)
                nc.tensor.matmul(bank(4)[:, 0:2 * HD], ident, kqS.rearrange("p i e -> p (i e)"), start=True, stop=False)
                nc.tensor.matmul(bank(4)[:, 0:2 * HD], cst[:, C_SWAP:C_SWAP + P], kqS.rearrange("p i e -> p (i e)"), start=False, stop=True).then_inc(S("kqS_ps"), 1)
                pe.wait_ge(S("pD"), 1)
                for b in range(DEC):
                    mm = nc.tensor.transpose(bank(7)[:, b * AH:(b + 1) * AH], sD[0:AH, b, :], ident[0:AH, 0:AH])
                mm.then_inc(S("pTD_ps"), 1)
                pe.wait_ge(S("pTD"), 1)
                pe.wait_ge(S("vc"), 32)
                for b in range(DEC):
                    mm = nc.tensor.matmul(bank(2)[:, b * AH:(b + 1) * AH], vc[:, b, :], pTD[:, b, :], start=True, stop=True)
                mm.then_inc(S("oD_ps"), 1)
                pe.wait_ge(S("oD"), 1)
                nc.tensor.matmul(bank(3)[:, 0:DEC * AH], cst[:, C_SWAP:C_SWAP + P], oD.rearrange("p b h -> p (b h)"), start=True, stop=True).then_inc(S("osw"), 1)
                pe.wait_ge(S("o_dn"), 1)
                nc.tensor.transpose(bank(7)[:, PR:2 * PR], o2[0:PR].rearrange("p i e -> p (i e)"), ident[0:PR, 0:PR]).then_inc(S("odT"), 1)

            @block.vector
            def _(v):
                tick = [0]

                def chain(ins):
                    tick[0] += 1
                    ins.then_inc(S("dve_decode"), 1)
                    v.wait_ge(S("dve_decode"), tick[0])

                chain(nc.vector.memset(relb[32:33, :], -BIG))
                v.wait_ge(S("d_rel"), 16)
                nc.vector.tensor_copy(relw[0:33], bc(relb[0:33], P)).then_inc(S("relw"), 1)
                v.wait_ge(S("qblk0"), 1)
                v.wait_ge(S("q_sw"), 1)
                qsw = bank(4)[:, P:P + 4 * DEC].rearrange("p (i b) -> p i b", b=DEC)
                for h in range(AH):
                    lo = (h // GQA) * HD
                    src = qf[lo:lo + HD, h // 2, SEQ:TOK] if (h % 2) * HD == lo else qsw[lo:lo + HD, h // 2, :]
                    nc.vector.tensor_copy(qblk[lo:lo + HD, :, h], src)
                nc.vector.tensor_copy(kcT[:, :, 0], kf[:, P + SEQ:]).then_inc(S("qblk"), 1)
                v.wait_ge(S("biasD_ps"), 1)
                nc.vector.tensor_copy(biasD[0:AH], bank(4)[0:AH, 0:P]).then_inc(S("biasD"), 1)
                v.wait_ge(S("biasD"), 1)
                v.wait_ge(S("sinks"), 32)
                nc.vector.tensor_copy(sinkB.rearrange("p (g a f) -> p g a f", g=2, a=2), sinkN.rearrange("p (g f a) -> p g a f", g=2, a=2))

                v.wait_ge(S("qkv"), 32)
                chain(nc.vector.tensor_tensor(sqd[:, 0:2], qkv[:, 0:2], qkv[:, 0:2], ALU.mult))
                chain(nc.vector.tensor_reduce(n2, sqd[:, 0:2], AX.X, ALU.add))
                nc.vector.tensor_scalar(m2[:, 0:1], n2[:, 0:1], float(HD), HD * EPS, ALU.mult, ALU.add)
                nc.vector.tensor_scalar(m2[:, 1:2], n2[:, 1:2], 1.0, EPS, ALU.mult, ALU.add).then_inc(S("n2"), 1)
                v.wait_ge(S("r2"), 1)
                for a in range(2):
                    rows = slice(a * PR, (a + 1) * PR)
                    ins = nc.vector.tensor_tensor(qkh[rows], qkv[rows, 0:2, a * HH:(a + 1) * HH], bc(r2[rows], HH), ALU.mult)
                ins.then_inc(S("qk_n"), 1)
                v.wait_ge(S("qk_n"), 1)
                chain(nc.vector.tensor_tensor(qkv[:, 0:2], qkv[:, 0:2], bc(r2, HD), ALU.mult))
                q_, k_, v_ = (qkv[:, i, :] for i in range(3))
                v.wait_ge(S("S0"), 32)
                chain(nc.vector.tensor_tensor(prod, S0.rearrange("p d e -> p e d"), bm(qkh[:, 1], HD), ALU.mult))
                nc.vector.tensor_reduce(kqS[:, 0], prod, AX.X, ALU.add).then_inc(S("kqS"), 1)
                chain(nc.vector.tensor_tensor(sqd[:, 2], q_, k_, ALU.mult))
                chain(nc.vector.tensor_reduce(qkD, sqd[:, 2], AX.X, ALU.add))

                v.wait_ge(S("sD_ps"), 1)
                sp_ = flat(5, 2)[0:AH].rearrange("p (b j) -> p b j", j=P)
                chain(nc.vector.scalar_tensor_tensor(sD[0:AH], sp_, HD ** -0.5, bm(biasD[0:AH], DEC), ALU.mult, ALU.add))
                chain(nc.vector.tensor_reduce(mD[0:AH], sD[0:AH], AX.X, ALU.max))
                chain(nc.vector.tensor_scalar(mD[0:AH], mD[0:AH], sinkC[0:AH], None, ALU.max))
                nc.vector.tensor_tensor(sD[0:AH], sD[0:AH], bc(mD[0:AH], P), ALU.subtract)
                nc.vector.tensor_scalar(eD[0:AH], mD[0:AH], sinkC[0:AH], -1.0, ALU.subtract, ALU.mult).then_inc(S("xD"), 1)

                v.wait_ge(S("qS"), 1)
                nc.vector.tensor_reduce(kqS[:, 1], prodq, AX.X, ALU.add).then_inc(S("kqS"), 1)
                v.wait_ge(S("egD"), 1)
                v.wait_ge(S("kqS_ps"), 1)
                chain(nc.vector.tensor_scalar(kS, bank(4)[:, 0:HD], egD, None, ALU.mult))
                chain(nc.vector.tensor_tensor(vn1, v_, kS, ALU.subtract))
                chain(nc.vector.tensor_scalar(vn1, vn1, bD, None, ALU.mult))
                chain(nc.vector.tensor_scalar(o1, bank(4)[:, HD:2 * HD], egD, None, ALU.mult))
                chain(nc.vector.scalar_tensor_tensor(o1, vn1, qkD, o1, ALU.mult, ALU.add))
                chain(nc.vector.tensor_tensor(sqd[0:PR, 0], o1[0:PR], o1[0:PR], ALU.mult))
                chain(nc.vector.tensor_reduce(n1[0:PR], sqd[0:PR, 0], AX.X, ALU.add))
                nc.vector.tensor_scalar(m1[0:PR], n1[0:PR], 1.0 / HD, EPS, ALU.mult, ALU.add).then_inc(S("n1"), 1)

                v.wait_ge(S("eD"), 1)
                chain(nc.vector.tensor_reduce(dD[0:AH], sD[0:AH], AX.X, ALU.add))
                chain(nc.vector.tensor_tensor(dD[0:AH], dD[0:AH], eD[0:AH], ALU.add))
                chain(nc.vector.reciprocal(rD[0:AH], dD[0:AH]))
                nc.vector.tensor_tensor(sD[0:AH], sD[0:AH], bc(rD[0:AH], P), ALU.mult).then_inc(S("pD"), 1)
                chain(nc.vector.tensor_tensor(prod.rearrange("p a b -> p (a b)").rearrange("p (d e) -> p d e", e=HD),
                                              bc(qkh[:, 1], HD), bm(vn1, HH), ALU.mult))
                v.wait_ge(S("pTD_ps"), 1)
                nc.vector.tensor_copy(pTD, bank(7)[:, 0:DEC * AH].rearrange("p (b h) -> p b h", h=AH)).then_inc(S("pTD"), 1)
                nc.vector.scalar_tensor_tensor(S0, S0, egD, prod.rearrange("p a b -> p (a b)").rearrange("p (d e) -> p d e", e=HD), ALU.mult, ALU.add).then_inc(S("S1"), 1)
                v.wait_ge(S("r1"), 1)
                v.wait_ge(S("szd"), 16)
                chain(nc.vector.scalar_tensor_tensor(o1[0:PR], o1[0:PR], r1[0:PR], normB[0:PR], ALU.mult, ALU.mult))
                nc.vector.tensor_tensor(o2[0:PR], bm(o1[0:PR], 2), bm(szd[0:PR], 2), ALU.mult).then_inc(S("o_dn"), 1)
                v.wait_ge(S("oD_ps"), 1)
                nc.vector.tensor_copy(oD, bank(2)[:, 0:DEC * AH].rearrange("p (b h) -> p b h", h=AH)).then_inc(S("oD"), 1)
                v.wait_ge(S("oD"), 1)
                v.wait_ge(S("osw"), 1)
                oS = bank(3)[:, 0:DEC * AH].rearrange("p (b h) -> p b h", h=AH)
                for h in range(AH):
                    lo = (h % 2) * HD
                    src = oD if (h // GQA) * HD == lo else oS
                    nc.vector.tensor_copy(mixD[lo:lo + HD, h // 2, :], src[lo:lo + HD, :, h])
                v.wait_ge(S("odT"), 1)
                for a in range(2):
                    rows = slice(a * HD, (a + 1) * HD)
                    ins = nc.vector.tensor_copy(mixD[rows, 4:8, :], bank(7)[rows, PR:2 * PR].rearrange("p (b k a) -> p a k b", k=4, a=2)[:, a])
                ins.then_inc(S("mixD"), 1)

        stage_ends()
        mem.at = mixer
        qst, kst, kswst, vst = mem.take(4, P), mem.take(2 * P), mem.take(2 * P), mem.take(2 * P)
        yst = mem.take(FT_DN, P)
        szst = mem.take(NH * HD)
        sA = [mem.take(GQA, 2 * P) for _ in range(2)]
        pT = mem.take(2 * GQA, P)
        mix = mem.take(KD, P)
        qk = mem.take(KD, P)
        qkT = mem.take(KD, P)
        vtok = mem.take(NH, HD)
        E_ = mem.take(NH, P)
        gU = mem.take(NH, P)
        AT = mem.take(NH, P)
        QK = mem.take(NH, P)
        Lo = [mem.take(NH, P) for _ in range(2)]
        Xs = mem.take(NH, P)
        sq = Xs.rearrange("p h i -> p (h i)")
        MT = [mem.take(NH, P) for _ in range(2)]
        M_ = mem.take(NH, P)
        r_, vn, vn2, tmp, o_ = (mem.take(NH, HD) for _ in range(5))
        Sst = mem.take(4, HD)
        xres, hh_, xs2 = mem.take(D), mem.take(D), mem.take(D)
        xT2 = mem.take(KD, P)
        ss16, m16, r16 = mem.take(16), mem.take(16), mem.take(16)
        ss8, m8, r8, egam, kdec, eglS, gam8 = (mem.take(NH) for _ in range(7))
        mx, mm_, nm_, es_, den, rcp = ([mem.take(GQA) for _ in range(2)] for _ in range(6))
        ssx, msx, rsx = mem.take(1), mem.take(1), mem.take(1)
        LV = 7

        ORD = (0, 2, 1, 3)
        SLOT = (0, 2, 4, 6, 1, 3, 5, 7)

        kqS_ps = flat(4, 2).rearrange("p (a n f e) -> p a n f e", a=2, n=2, f=4)

        def slots(x):
            return x.rearrange("p (a f) d -> p a f d", a=2)

        def natural(x):
            return x.rearrange("p (f a d) -> p a f d", a=2, d=HD)

        def scores_ps(g):
            return flat(2 * g, 2).rearrange("p (h j) -> p h j", h=GQA)

        with nc.Block() as block:
            @block.sync
            def _(sp):

                def load_tile(t, xrows, first=False):
                    rows = t * P if first else sp.snap(t * P)
                    if not first:
                        sp.wait_ge(S("tokv_ps"), t)
                        settle(sp)
                    sp.dma_start(yst, y_d[:, :, bass.ds(rows, P)]).then_inc(S("y_in"), 16)
                    if not first:
                        sp.wait_ge(S("av_ps"), t)
                    sp.dma_start(qst, qf[:, :, bass.ds(rows, P)]).then_inc(S("att_in"), 16)
                    sp.dma_start(kst, kf[:, bass.ds(rows, 2 * P)]).then_inc(S("att_in"), 16)
                    sp.dma_start(kswst, ksw[:, bass.ds(rows, 2 * P)]).then_inc(S("att_in"), 16)
                    sp.dma_start(vst.rearrange("p (a b) -> p a b", b=P), vt[:, bass.ds(t, 2), :]).then_inc(S("att_in"), 16)
                    if not first:
                        sp.wait_ge(S("h"), t)
                    sp.dma_start(xres[0:xrows.shape[0]], xrows).then_inc(S("xres"), 16)
                    if not first:
                        sp.wait_ge(S("og"), t)
                    sp.dma_start(szst, sz_d[bass.ds(rows, P), :]).then_inc(S("sz_in"), 16)

                load_tile(0, I["x_sample"][:, 0, :], first=True)
                with sp.Fori(1, NT) as t:
                    load_tile(t, I["x_prompt"][0, bass.ds(sp.snap(t * P - P), P), :])
                sp.wait_ge(S("h"), NT)
                sp.dma_start(xres, I["x_prompt"][0, SEQ - P:SEQ, :]).then_inc(S("xres"), 16)
                sp.wait_ge(S("S"), NT + 1)
                for hp in range(2):
                    sp.dma_start(O["state_S_prompt"][0, 0, hp::2].rearrange("h d e -> d h e"), Sst[hp * HD:(hp + 1) * HD]).then_inc(S("o3"), 16)
                sp.wait_ge(S("o3"), 32)

            @block.gpsimd
            def _(g):
                g.memset(Sst, 0.0).then_inc(S("S"), 1)
                g.wait_ge(S("S"), 1)

                def rms_pow(name, out, in_, n, t):
                    g.wait_ge(S("m_" + name), t + 1)
                    g.tensor_tensor(out, in_, half[0:out.shape[0]].to_broadcast([out.shape[0], n]), ALU.pow).then_inc(S("r_" + name), 1)

                def tile(t, first=False):
                    if not first:
                        g.wait_ge(S("gam_ps"), t)
                    g.tensor_tensor(gU, bm(cst[:, C_U:C_U + P], NH), bc(gb[:, t, NH:2 * NH], P), ALU.mult).then_inc(S("gU"), 1)
                    if not first:
                        rms_pow("o", r8, m8, NH, t - 1)
                    rms_pow("qk", r16, m16, 16, t)
                    R = DEC if first else P
                    rms_pow("x", rsx[0:R], msx[0:R], 1, t)
                    for l in range(1, LV):
                        if l == 1:
                            g.wait_ge(S("AT"), t + 1)
                            g.wait_ge(S("X1_ps"), (LV - 1) * t)
                        elif l >= 3:
                            g.wait_ge(S("X1_ps"), (LV - 1) * t + l - 2)
                        elif l == 2:
                            g.wait_ge(S("MT1"), LV * t + 1)
                        g.tensor_tensor(Lo[l % 2], AT, bm(cst[:, C_LV + l * P:C_LV + (l + 1) * P], NH), ALU.mult).then_inc(S("Lo"), 1)

                tile(0, first=True)
                with g.Fori(1, NT) as t:
                    tile(t)
                rms_pow("o", r8, m8, NH, NT - 1)
                rms_pow("x", rsx, msx, 1, NT)

            @block.vector
            def _(v):
                V = nc.vector

                def residual(t, R):
                    v.wait_ge(S("proj_ps"), t + 1)
                    v.wait_ge(S("xres"), 16 * t + 16)
                    v.wait_ge(S("h_out"), 16 * t)
                    V.tensor_tensor(hh_[0:R], xres[0:R], flat(2, 2)[0:R], ALU.add).then_inc(S("h"), 1)

                def normed(t, R):
                    v.wait_ge(S("ssx"), t + 1)
                    V.tensor_scalar(msx[0:R], ssx[0:R], 1.0 / D, EPS, ALU.mult, ALU.add).then_inc(S("m_x"), 1)
                    v.wait_ge(S("r_x"), t + 1)
                    V.tensor_scalar(xs2[0:R], hh_[0:R], rsx[0:R], None, ALU.mult).then_inc(S("xs2"), 1)

                def gain(t, R):
                    v.wait_ge(S("xT2_ps"), t + 1)
                    V.tensor_tensor(xT2[:, :, 0:R], flat(0, 2).rearrange("p (k c) -> p k c", c=P)[:, :, 0:R], bc(g_ffn, R), ALU.mult).then_inc(S("xT2"), 1)

                def logits(t, R, dst):
                    v.wait_ge(S("lg_ps"), t + 1)
                    V.tensor_copy(dst, bank(3)[0:R, 0:NG + NE]).then_inc(S("lg"), 1)

                def gated(t):
                    v.wait_ge(S("osq"), t + 1)
                    V.tensor_reduce(ss8, tmp, AX.X, ALU.add).then_inc(S("v_ss8"), 1)
                    v.wait_ge(S("v_ss8"), t + 1)
                    V.tensor_scalar(m8, ss8, 1.0 / HD, EPS, ALU.mult, ALU.add).then_inc(S("m_o"), 1)
                    v.wait_ge(S("sz_in"), 16 * t + 16)
                    V.tensor_tensor(slots(r_), natural(szst), slots(bm(normB, NH)), ALU.mult).then_inc(S("v_sz"), 1)

                def gated_out(t):
                    v.wait_ge(S("r_o"), t + 1)
                    V.tensor_tensor(o_, o_, bc(r8, HD), ALU.mult).then_inc(S("v_on"), 1)
                    v.wait_ge(S("v_on"), t + 1)
                    V.tensor_tensor(natural(vn.rearrange("p h d -> p (h d)")), slots(o_), slots(r_), ALU.mult).then_inc(S("og"), 1)

                def tile(t, R, dst, first=False):
                    if not first:
                        gated(t - 1)
                    for g in range(2):
                        if g == 1 and not first:
                            gated_out(t - 1)
                        v.wait_ge(S(f"sc{g}"), t + 1)
                        V.scalar_tensor_tensor(sA[g], scores_ps(g), HD ** -0.5, biasS[:, GQA * g:GQA * g + GQA, :], ALU.mult, ALU.add).then_inc(S(f"s{g}"), 1)
                    for g in range(2):
                        v.wait_ge(S(f"s{g}"), t + 1)
                        V.tensor_scalar(sA[g][:, :, 0:P], sA[g][:, :, 0:P], cst[:, bass.ds(C_FLAG + t, 1)], None, ALU.add).then_inc(S(f"sf{g}"), 1)
                    v.wait_ge(S("gam_ps"), t + 1)
                    gB = flat(4, 2).rearrange("p (h i) -> p h i", i=P)
                    gL = gB[:, :, P - 1]
                    V.tensor_copy(gam8, bank(6)[:, 0:NH]).then_inc(S("v_gC"), 1)
                    v.wait_ge(S("v_gC"), t + 1)
                    V.tensor_tensor(E_, gB, bc(gam8, P), ALU.subtract).then_inc(S("v_D"), 1)
                    V.tensor_tensor(kdec, gL, gam8, ALU.subtract).then_inc(S("kd_in"), 1)
                    v.wait_ge(S("v_D"), t + 1)
                    V.tensor_tensor(E_, E_, bm(cst[:, C_NEG:C_NEG + P], NH), ALU.add).then_inc(S("D"), 1)
                    for g in range(2):
                        v.wait_ge(S(f"sf{g}"), t + 1)
                        V.tensor_reduce(mx[g], sA[g], AX.X, ALU.max).then_inc(S(f"v_mx{g}"), 1)
                        v.wait_ge(S(f"v_mx{g}"), t + 1)
                        V.tensor_tensor(mm_[g], mx[g], sinkB[:, GQA * g:GQA * g + GQA], ALU.max).then_inc(S(f"v_mm{g}"), 1)
                        v.wait_ge(S(f"v_mm{g}"), t + 1)
                        V.tensor_scalar(nm_[g], mm_[g], -1.0, None, ALU.mult)
                        V.tensor_tensor(es_[g], sinkB[:, GQA * g:GQA * g + GQA], mm_[g], ALU.subtract).then_inc(S(f"nm{g}"), 1)
                    v.wait_ge(S("E"), t + 1)
                    V.tensor_tensor(gU, E_, bc(gb[:, t, 0:NH], P), ALU.mult).then_inc(S("Eb"), 1)
                    v.wait_ge(S("sq"), t + 1)
                    V.tensor_reduce(ss16, sq.rearrange("p (h d) -> p h d", d=HD), AX.X, ALU.add).then_inc(S("v_ss"), 1)
                    v.wait_ge(S("v_ss"), t + 1)
                    V.tensor_scalar(m16[:, 0:NH], ss16[:, 0:NH], float(HD), HD * EPS, ALU.mult, ALU.add)
                    V.tensor_scalar(m16[:, NH:], ss16[:, NH:], 1.0, EPS, ALU.mult, ALU.add).then_inc(S("m_qk"), 1)
                    for g in range(2):
                        v.wait_ge(S(f"p{g}"), t + 1)
                        V.tensor_tensor(den[g], den[g], es_[g], ALU.add).then_inc(S(f"v_den{g}"), 1)
                        v.wait_ge(S(f"v_den{g}"), t + 1)
                        V.reciprocal(rcp[g], den[g]).then_inc(S(f"v_rcp{g}"), 1)
                        v.wait_ge(S(f"v_rcp{g}"), t + 1)
                        V.tensor_tensor(sA[g], sA[g], bc(rcp[g], 2 * P), ALU.mult).then_inc(S(f"pn{g}"), 1)
                        if g == 0:
                            v.wait_ge(S("r_qk"), t + 1)
                            V.tensor_tensor(qk.rearrange("p f (a d) -> p (f a) d", d=HD), flat(0, 2).rearrange("p (h d) -> p h d", d=HD),
                                            bc(r16, HD), ALU.mult).then_inc(S("qk"), 1)
                    residual(t, R)
                    normed(t, R)
                    v.wait_ge(S("G_ps"), t + 1)
                    v.wait_ge(S("Eb"), t + 1)
                    v.wait_ge(S("Lo"), (LV - 1) * t)
                    V.tensor_tensor(AT, flat(6, 2).rearrange("p (h i) -> p h i", i=P), gU, ALU.mult).then_inc(S("AT"), 1)
                    v.wait_ge(S("AT"), t + 1)
                    for g in range(2):
                        hs = slice(4 * g, 4 * g + 4)
                        V.tensor_tensor(Lo[0][:, hs], AT[:, hs], bm(cst[:, C_LV:C_LV + P], 4), ALU.mult).then_inc(S("v_L0"), 1)
                        v.wait_ge(S("v_L0"), 2 * t + g + 1)
                        V.tensor_tensor(MT[0][:, hs], bm(ident, 4), Lo[0][:, hs], ALU.subtract).then_inc(S(f"MT{g}"), 1)
                    gain(t, R)
                    logits(t, R, dst)
                    v.wait_ge(S("QK_ps"), t + 1)
                    V.tensor_tensor(QK, flat(4, 2).rearrange("p (h i) -> p h i", i=P), E_, ALU.mult).then_inc(S("QK"), 1)
                    for l in range(1, LV):
                        for g in range(2):
                            hs = slice(4 * g, 4 * g + 4)
                            v.wait_ge(S(f"PT{g}_ps"), (LV - 1) * t + l)
                            V.tensor_tensor(MT[l % 2][:, hs], MT[(l - 1) % 2][:, hs], bank(6 + g).rearrange("p (h i) -> p h i", i=P),
                                            ALU.subtract).then_inc(S(f"MT{g}"), 1)
                        if l == 2:
                            v.wait_ge(S("egam"), t + 1)
                            v.wait_ge(S("kS_ps"), t + 1)
                            V.tensor_tensor(slots(tmp), kqS_ps[:, :, 0], slots(bc(egam, HD)), ALU.mult).then_inc(S("v_kS"), 1)
                        if l == 3:
                            v.wait_ge(S("v_kS"), t + 1)
                            V.tensor_tensor(r_, vtok, tmp, ALU.subtract).then_inc(S("r"), 1)
                        if l == 4:
                            v.wait_ge(S("r"), t + 1)
                            V.tensor_tensor(slots(tmp), kqS_ps[:, :, 1], slots(bc(egam, HD)), ALU.mult).then_inc(S("v_qS"), 1)
                            V.tensor_tensor(Sst, Sst, bc(eglS[:, 0:4], HD), ALU.mult).then_inc(S("v_S"), 1)
                    for g in range(2):
                        hs = slice(4 * g, 4 * g + 4)
                        v.wait_ge(S(f"v{g}_ps"), t + 1)
                        V.tensor_tensor(vn[:, hs], bank(2 * (1 - g))[:, 0:4 * HD].rearrange("p (h d) -> p h d", d=HD), bc(gb[:, t, 4 * g:4 * g + 4], HD),
                                        ALU.mult).then_inc(S(f"vn{g}"), 1)
                    v.wait_ge(S("vn1"), t + 1)
                    V.tensor_tensor(vn2, vn, bc(kdec, HD), ALU.mult).then_inc(S("vn2"), 1)
                    for g in range(2):
                        hs = slice(4 * g, 4 * g + 4)
                        v.wait_ge(S(f"o{g}_ps"), t + 1)
                        V.tensor_tensor(o_[:, hs], bank(3 - 2 * g)[:, 0:4 * HD].rearrange("p (h d) -> p h d", d=HD), tmp[:, hs], ALU.add).then_inc(S("o"), 1)
                    v.wait_ge(S("v_S"), t + 1)
                    v.wait_ge(S("dS_ps"), t + 1)
                    V.tensor_tensor(Sst, Sst, bank(6)[:, 0:4 * HD].rearrange("p (f e) -> p f e", e=HD), ALU.add).then_inc(S("S"), 1)

                tile(0, DEC, lg[0:DEC, NT, :], first=True)
                with v.Fori(1, NT) as t:
                    tile(t, P, lg[:, bass.ds(t - 1, 1), :].rearrange("p a n -> p (a n)"))
                gated(NT - 1)
                gated_out(NT - 1)
                residual(NT, P)
                normed(NT, P)
                gain(NT, P)
                logits(NT, P, lg[:, NT - 1, :])

            @block.scalar
            def _(act):
                A = nc.scalar

                def norm_rows(t, R, rows):
                    act.wait_ge(S("h"), t + 1)
                    act.wait_ge(S("xT2_ps"), t)
                    act.wait_ge(S("xs_out"), 16 * t)
                    A.activation(xs2[0:R], hh_[0:R], ACT.Square, accum_out=ssx[0:R]).then_inc(S("ssx"), 1)
                    act.dma_start(h_d[rows, :], hh_[0:R]).then_inc(S("h_out"), 16)

                def store_rows(t, R, rows):
                    act.wait_ge(S("xs2"), t + 1)
                    act.dma_start(xs_d[rows, :], xs2[0:R]).then_inc(S("xs_out"), 16)

                def mix_rows(t):
                    act.wait_ge(S("oT_ps"), t + 1)
                    A.activation(mix[:, 4:8, :], bank(7).rearrange("p (f q) -> p f q", q=P), ACT.Copy).then_inc(S("mixB"), 1)

                def tile(t, R, rows, first=False):
                    if not first:
                        mix_rows(t - 1)
                    act.wait_ge(S("tok_ps"), t + 1)
                    A.activation(sq, flat(0, 2), ACT.Square).then_inc(S("sq"), 1)
                    act.wait_ge(S("D"), t + 1)
                    act.wait_ge(S("kd_in"), t + 1)
                    A.activation(E_, E_, ACT.Exp).then_inc(S("E"), 1)
                    A.activation(kdec, kdec, ACT.Exp)
                    A.activation(egam, bank(6)[:, 0:NH], ACT.Exp)
                    gL = flat(4, 2).rearrange("p (h i) -> p h i", i=P)[:, :, P - 1]
                    A.activation(eglS[0:HD, 0:4], gL[0:HD, 0:4], ACT.Exp)
                    A.activation(eglS[HD:P, 0:4], gL[HD:P, 4:8], ACT.Exp).then_inc(S("egam"), 1)
                    act.wait_ge(S("tokv_ps"), t + 1)
                    A.activation(slots(vtok), natural(bank(7)), ACT.Copy).then_inc(S("vtok"), 1)
                    for g in range(2):
                        act.wait_ge(S(f"nm{g}"), t + 1)
                        for i in range(GQA):
                            A.activation(sA[g][:, i, :], sA[g][:, i, :], ACT.Exp, bias=nm_[g][:, i:i + 1], accum_out=den[g][:, i:i + 1])
                        A.activation(es_[g], es_[g], ACT.Exp).then_inc(S(f"p{g}"), 1)
                    act.wait_ge(S("qkT_ps"), t + 1)
                    A.activation(qkT, flat(4, 2).rearrange("p (a q) -> p a q", q=P), ACT.Copy).then_inc(S("qkT"), 1)
                    act.wait_ge(S("pT0_ps"), t + 1)
                    A.activation(pT, flat(2, 2).rearrange("p (a q) -> p a q", q=P), ACT.Copy).then_inc(S("pT0"), 1)
                    norm_rows(t, R, rows)
                    act.wait_ge(S("pT1_ps"), t + 1)
                    act.wait_ge(S("av0_ps"), t + 1)
                    A.activation(pT, flat(0, 2).rearrange("p (a q) -> p a q", q=P), ACT.Copy).then_inc(S("pT1"), 1)
                    act.wait_ge(S("av_ps"), t + 1)
                    A.activation(mix[:, 0:4, :], bank(2).rearrange("p (f q) -> p f q", q=P), ACT.Copy).then_inc(S("mixA"), 1)
                    store_rows(t, R, rows)
                    for l in range(LV):
                        for g in range(2):
                            hs = slice(4 * g, 4 * g + 4)
                            if l > 0:
                                act.wait_ge(S(f"X{g}_ps"), (LV - 1) * t + l)
                                A.activation(Xs[:, hs], bank(2 + g).rearrange("p (h i) -> p h i", i=P), ACT.Copy).then_inc(S(f"X{g}"), 1)
                        for g in range(2):
                            hs = slice(4 * g, 4 * g + 4)
                            if l < LV - 1:
                                act.wait_ge(S(f"Tr{g}_ps"), (LV - 1) * t + l + 1)
                                A.activation(M_[:, hs], bank(g).rearrange("p (h i) -> p h i", i=P), ACT.Copy).then_inc(S(f"M{g}"), 1)
                    act.wait_ge(S("o"), 2 * t + 2)
                    A.activation(tmp, o_, ACT.Square).then_inc(S("osq"), 1)

                tile(0, DEC, slice(SEQ, TOK), first=True)
                with act.Fori(1, NT) as t:
                    tile(t, P, bass.ds(act.snap(t * P - P), P))
                mix_rows(NT - 1)
                norm_rows(NT, P, slice(SEQ - P, SEQ))
                store_rows(NT, P, slice(SEQ - P, SEQ))
                act.wait_ge(S("h_out"), 16 * (NT + 1))
                act.wait_ge(S("xs_out"), 16 * (NT + 1))

            @block.tensor
            def _(pe):
                T = nc.tensor

                def half_of(h):
                    return slice((h % 2) * HD, (h % 2) * HD + HD)

                def turn_out(t):
                    pe.wait_ge(S("og"), t + 1)
                    for f in range(4):
                        mm = T.transpose(bank(7)[:, f * P:(f + 1) * P], vn.rearrange("p h d -> p (h d)")[:, f * P:(f + 1) * P], ident)
                    mm.then_inc(S("oT_ps"), 1)

                def project(t, R, src, n):
                    for k in range(KD):
                        mm = T.matmul(bank(2 + n)[0:R], src[:, k, :], wout[:, k, n * 512:(n + 1) * 512], start=(k == 0), stop=(k == KD - 1))
                    return mm

                def turn_rows(t, R):
                    pe.wait_ge(S("xs2"), t + 1)
                    for k in range(KD):
                        mm = T.transpose(flat(0, 2)[:, k * P:k * P + R], xs2[0:R].rearrange("p (c k) -> p k c", k=KD)[:, k, :], ident[0:R, 0:R])
                    mm.then_inc(S("xT2_ps"), 1)

                def route(t, R):
                    pe.wait_ge(S("xT2"), t + 1)
                    pe.wait_ge(L("wr"), 32)
                    for k in range(KD):
                        mm = T.matmul(bank(3)[0:R, 0:NG + NE], xT2[:, k, 0:R], wr[:, k, :], start=(k == 0), stop=(k == KD - 1))
                    mm.then_inc(S("lg_ps"), 1)

                def tile(t, R, src, first=False):
                    pe.wait_ge(S("att_in"), 64 * t + 64)
                    pe.wait_ge(S("o"), 2 * t)
                    for g in range(2):
                        for i in range(GQA):
                            h = GQA * g + ORD[i]
                            ks = kst if h % 2 == g else kswst
                            mm = T.matmul(scores_ps(g)[:, i, :], qst[half_of(h), h // 2, :], ks[half_of(h), :], start=True, stop=True)
                        mm.then_inc(S(f"sc{g}"), 1)
                    pe.wait_ge(S("gU"), t + 1)
                    pe.wait_ge(S("S"), t + 1)
                    T.matmul(bank(6)[:, 0:NH], cst[:, C_U:C_U + P], gb[:, t, NH:2 * NH], start=True, stop=True)
                    for n in range(2):
                        mm = T.matmul(bank(4 + n), ones, gU[:, 4 * n:4 * n + 4].rearrange("p h i -> p (h i)"), start=True, stop=True)
                    mm.then_inc(S("gam_ps"), 1)
                    if not first:
                        turn_out(t - 1)
                    pe.wait_ge(S("y_in"), 16 * t + 16)
                    pe.wait_ge(S("s0"), t + 1)
                    for f in range(8):
                        mm = T.transpose(flat(0, 2)[:, f * P:(f + 1) * P], yst[:, f, :], ident)
                    mm.then_inc(S("tok_ps"), 1)
                    if not first:
                        pe.wait_ge(S("mixB"), t)
                    pe.wait_ge(L("wout"), 16)
                    pe.wait_ge(S("s1"), t + 1)
                    project(t, R, src, 0)
                    for f in range(4):
                        mm = T.transpose(bank(7)[:, f * P:(f + 1) * P], yst[:, 8 + f, :], ident)
                    mm.then_inc(S("tokv_ps"), 1)
                    project(t, R, src, 1).then_inc(S("proj_ps"), 1)
                    pe.wait_ge(S("qk"), t + 1)
                    pe.wait_ge(S("D"), t + 1)
                    pe.wait_ge(S("egam"), t + 1)
                    for f in range(8):
                        mm = T.transpose(flat(4, 2)[:, f * P:(f + 1) * P], qk[:, f, :], ident)
                    mm.then_inc(S("qkT_ps"), 1)
                    for g in range(2):
                        pe.wait_ge(S(f"pn{g}"), t + 1)
                        if g == 0:
                            pe.wait_ge(S("h"), t + 1)
                        for i in range(GQA):
                            for b in range(2):
                                mm = T.transpose(flat(2 - 2 * g, 2)[:, (2 * i + b) * P:(2 * i + b + 1) * P], sA[g][:, i, b * P:(b + 1) * P], ident)
                        mm.then_inc(S(f"pT{g}_ps"), 1)
                    pe.wait_ge(S("qkT"), t + 1)
                    pe.wait_ge(S("vtok"), t + 1)
                    for s, h in enumerate(SLOT):
                        kT = qkT[half_of(h), 4 + h // 2, :]
                        mm = T.matmul(flat(6, 2)[:, s * P:(s + 1) * P], kT, kT, start=True, stop=True)
                    mm.then_inc(S("G_ps"), 1)

                    def values(g):
                        pe.wait_ge(S(f"pT{g}"), t + 1)
                        for i in range(GQA):
                            h = GQA * g + ORD[i]
                            for b in range(2):
                                mm = T.matmul(bank(2)[half_of(h), (h // 2) * P:(h // 2 + 1) * P], vst[:, b * P + g * HD:b * P + g * HD + HD],
                                              pT[:, 2 * i + b, :], start=(b == 0), stop=(b == 1))
                        return mm

                    values(0).then_inc(S("av0_ps"), 1)
                    for s, h in enumerate(SLOT):
                        mm = T.matmul(flat(4, 2)[:, s * P:(s + 1) * P], qkT[half_of(h), 4 + h // 2, :], qkT[half_of(h), h // 2, :], start=True, stop=True)
                    mm.then_inc(S("QK_ps"), 1)
                    pe.wait_ge(S("pT1"), t + 1)
                    turn_rows(t, R)
                    values(1).then_inc(S("av_ps"), 1)
                    for l in range(LV):
                        if l > 0:
                            for g in range(2):
                                pe.wait_ge(S(f"M{g}"), (LV - 1) * t + l)
                                pe.wait_ge(S("Lo"), (LV - 1) * t + l)
                                for h in range(4 * g, 4 * g + 4):
                                    mm = T.matmul(bank(2 + g)[:, (h % 4) * P:(h % 4 + 1) * P], Lo[l % 2][:, h, :], M_[:, h, :], start=True, stop=True)
                                mm.then_inc(S(f"X{g}_ps"), 1)
                            if l == 2:
                                pe.wait_ge(S("QK"), t + 1)
                                for n in range(2):
                                    for h in SLOT:
                                        mm = T.matmul(kqS_ps[:, h % 2, n, h // 2, :], qkT[half_of(h), 4 - 4 * n + h // 2, :], Sst[half_of(h), h // 2, :], start=True, stop=True)
                                mm.then_inc(S("kS_ps"), 1)
                            for g in range(2):
                                pe.wait_ge(S(f"X{g}"), (LV - 1) * t + l)
                                if l == 1:
                                    pe.wait_ge(S("AT"), t + 1)
                                for h in range(4 * g, 4 * g + 4):
                                    mm = T.matmul(bank(6 + g)[:, (h % 4) * P:(h % 4 + 1) * P], Xs[:, h, :], MT[(l - 1) % 2][:, h, :], start=True, stop=True)
                                mm.then_inc(S(f"PT{g}_ps"), 1)
                        if l < LV - 1:
                            for g in range(2):
                                pe.wait_ge(S(f"MT{g}"), LV * t + l + 1)
                                if l == 0:
                                    pe.wait_ge(S("xT2"), t + 1)
                                for h in range(4 * g, 4 * g + 4):
                                    mm = T.transpose(bank(g)[:, (h % 4) * P:(h % 4 + 1) * P], MT[l % 2][:, h, :], ident)
                                mm.then_inc(S(f"Tr{g}_ps"), 1)
                        if l == 0:
                            route(t, R)
                            pe.wait_ge(S("lg"), t + 1)
                            pe.wait_ge(S("mixA"), t + 1)
                    pe.wait_ge(S("r"), t + 1)
                    for g in range(2):
                        pe.wait_ge(S(f"MT{g}"), LV * t + LV)
                        for h in range(4 * g, 4 * g + 4):
                            mm = T.matmul(bank(2 * (1 - g))[:, (h % 4) * HD:(h % 4 + 1) * HD], MT[(LV - 1) % 2][:, h, :], r_[:, h, :], start=True, stop=True)
                        mm.then_inc(S(f"v{g}_ps"), 1)
                    for g in range(2):
                        pe.wait_ge(S(f"vn{g}"), t + 1)
                        for h in range(4 * g, 4 * g + 4):
                            mm = T.matmul(bank(3 - 2 * g)[:, (h % 4) * HD:(h % 4 + 1) * HD], QK[:, h, :], vn[:, h, :], start=True, stop=True)
                        mm.then_inc(S(f"o{g}_ps"), 1)
                    pe.wait_ge(S("vn2"), t + 1)
                    for s, h in enumerate(SLOT):
                        mm = T.matmul(bank(6)[half_of(h), (h // 2) * HD:(h // 2 + 1) * HD], qk[:, 4 + h // 2, half_of(h)], vn2[:, s, :], start=True, stop=True)
                    mm.then_inc(S("dS_ps"), 1)

                tile(0, DEC, mixD, first=True)
                with pe.Fori(1, NT) as t:
                    tile(t, P, mix)
                turn_out(NT - 1)
                pe.wait_ge(S("mixB"), NT)
                project(NT, P, mix, 0)
                project(NT, P, mix, 1).then_inc(S("proj_ps"), 1)
                turn_rows(NT, P)
                route(NT, P)

        stage_ends()
        until_mixed.close()
        mem = room("experts", WORDS - ALL, es)
        U = 4
        wgu = [mem.take(KD, 2 * DE) for _ in range(U)]
        wd = [mem.take(KE, D) for _ in range(U)]
        after_weights = mem.at
        NTT = NT + 1
        fill = mem.take(MAXB, 4).bitcast(I32)
        gmx, pm, sm, pgs, m1, m2, ex, dn, gate1, gate2 = (mem.take(NTT) for _ in range(10))
        eqg, selg, exg = mem.take(NTT, NG), mem.take(NTT, NG), mem.take(NTT, NG)
        wide, oh1, oh2, slotE, geb = (mem.take(NTT, NE) for _ in range(5))
        mask = mem.take(NTT, NE)
        le, le2, q1, q2, e1h, e2h = (mem.take(NTT, EPG) for _ in range(6))
        cnt, ext, incl, base = (mem.take(NE) for _ in range(4))
        cmp8 = mem.take(NE, 8)
        cmpo, cmpo2, eo = mem.take(XB, NE), mem.take(XB, NE), mem.take(XB + 1)
        dst, dsti = mem.take(2, NTT), mem.take(2, NTT).bitcast(I32)
        pay = mem.take(2, NTT * 4).rearrange("p k (t c) -> p k t c", c=4).bitcast(I32)
        tabrow = mem.take(P, 4)

        def cols(c0, n):
            return cst[:, c0:c0 + n]

        def load_expert(sp, u, e, gate_up, down):
            for w, lo in (("w_gate", 0), ("w_up", DE)):
                sp.dma_start(wgu[u][:, :, lo:lo + DE], I[w][0, bass.ds(e, 1)].rearrange("a (p k) n -> p (a k) n", k=KD)).then_inc(gate_up, 16)
            sp.dma_start(wd[u].rearrange("p k n -> p (k n)"), I["w_down"][0, bass.ds(e, 1)].rearrange("a (p k) n -> p (a k n)", k=KE)).then_inc(down, 16)

        with nc.Block() as block:
            @block.sync
            def _(sp):
                for u in range(U):
                    load_expert(sp, u, u, L(f"wgu{u}"), L(f"wd{u}"))

            @block.vector
            def _(v):
                V = nc.vector
                tick = [0]

                def chain(ins):
                    tick[0] += 1
                    ins.then_inc(S("dve_route"), 1)
                    v.wait_ge(S("dve_route"), tick[0])

                def first(values, best, prio, marks, out):
                    n = values.shape[2]
                    chain(V.tensor_tensor(marks, values, bc(best, n), ALU.is_ge))
                    chain(V.tensor_tensor(marks, marks, bm(prio, NTT), ALU.mult))
                    chain(V.tensor_reduce(pm, marks, AX.X, ALU.max))
                    chain(V.tensor_tensor(out, marks, bc(pm, n), ALU.is_equal))

                chain(V.memset(fill, 0))
                chain(V.memset(fill[:, :, 1], DUMP))
                V.memset(pay, 0).then_inc(S("fill"), 1)
                G = lg[:, :, 0:NG]
                chain(V.tensor_reduce(gmx, G, AX.X, ALU.max))
                V.tensor_tensor(exg, G, bc(gmx, NG), ALU.subtract).then_inc(S("exg"), 1)
                first(G, gmx, cols(C_GP, NG), eqg, selg)
                w4 = wide.rearrange("p t (g j) -> p t g j", g=NG)
                l4 = lg[:, :, NG:].rearrange("p t (g j) -> p t g j", g=NG)
                s4 = selg.unsqueeze(3).to_broadcast([P, NTT, NG, EPG])
                chain(V.tensor_tensor(w4, l4, s4, ALU.mult))
                chain(V.tensor_reduce(le, wide.rearrange("p t (g j) -> p t j g", g=NG), AX.X, ALU.add))
                chain(V.tensor_reduce(m1, le, AX.X, ALU.max))
                first(le, m1, cols(C_EP, EPG), q1, e1h)
                chain(V.scalar_tensor_tensor(le2, e1h, -BIG, le, ALU.mult, ALU.add))
                chain(V.tensor_reduce(m2, le2, AX.X, ALU.max))
                first(le2, m2, cols(C_EP, EPG), q2, e2h)
                V.tensor_tensor(ex, m2, m1, ALU.subtract).then_inc(S("ex"), 1)
                val = cols(C_VAL, NTT)
                for e_, o in ((e1h, oh1), (e2h, oh2)):
                    o4 = o.rearrange("p t (g j) -> p t g j", g=NG)
                    chain(V.tensor_tensor(o4, s4, e_.unsqueeze(2).to_broadcast([P, NTT, NG, EPG]), ALU.mult))
                    chain(V.tensor_tensor(o, o, bc(val, NE), ALU.mult))
                V.tensor_tensor(mask, oh1, oh2, ALU.add).then_inc(S("mask"), 1)
                v.wait_ge(S("exps"), 1)
                chain(V.tensor_reduce(sm, exg, AX.X, ALU.add))
                chain(V.tensor_scalar(dn, ex, 1.0, None, ALU.add))
                chain(V.tensor_tensor(dn, dn, sm, ALU.mult))
                chain(V.reciprocal(gate1, dn))
                chain(V.tensor_tensor(gate2, gate1, ex, ALU.mult))
                for k, gt in ((0, gate1), (1, gate2)):
                    V.tensor_copy(pay[:, k, :, 0], cols(C_TT, NTT))
                    V.tensor_scalar(pay[:, k, :, 1], cols(C_TT, NTT), float(k * TOK), None, ALU.add)
                    chain(V.tensor_copy(pay[:, k, :, 2], gt.bitcast(I32)))
                v.wait_ge(S("pos"), 1)
                pos = bank(0)[:, 0:NTT * NE].rearrange("p (t e) -> p t e", e=NE)
                chain(V.tensor_copy(cnt, bank(1)[:, 0:NE]))
                chain(V.tensor_tensor(cmp8, bc(cnt, 8), bm(cols(C_THR, 8), NE), ALU.is_gt))
                chain(V.tensor_reduce(ext, cmp8, AX.X, ALU.add))
                chain(V.tensor_tensor_scan(incl, ones[:, 0:NE], ext, 0.0, ALU.mult, ALU.add))
                chain(V.tensor_tensor(base, incl, ext, ALU.subtract))
                chain(V.tensor_tensor(cmpo, bc(cols(C_OV, XB), NE), bm(base, XB), ALU.is_ge))
                chain(V.tensor_scalar(base, base, float(P), float((NE - 1) * P), ALU.mult, ALU.add))
                chain(V.tensor_tensor(base, base, cols(C_E128, NE), ALU.subtract))
                chain(V.tensor_scalar(geb, pos, float(P), None, ALU.is_ge))
                chain(V.tensor_tensor(geb, geb, bm(base, NTT), ALU.mult))
                chain(V.tensor_tensor(slotE, pos, bm(cols(C_E128, NE), NTT), ALU.add))
                chain(V.tensor_tensor(slotE, slotE, geb, ALU.add))
                for k, o in ((0, oh1), (1, oh2)):
                    chain(V.tensor_tensor(wide, slotE, o, ALU.mult))
                    chain(V.tensor_reduce(dst[:, k], wide, AX.X, ALU.add))
                chain(V.tensor_scalar(pm, val, -float(DUMP), float(DUMP), ALU.mult, ALU.add))
                chain(V.tensor_tensor(dst, dst, bm(pm, 2), ALU.add))
                V.tensor_copy(dsti, dst).then_inc(S("dst"), 1)
                chain(V.tensor_tensor(cmpo2, bc(cols(C_OV, XB), NE), bm(incl, XB), ALU.is_lt))
                chain(V.tensor_tensor(cmpo, cmpo, cmpo2, ALU.mult))
                chain(V.tensor_tensor(cmpo, cmpo, bm(cols(C_EI, NE), XB), ALU.mult))
                chain(V.tensor_reduce(eo[:, 0:XB], cmpo, AX.X, ALU.add))
                chain(V.tensor_copy(eo[:, XB:], incl[:, NE - 1:NE]))
                V.tensor_copy(blk[0:1], eo[0:1]).then_inc(S("blk"), 1)
                v.wait_ge(S("tabT"), 1)
                V.tensor_copy(tabI[:, 0:3], bank(2)[:, 0:3 * MAXB].rearrange("p (c b) -> p c b", b=MAXB).bitcast(I32)).then_inc(S("tabI"), 1)

            @block.scalar
            def _(act):
                act.wait_ge(S("exg"), 1)
                nc.scalar.activation(exg, exg, ACT.Exp)
                act.wait_ge(S("ex"), 1)
                nc.scalar.activation(ex, ex, ACT.Exp).then_inc(S("exps"), 1)

            @block.tensor
            def _(pe):
                pe.wait_ge(S("mask"), 1)
                mk = mask.rearrange("p t e -> p (t e)")
                nc.tensor.matmul(bank(0)[:, 0:NTT * NE], cols(C_US, P), mk, start=True, stop=False, skip_group_check=True)
                for s in range(1, NTT):
                    nc.tensor.matmul(bank(0)[:, s * NE:NTT * NE], ones, mk[:, 0:(NTT - s) * NE], start=False, stop=(s == NTT - 1), skip_group_check=True)
                for t in range(NTT):
                    mm = nc.tensor.matmul(bank(1)[:, 0:NE], ones, mask[:, t, :], start=(t == 0), stop=(t == NTT - 1))
                mm.then_inc(S("pos"), 1)
                pe.wait_ge(S("tabrow"), 16)
                for c in range(3):
                    mm = nc.tensor.transpose(bank(2)[:, c * MAXB:(c + 1) * MAXB], tabrow[0:MAXB, :, c], ident[0:MAXB, 0:MAXB])
                mm.then_inc(S("tabT"), 1)

            @block.gpsimd
            def _(g):
                g.wait_ge(S("fill"), 1)
                g.dma_start(tab_d.rearrange("(p b) c -> p b c", b=MAXB), fill).then_inc(S("filled"), 16)
                g.wait_ge(S("filled"), 16)
                g.wait_ge(S("dst"), 1)
                n = 0
                for k in range(2):
                    for t in range(NTT):
                        g.indirect_dma_start(out=tab_d, out_offset=bass.IndirectOffsetOnAxis(ap=dsti[:, k, t:t + 1], axis=0),
                                             in_=pay[:, k, t, :], in_offset=None, bounds_check=MAXB * P - 1, oob_is_err=False).then_inc(S("scat"), 16)
                        n += 16
                g.wait_ge(S("scat"), n)
                g.dma_start(tabrow[0:MAXB].bitcast(I32), tab_d.rearrange("(b s) c -> b s c", s=P)).then_inc(S("tabrow"), 16)
                g.wait_ge(S("tabrow"), 16)

        stage_ends()
        mem.at = after_weights
        xg = [mem.take(D) for _ in range(U)]
        xgT = [mem.take(KD, P) for _ in range(2)]
        sg = [mem.take(DE) for _ in range(2)]
        hm = [mem.take(DE) for _ in range(2)]
        hT = [mem.take(KE, P) for _ in range(2)]
        ye = [mem.take(D) for _ in range(2)]
        it, io = ([mem.take(1).bitcast(I32) for _ in range(U)] for _ in range(2))
        gt = [mem.take(1) for _ in range(U)]
        wpg, wpp, gfB = mem.take(KD, D), mem.take(KE, D), mem.take(D)

        class Slot:

            def __init__(self, u, n, b, m=None):
                self.u, self.n, self.b = u, n, b
                self.v = u % 2
                self.m = 2 * n + u // 2 if m is None else m
                self.a, self.h = f"{u}", f"{u % 2}h"

        def load_block(sp, s, e):
            sp.wait_ge(S("down" + s.a), s.n)
            load_expert(sp, s.u, e, L(f"wgu{s.u}"), L(f"wd{s.u}"))

        def gather(g, s):
            g.wait_ge(S("xgT_ps" + s.a), s.n)
            g.wait_ge(S("hm" + s.a), s.n)
            g.tensor_copy(it[s.u], tabI[:, 0, bass.ds(s.b, 1)])
            g.tensor_copy(gt[s.u].bitcast(I32), tabI[:, 2, bass.ds(s.b, 1)]).then_inc(S("idx" + s.a), 1)
            g.wait_ge(S("idx" + s.a), s.n + 1)
            settle(g)
            g.indirect_dma_start(out=xg[s.u], out_offset=None, in_=xs_d,
                                 in_offset=bass.IndirectOffsetOnAxis(ap=it[s.u], axis=0)).then_inc(S("xg" + s.a), 16)

        def scatter(g, s):
            g.wait_ge(S("ye_out" + s.a), 16 * s.n)
            g.tensor_copy(io[s.u], tabI[:, 1, bass.ds(s.b, 1)]).then_inc(S("rows" + s.a), 1)
            g.wait_ge(S("ye" + s.h), s.m + 1)
            g.wait_ge(S("rows" + s.a), s.n + 1)
            settle(g)
            g.indirect_dma_start(out=ye_d, out_offset=bass.IndirectOffsetOnAxis(ap=io[s.u], axis=0), in_=ye[s.v], in_offset=None,
                                 bounds_check=2 * TOK - 1, oob_is_err=False).then_inc(S("ye_out" + s.a), 16)

        def turn_block(pe, s):
            pe.wait_ge(S("xg" + s.a), 16 * s.n + 16)
            pe.wait_ge(S("xgT_all"), s.b)
            for k in range(KD):
                mm = nc.tensor.transpose(flat(0, 2)[:, k * P:(k + 1) * P], xg[s.u].rearrange("p (c k) -> p k c", k=KD)[:, k, :], ident)
            mm.then_inc(S("xgT_ps" + s.a), 1)

        def up_block(pe, s):
            pe.wait_ge(S("xgT" + s.h), s.m + 1)
            pe.wait_ge(L(f"wgu{s.u}"), 32 * s.n + 32)
            pe.wait_ge(S("hm" + s.h), s.m)
            for k in range(KD):
                mm = nc.tensor.matmul(bank(2 + s.v), xgT[s.v][:, k, :], wgu[s.u][:, k, :], start=(k == 0), stop=(k == KD - 1))
            mm.then_inc(S("gu" + s.h), 1)

        def turn_hidden(pe, s):
            pe.wait_ge(S("hm" + s.h), s.m + 1)
            pe.wait_ge(S("hT_all"), s.b)
            for k in range(KE):
                mm = nc.tensor.transpose(bank(4)[:, k * P:(k + 1) * P], hm[s.v].rearrange("p (c k) -> p k c", k=KE)[:, k, :], ident)
            mm.then_inc(S("hT_ps" + s.h), 1)

        def down_block(pe, s):
            pe.wait_ge(S("hT" + s.h), s.m + 1)
            pe.wait_ge(L(f"wd{s.u}"), 16 * s.n + 16)
            pe.wait_ge(S("ye_all"), s.b)
            for n in range(2):
                for k in range(KE):
                    mm = nc.tensor.matmul(bank(6 + n), hT[s.v][:, k, :], wd[s.u][:, k, n * 512:(n + 1) * 512], start=(k == 0), stop=(k == KE - 1))
            mm.then_inc(S("down" + s.a), 1)

        def gain_block(v, s):
            v.wait_ge(S("xgT_ps" + s.a), s.n + 1)
            v.wait_ge(S("gu" + s.h), s.m)
            nc.vector.tensor_tensor(xgT[s.v], flat(0, 2).rearrange("p (k c) -> p k c", c=P), bc(g_ffn, P), ALU.mult).then_inc(S("xgT" + s.h), 1)
            v.wait_ge(S("xgT" + s.h), s.m + 1)
            v.sem_inc(S("xgT_all"), 1)

        def hidden_block(v, s):
            v.wait_ge(S("sg" + s.h), s.m + 1)
            v.wait_ge(S("idx" + s.a), s.n + 1)
            v.wait_ge(S("hT_ps" + s.h), s.m)
            nc.vector.scalar_tensor_tensor(hm[s.v], sg[s.v], gt[s.u], bank(2 + s.v)[:, DE:], ALU.mult, ALU.mult).then_inc(S("hm" + s.h), 1)
            v.wait_ge(S("hm" + s.h), s.m + 1)
            v.sem_inc(S("hm" + s.a), 1)

        def hidden_out(v, s):
            v.wait_ge(S("hT_ps" + s.h), s.m + 1)
            nc.vector.tensor_copy(hT[s.v].rearrange("p k c -> p (k c)"), bank(4)[:, 0:KE * P]).then_inc(S("hT" + s.h), 1)
            v.wait_ge(S("hT" + s.h), s.m + 1)
            v.sem_inc(S("hT_all"), 1)

        def silu_block(act, s):
            act.wait_ge(S("gu" + s.h), s.m + 1)
            act.wait_ge(S("hm" + s.h), s.m)
            nc.scalar.activation(sg[s.v], bank(2 + s.v)[:, 0:DE], ACT.Silu).then_inc(S("sg" + s.h), 1)

        def out_block(act, s, before, scattered):
            act.wait_ge(S("down" + s.a), s.n + 1)
            if before:
                act.wait_ge(S("ye_out" + before.a), scattered)
            nc.scalar.activation(ye[s.v], flat(6, 2), ACT.Copy).then_inc(S("ye" + s.h), 1)
            act.wait_ge(S("ye" + s.h), s.m + 1)
            act.sem_inc(S("ye_all"), 1)

        def slot(n, u):
            if u < 0:
                return slot(n - 1, u + U)
            if u >= U:
                return slot(n + 1, u - U)
            return Slot(u, n, n * U + u)

        def rounds(eng, body):
            for u in range(U):
                body(0, u, u)
            with eng.Fori(1, NE // U) as n:
                for u in range(U):
                    body(n, u, U)

        def overflow(eng, body):
            count = eng.value_load(blk[0:1, XB:XB + 1], min_val=0, max_val=XB)
            with eng.If(count > 1):
                with eng.Fori(1, XB) as o:
                    with eng.If(count > o):
                        body(Slot(0, eng.snap(o + NE // U), eng.snap(o + NE), eng.snap(o + 2 * NE // U)), o)

        with nc.Block() as block:
            @block.sync
            def _(sp):
                with sp.Fori(1, NE // U) as n:
                    for u in range(U):
                        load_block(sp, slot(n, u), sp.snap(n * U + u))
                load_block(sp, slot(NE // U, 0), sp.value_load(blk[0:1, 0:1], min_val=0, max_val=NE - 1))
                sp.dma_start(wpp, I["w_ple_proj"][0].rearrange("(k p) n -> p k n", p=P)).then_inc(L("wpp"), 16)
                sp.dma_start(wpg, I["w_ple_gate"][0].rearrange("(p k) n -> p k n", k=KD)).then_inc(L("wpg"), 16)
                sp.dma_start(gfB, I["norm_final"].partition_broadcast(P)).then_inc(L("gf"), 16)
                overflow(sp, lambda s, o: load_block(sp, s, sp.value_load(blk[0:1, bass.ds(o, 1)], min_val=0, max_val=NE - 1)))

            @block.gpsimd
            def _(g):
                def body(n, u, seen, last=False):
                    if not last:
                        gather(g, slot(n, u + 2))
                    if seen >= 2:
                        scatter(g, slot(n, u - 2))

                gather(g, slot(0, 0))
                gather(g, slot(0, 1))
                for u in range(U):
                    body(0, u, u)
                with g.Fori(1, NE // U - 1) as n:
                    for u in range(U):
                        body(n, u, U)
                for u in range(U + 1):
                    body(NE // U - 1, u, U, last=(u >= U - 1))
                scatter(g, slot(NE // U, -1))
                scatter(g, slot(NE // U, 0))
                for u in range(U):
                    g.wait_ge(S(f"ye_out{u}"), 16 * (NE // U + (u == 0)))

                def alone(s, o):
                    gather(g, s)
                    scatter(g, s)
                    g.wait_ge(S("ye_out0"), 16 * s.n + 16)
                    settle(g)

                overflow(g, alone)

            @block.tensor
            def _(pe):
                turn_block(pe, slot(0, 0))

                def body(n, u, seen, last=False):
                    up_block(pe, slot(n, u))
                    if seen >= 1:
                        turn_hidden(pe, slot(n, u - 1))
                    if not last:
                        turn_block(pe, slot(n, u + 1))
                    if seen >= 1:
                        down_block(pe, slot(n, u - 1))

                for u in range(U):
                    body(0, u, u)
                with pe.Fori(1, NE // U - 1) as n:
                    for u in range(U):
                        body(n, u, U)
                for u in range(U + 1):
                    body(NE // U - 1, u, U, last=(u == U))
                turn_hidden(pe, slot(NE // U, 0))
                down_block(pe, slot(NE // U, 0))

                def alone(s, o):
                    turn_block(pe, s)
                    up_block(pe, s)
                    turn_hidden(pe, s)
                    down_block(pe, s)

                overflow(pe, alone)

            @block.vector
            def _(v):
                def body(n, u, seen, last=False):
                    if seen >= 1:
                        hidden_out(v, slot(n, u - 1))
                    if not last:
                        gain_block(v, slot(n, u + 1))
                    hidden_block(v, slot(n, u))

                gain_block(v, slot(0, 0))
                for u in range(U):
                    body(0, u, u)
                with v.Fori(1, NE // U - 1) as n:
                    for u in range(U):
                        body(n, u, U)
                for u in range(U + 1):
                    body(NE // U - 1, u, U, last=(u == U))
                hidden_out(v, slot(NE // U, 0))

                def alone(s, o):
                    gain_block(v, s)
                    hidden_block(v, s)
                    hidden_out(v, s)

                overflow(v, alone)

            @block.scalar
            def _(act):
                def body(n, u, seen):
                    silu_block(act, slot(n, u))
                    if seen >= 1:
                        s, before = slot(n, u - 1), slot(n, u - 3)
                        out_block(act, s, before if seen >= 3 else None, 16 * before.n + 16)

                rounds(act, body)
                body(NE // U, 0, U)
                out_block(act, slot(NE // U, 0), slot(NE // U, -2), 16 * NE // U)

                def alone(s, o):
                    silu_block(act, s)
                    out_block(act, s, s, 16 * s.n)

                overflow(act, alone)

        stage_ends()
        mem.at = 0
        F = 3
        hf, y0, y1, xf, sgf, of = ([mem.take(D) for _ in range(F)] for _ in range(6))
        xfT = [mem.take(KD, P) for _ in range(F)]
        pf, pfT = [mem.take(PLE) for _ in range(F)], [mem.take(KE, P) for _ in range(F)]
        sc = [[mem.take(1) for _ in range(6)] for _ in range(F)]

        def nth(n, u):
            return (n, u) if u < F else (n + 1, u - F)

        def steps(eng, step):
            for u in range(F):
                step(0, u, F)
            with eng.Fori(1, NT // F) as n:
                for u in range(F):
                    step(n, u, F)
            for u in range(F):
                step(NT // F, u, F - 1 - u)

        def before(name, n, u):
            return (S(f"{name}{u - 1}"), n + 1) if u else (S(f"{name}{F - 1}"), n)

        with nc.Block() as block:
            @block.sync
            def _(sp):
                def load(n, u, t):
                    R, rows = (DEC, slice(SEQ, TOK)) if t is None else (P, bass.ds(t * P, P))
                    yrow = [slice(k * TOK + SEQ, k * TOK + TOK) if t is None else bass.ds(t * P + k * TOK, P) for k in range(2)]
                    psrc = I["p_sample"][0, :, 0, :] if t is None else I["p_prompt"][0, 0, rows, :]
                    sp.wait_ge(S(f"h3{u}"), n)
                    sp.wait_ge(S(f"pT_ps{u}"), n)
                    for dst_, src in ((hf[u], h_d[rows, :]), (y0[u], ye_d[yrow[0], :]), (y1[u], ye_d[yrow[1], :]), (pf[u], psrc)):
                        sp.dma_start(dst_[0:R], src).then_inc(S(f"in{u}"), 16)

                for u in range(F):
                    load(0, u, u)
                with sp.Fori(1, NT // F) as n:
                    for u in range(F):
                        load(n, u, sp.snap(F * n + u))
                for t in range(NT - NT % F, NT):
                    load(NT // F, t % F, t)
                load(NT // F, NT % F, None)

            @block.gpsimd
            def _(g):
                def power(n, u, which):
                    g.wait_ge(S(f"ms{which}{u}"), n + 1)
                    g.tensor_tensor(sc[u][3 * which + 2], sc[u][3 * which + 1], half, ALU.pow).then_inc(S(f"rs{which}{u}"), 1)

                power(0, 0, 0)
                power(0, 1, 0)

                def step(n, u, left):
                    if left > 1:
                        power(*nth(n, u + 2), 0)
                    power(n, u, 1)

                steps(g, step)

            @block.vector
            def _(v):
                V = nc.vector

                def sum_in(n, u):
                    v.wait_ge(S(f"in{u}"), 64 * n + 64)
                    V.tensor_tensor(hf[u], hf[u], y0[u], ALU.add).then_inc(S(f"v_h{u}"), 1)
                    v.wait_ge(S(f"v_h{u}"), n + 1)
                    V.tensor_tensor(hf[u], hf[u], y1[u], ALU.add).then_inc(S(f"h2{u}"), 1)
                    v.wait_ge(S(f"ssA{u}"), n + 1)
                    V.tensor_scalar(sc[u][1], sc[u][0], 1.0 / D, EPS, ALU.mult, ALU.add).then_inc(S(f"ms0{u}"), 1)
                    v.wait_ge(S(f"rs0{u}"), n + 1)
                    V.tensor_scalar(xf[u], hf[u], sc[u][2], None, ALU.mult).then_inc(S(f"xf{u}"), 1)

                def gain(n, u):
                    v.wait_ge(S(f"xfT_ps{u}"), n + 1)
                    v.wait_ge(S(f"gate_ps{u}"), n)
                    V.tensor_tensor(xfT[u], flat(0, 2).rearrange("p (k c) -> p k c", c=P), bc(g_ple, P), ALU.mult).then_inc(S(f"xfT{u}"), 1)
                    v.wait_ge(S(f"pT_ps{u}"), n + 1)
                    v.wait_ge(S(f"pp_ps{u}"), n)
                    V.tensor_copy(pfT[u].rearrange("p k c -> p (k c)"), bank(2)[:, 0:KE * P]).then_inc(S(f"pfT{u}"), 1)

                def close(n, u):
                    v.wait_ge(S(f"pp_ps{u}"), n + 1)
                    v.wait_ge(S(f"sgf{u}"), n + 1)
                    V.tensor_tensor(sgf[u], sgf[u], flat(6, 2), ALU.mult).then_inc(S(f"pg{u}"), 1)
                    v.wait_ge(S(f"pg{u}"), n + 1)
                    V.tensor_tensor(sgf[u], sgf[u], hf[u], ALU.add).then_inc(S(f"h3{u}"), 1)
                    v.wait_ge(S(f"ssB{u}"), n + 1)
                    V.tensor_scalar(sc[u][4], sc[u][3], 1.0 / D, EPS, ALU.mult, ALU.add).then_inc(S(f"ms1{u}"), 1)
                    v.wait_ge(S(f"rs1{u}"), n + 1)
                    v.wait_ge(L("gf"), 16)
                    V.scalar_tensor_tensor(of[u], sgf[u], sc[u][5], gfB, ALU.mult, ALU.mult).then_inc(S(f"of{u}"), 1)

                sum_in(0, 0)
                sum_in(0, 1)
                gain(0, 0)

                def step(n, u, left):
                    if left > 1:
                        sum_in(*nth(n, u + 2))
                    if left > 0:
                        gain(*nth(n, u + 1))
                    close(n, u)

                steps(v, step)

            @block.scalar
            def _(act):
                A = nc.scalar

                def square_in(n, u):
                    act.wait_ge(S(f"h2{u}"), n + 1)
                    act.wait_ge(S(f"xfT_ps{u}"), n)
                    A.activation(xf[u], hf[u], ACT.Square, accum_out=sc[u][0]).then_inc(S(f"ssA{u}"), 1)

                def sigmoid(n, u):
                    act.wait_ge(S(f"gate_ps{u}"), n + 1)
                    act.wait_ge(S(f"of{u}"), n)
                    A.activation(sgf[u], flat(4, 2), ACT.Sigmoid).then_inc(S(f"sgf{u}"), 1)

                def close(n, u, rows, R):
                    act.wait_ge(S(f"h3{u}"), n + 1)
                    act.wait_ge(S(f"out{u}"), 16 * n)
                    A.activation(of[u], sgf[u], ACT.Square, accum_out=sc[u][3]).then_inc(S(f"ssB{u}"), 1)
                    act.wait_ge(S(f"of{u}"), n + 1)
                    act.dma_start(O["y_prompt"][0, rows, :] if R == P else O["y_sample"][:, 0, :], of[u][0:R]).then_inc(S(f"out{u}"), 16)

                square_in(0, 0)
                square_in(0, 1)

                def step(n, u, left):
                    if left > 1:
                        square_in(*nth(n, u + 2))
                    sigmoid(n, u)
                    if left:
                        rows = bass.ds((F * n + u) * P if isinstance(n, int) else act.snap((F * n + u) * P), P) if left == F else slice((NT - left) * P, (NT - left + 1) * P)
                        close(n, u, rows, P)
                    else:
                        close(n, u, None, DEC)

                steps(act, step)
                for u in range(F):
                    act.wait_ge(S(f"out{u}"), 16 * 3)

            @block.tensor
            def _(pe):
                def turn(n, u):
                    pe.wait_ge(S(f"xf{u}"), n + 1)
                    pe.wait_ge(*before("xfT", n, u))
                    pe.wait_ge(*before("pfT", n, u))
                    for k in range(KD):
                        mm = nc.tensor.transpose(flat(0, 2)[:, k * P:(k + 1) * P], xf[u].rearrange("p (c k) -> p k c", k=KD)[:, k, :], ident)
                    mm.then_inc(S(f"xfT_ps{u}"), 1)
                    for k in range(KE):
                        mm = nc.tensor.transpose(bank(2)[:, k * P:(k + 1) * P], pf[u][:, k * P:(k + 1) * P], ident)
                    mm.then_inc(S(f"pT_ps{u}"), 1)

                def products(n, u):
                    pe.wait_ge(S(f"xfT{u}"), n + 1)
                    pe.wait_ge(*before("sgf", n, u))
                    pe.wait_ge(L("wpg"), 16)
                    for m in range(2):
                        for k in range(KD):
                            mm = nc.tensor.matmul(bank(4 + m), xfT[u][:, k, :], wpg[:, k, m * 512:(m + 1) * 512], start=(k == 0), stop=(k == KD - 1))
                    mm.then_inc(S(f"gate_ps{u}"), 1)
                    pe.wait_ge(S(f"pfT{u}"), n + 1)
                    pe.wait_ge(*before("pg", n, u))
                    pe.wait_ge(L("wpp"), 16)
                    for m in range(2):
                        for k in range(KE):
                            mm = nc.tensor.matmul(bank(6 + m), pfT[u][:, k, :], wpp[:, k, m * 512:(m + 1) * 512], start=(k == 0), stop=(k == KE - 1))
                    mm.then_inc(S(f"pp_ps{u}"), 1)

                turn(0, 0)

                def step(n, u, left):
                    if left > 0:
                        turn(*nth(n, u + 1))
                    products(n, u)

                steps(pe, step)




_INS = ["x_prompt", "x_sample", "p_prompt", "p_sample", "cache_k", "cache_v", "state_conv", "state_S", "rel_bias",
        "norm_mix", "w_in", "att_sink", "conv_w", "dn_A_log", "dn_dt_bias", "dn_norm", "w_out", "norm_ffn",
        "w_router_group", "w_router_expert", "w_gate", "w_up", "w_down", "w_ple_proj", "w_ple_gate", "norm_ple",
        "norm_final"]
_OUTS = [("y_prompt", (1, SEQ, D)), ("y_sample", (DEC, 1, D)),
         ("cache_k_prompt", (1, 1, P, 2, HD)), ("cache_v_prompt", (1, 1, P, 2, HD)),
         ("state_conv_prompt", (1, 1, CW - 1, CCH)), ("state_S_prompt", (1, 1, NH, HD, HD)),
         ("cache_k_sample", (1, DEC, P, 2, HD)), ("cache_v_sample", (1, DEC, P, 2, HD)),
         ("state_conv_sample", (1, DEC, CW - 1, CCH)), ("state_S_sample", (1, DEC, NH, HD, HD))]


def kernel(**inputs):
    import concourse.bacc as _bacc
    from concourse.bass_utils import run_bass_kernel_spmd as _run

    nc = _bacc.Bacc("TRN2", target_bir_lowering=False, num_devices=1)
    arrays = {f"in_{name}": np.ascontiguousarray(inputs[name]) for name in _INS}
    arrays["in_cst"] = constants()
    ins = {name[3:]: nc.dram_tensor(name, a.shape, F32, kind="ExternalInput").ap() for name, a in arrays.items()}
    outs = {name: nc.dram_tensor(f"out_{name}", shape, F32, kind="ExternalOutput").ap() for name, shape in _OUTS}
    program(nc, ins, outs)
    r = _run(nc, [arrays], core_ids=[0])
    return tuple(r.results[0][f"out_{name}"] for name, _ in _OUTS)
```
